# Optimizing a Trainium2 kernel written in Bass

```python
import math
import jax, jax.numpy as jnp
from jax import lax
import numpy as np

D_MODEL = 1024
BATCH = 1
SEQ = 256
DEPTH = 1

HEAD_DIM = 64
SB_HEADS = 8
SB_WIDTH = SB_HEADS * HEAD_DIM
RG_BLOCKS = 4
RG_BLOCK_DIM = 64
RG_WIDTH = RG_BLOCKS * RG_BLOCK_DIM
CA_HEADS = 4
CA_WIDTH = CA_HEADS * HEAD_DIM
D_MIX = SB_WIDTH + RG_WIDTH + CA_WIDTH
D_IN = 3 * SB_WIDTH + 2 * RG_WIDTH + CA_WIDTH
IN_SPLITS = (SB_WIDTH, 2 * SB_WIDTH, 3 * SB_WIDTH, 3 * SB_WIDTH + RG_WIDTH, 3 * SB_WIDTH + 2 * RG_WIDTH)
MEM_LEN = 256
CONV_WIDTH = 4
LRU_C = 8.0
SB_BLOCK = 128
N_EXPERTS = 64
TOP_K = 8
N_GROUPS = 8
TOPK_GROUPS = 4
D_EXPERT = 256
D_SHARED = 256
ROUTED_SCALE = 2.5
RMS_EPS = 1e-6

kernel_name = 'hybrid_stickbreak_rglru_memxattn_moe'

def rms_norm(x, g):
    xf = x.astype(jnp.float32)
    y = xf * lax.rsqrt(jnp.mean(xf * xf, axis=-1, keepdims=True) + RMS_EPS)
    return (y * g.astype(jnp.float32)).astype(x.dtype)

def split_heads(t, n_heads):
    b, s, _ = t.shape
    return t.reshape(b, s, n_heads, HEAD_DIM).transpose(0, 2, 1, 3)

def merge_heads(t):
    b, n, s, d = t.shape
    return t.transpose(0, 2, 1, 3).reshape(b, s, n * d)

def stick_breaking_attention(q, k, v):
    b, h, s, d = q.shape
    n_blocks = s // SB_BLOCK
    scale = 1.0 / math.sqrt(d)
    kf = k.astype(jnp.float32)
    vf = v.astype(jnp.float32)
    q_blocks = q.reshape(b, h, n_blocks, SB_BLOCK, d).transpose(2, 0, 1, 3, 4)
    key_pos = jnp.arange(s)

    def one_block(args):
        q_blk, blk = args
        z = jnp.einsum('bhqd,bhkd->bhqk', q_blk.astype(jnp.float32), kf) * scale
        query_pos = blk * SB_BLOCK + jnp.arange(SB_BLOCK)
        strict = key_pos[None, :] < query_pos[:, None]
        log_beta = jax.nn.log_sigmoid(z)
        log_not = jnp.where(strict, jax.nn.log_sigmoid(-z), 0.0)
        between = lax.cumsum(log_not, axis=3, reverse=True) - log_not
        w = jnp.where(strict, jnp.exp(log_beta + between), 0.0)
        return jnp.einsum('bhqk,bhkd->bhqd', w, vf)

    out = lax.map(one_block, (q_blocks, jnp.arange(n_blocks)))
    return out.transpose(1, 2, 0, 3, 4).reshape(b, h, s, d).astype(q.dtype)

def causal_depthwise_conv(x, w, bias):
    s = x.shape[1]
    xp = jnp.pad(x, ((0, 0), (CONV_WIDTH - 1, 0), (0, 0)))
    out = bias
    for tap in range(CONV_WIDTH):
        out = out + w[tap] * xp[:, tap:tap + s]
    return out

def rg_lru(x, w_rgate, b_rgate, w_igate, b_igate, lru_lambda):
    bsz, s, c = x.shape
    xf = x.astype(jnp.float32)
    xb = xf.reshape(bsz, s, RG_BLOCKS, RG_BLOCK_DIM)
    r = jax.nn.sigmoid(jnp.einsum('bsnc,ncd->bsnd', xb, w_rgate.astype(jnp.float32)).reshape(bsz, s, c)
                       + b_rgate.astype(jnp.float32))
    i = jax.nn.sigmoid(jnp.einsum('bsnc,ncd->bsnd', xb, w_igate.astype(jnp.float32)).reshape(bsz, s, c)
                       + b_igate.astype(jnp.float32))
    log_a = -LRU_C * r * jax.nn.softplus(-lru_lambda.astype(jnp.float32))
    a = jnp.exp(log_a)
    u = jnp.sqrt(-jnp.expm1(2.0 * log_a)) * (i * xf)

    def combine(left, right):
        a_l, h_l = left
        a_r, h_r = right
        return a_l * a_r, a_r * h_l + h_r

    _, h = lax.associative_scan(combine, (a, u), axis=1)
    return h

def memory_cross_attention(q, mem, norm_mem_g, w_mem_kv, q_norm_g, k_norm_g):
    mem_n = rms_norm(mem, norm_mem_g)
    k, v = jnp.split(mem_n @ w_mem_kv, 2, axis=-1)
    qh = rms_norm(split_heads(q, CA_HEADS), q_norm_g)
    kh = rms_norm(split_heads(k, CA_HEADS), k_norm_g)
    vh = split_heads(v, CA_HEADS)
    z = jnp.einsum('bhsd,bhmd->bhsm', qh.astype(jnp.float32), kh.astype(jnp.float32)) / math.sqrt(HEAD_DIM)
    p = jax.nn.softmax(z, axis=-1)
    o = jnp.einsum('bhsm,bhmd->bhsd', p, vh.astype(jnp.float32))
    return merge_heads(o).astype(q.dtype)

def hybrid_mixer(x, mem, norm_mix_g, norm_mem_g, w_in, conv_w, conv_b, w_rgate, b_rgate, w_igate,
                 b_igate, lru_lambda, w_mem_kv, q_norm_g, k_norm_g, g_out_sb, g_out_rg, g_out_ca, w_out):
    h = rms_norm(x, norm_mix_g)
    proj = h @ w_in
    q_sb, k_sb, v_sb, x_rg, gate_rg, q_ca = jnp.split(proj, IN_SPLITS, axis=-1)
    o_sb = merge_heads(stick_breaking_attention(split_heads(q_sb, SB_HEADS), split_heads(k_sb, SB_HEADS),
                                                split_heads(v_sb, SB_HEADS)))
    xc = causal_depthwise_conv(x_rg, conv_w, conv_b)
    hr = rg_lru(xc, w_rgate, b_rgate, w_igate, b_igate, lru_lambda)
    o_rg = (jax.nn.gelu(gate_rg.astype(jnp.float32)) * hr).astype(x.dtype)
    o_ca = memory_cross_attention(q_ca, mem, norm_mem_g, w_mem_kv, q_norm_g, k_norm_g)
    y = jnp.concatenate([rms_norm(o_sb, g_out_sb), rms_norm(o_rg, g_out_rg), rms_norm(o_ca, g_out_ca)], axis=-1)
    return y @ w_out

def moe_ffn(xn, w_router, router_bias, w_gate_e, w_up_e, w_down_e, w_gate_sh, w_up_sh, w_down_sh):
    bsz, s, d = xn.shape
    t = xn.reshape(bsz * s, d)
    n_tok = t.shape[0]
    scores = jax.nn.sigmoid(t.astype(jnp.float32) @ w_router.astype(jnp.float32))
    choice = scores + router_bias.astype(jnp.float32)
    grp = choice.reshape(n_tok, N_GROUPS, N_EXPERTS // N_GROUPS)
    grp_score = lax.top_k(grp, 2)[0].sum(axis=-1)
    _, gidx = lax.top_k(grp_score, TOPK_GROUPS)
    gmask = jax.nn.one_hot(gidx, N_GROUPS, dtype=jnp.float32).sum(axis=1) > 0
    emask = jnp.repeat(gmask, N_EXPERTS // N_GROUPS, axis=1)
    _, eidx = lax.top_k(jnp.where(emask, choice, -jnp.inf), TOP_K)
    w = jnp.take_along_axis(scores, eidx, axis=1)
    w = w / (w.sum(axis=-1, keepdims=True) + 1e-20) * ROUTED_SCALE
    rows = jnp.arange(n_tok)[:, None]
    gates = jnp.zeros((n_tok, N_EXPERTS), jnp.float32).at[rows, eidx].set(w)

    def add_expert(acc, params):
        wg, wu, wd, g = params
        hid = jax.nn.silu(t @ wg) * (t @ wu)
        return acc + g[:, None] * (hid @ wd).astype(jnp.float32), None

    routed, _ = lax.scan(add_expert, jnp.zeros((n_tok, d), jnp.float32),
                         (w_gate_e, w_up_e, w_down_e, gates.T))
    shared = (jax.nn.silu(t @ w_gate_sh) * (t @ w_up_sh)) @ w_down_sh
    return (routed + shared.astype(jnp.float32)).reshape(bsz, s, d).astype(xn.dtype)

def setup_inputs(seed: int = 0) -> dict:
    key = jax.random.key(seed)
    ks = jax.random.split(key, 28)
    f = jnp.float32
    L = DEPTH

    def nrm(k, shape, fan_in):
        return jax.random.normal(k, shape, f) * fan_in ** -0.5

    def gain(k, shape):
        return 1.0 + 0.02 * jax.random.normal(k, shape, f)

    def small(k, shape):
        return 0.02 * jax.random.normal(k, shape, f)

    u = jax.random.uniform(ks[11], (L, RG_WIDTH), f, 0.9, 0.999)
    a0 = u ** (1.0 / LRU_C)
    lru_lambda = jnp.log(a0) - jnp.log1p(-a0)
    return {
        'x': jax.random.normal(ks[0], (BATCH, SEQ, D_MODEL), f),
        'mem': jax.random.normal(ks[1], (BATCH, MEM_LEN, D_MODEL), f),
        'norm_mix_g': gain(ks[2], (L, D_MODEL)),
        'norm_mem_g': gain(ks[3], (L, D_MODEL)),
        'w_in': nrm(ks[4], (L, D_MODEL, D_IN), D_MODEL),
        'conv_w': nrm(ks[5], (L, CONV_WIDTH, RG_WIDTH), CONV_WIDTH),
        'conv_b': small(ks[6], (L, RG_WIDTH)),
        'w_rgate': nrm(ks[7], (L, RG_BLOCKS, RG_BLOCK_DIM, RG_BLOCK_DIM), RG_BLOCK_DIM),
        'b_rgate': small(ks[8], (L, RG_WIDTH)),
        'w_igate': nrm(ks[9], (L, RG_BLOCKS, RG_BLOCK_DIM, RG_BLOCK_DIM), RG_BLOCK_DIM),
        'b_igate': small(ks[10], (L, RG_WIDTH)),
        'lru_lambda': lru_lambda,
        'w_mem_kv': nrm(ks[12], (L, D_MODEL, 2 * CA_WIDTH), D_MODEL),
        'q_norm_g': gain(ks[13], (L, HEAD_DIM)),
        'k_norm_g': gain(ks[14], (L, HEAD_DIM)),
        'g_out_sb': gain(ks[15], (L, SB_WIDTH)),
        'g_out_rg': gain(ks[16], (L, RG_WIDTH)),
        'g_out_ca': gain(ks[17], (L, CA_WIDTH)),
        'w_out': nrm(ks[18], (L, D_MIX, D_MODEL), D_MIX),
        'norm_ffn_g': gain(ks[19], (L, D_MODEL)),
        'w_router': nrm(ks[20], (L, D_MODEL, N_EXPERTS), D_MODEL),
        'router_bias': 0.01 * jax.random.normal(ks[21], (L, N_EXPERTS), f),
        'w_gate_e': nrm(ks[22], (L, N_EXPERTS, D_MODEL, D_EXPERT), D_MODEL),
        'w_up_e': nrm(ks[23], (L, N_EXPERTS, D_MODEL, D_EXPERT), D_MODEL),
        'w_down_e': nrm(ks[24], (L, N_EXPERTS, D_EXPERT, D_MODEL), D_EXPERT),
        'w_gate_sh': nrm(ks[25], (L, D_MODEL, D_SHARED), D_MODEL),
        'w_up_sh': nrm(ks[26], (L, D_MODEL, D_SHARED), D_MODEL),
        'w_down_sh': nrm(ks[27], (L, D_SHARED, D_MODEL), D_SHARED),
    }

def reference(x, mem, norm_mix_g, norm_mem_g, w_in, conv_w, conv_b, w_rgate, b_rgate, w_igate, b_igate,
              lru_lambda, w_mem_kv, q_norm_g, k_norm_g, g_out_sb, g_out_rg, g_out_ca, w_out, norm_ffn_g,
              w_router, router_bias, w_gate_e, w_up_e, w_down_e, w_gate_sh, w_up_sh, w_down_sh):
    for layer in range(DEPTH):
        x = x + hybrid_mixer(x, mem, norm_mix_g[layer], norm_mem_g[layer], w_in[layer], conv_w[layer],
                             conv_b[layer], w_rgate[layer], b_rgate[layer], w_igate[layer], b_igate[layer],
                             lru_lambda[layer], w_mem_kv[layer], q_norm_g[layer], k_norm_g[layer],
                             g_out_sb[layer], g_out_rg[layer], g_out_ca[layer], w_out[layer])
        x = x + moe_ffn(rms_norm(x, norm_ffn_g[layer]), w_router[layer], router_bias[layer], w_gate_e[layer],
                        w_up_e[layer], w_down_e[layer], w_gate_sh[layer], w_up_sh[layer], w_down_sh[layer])
    return x


_drawn_inputs = setup_inputs


def setup_inputs(seed=0):
    import zlib

    import numpy as np

    out = dict(_drawn_inputs(seed))
    spreads = {}
    factors = {'b_rgate': 3.591, 'b_igate': 2.779}
    for name, (base, spread) in spreads.items():
        noise = np.random.default_rng([zlib.crc32(name.encode()), seed]).standard_normal(out[name].shape)
        drawn = base * np.exp(spread * noise) if base else spread * noise
        out[name] = __import__('jax').numpy.asarray(drawn.astype(out[name].dtype))
    for name, factor in factors.items():
        out[name] = (out[name] * factor).astype(out[name].dtype)
    return out
```

```python
import concourse.bass as bass
from concourse import mybir
from contextlib import ExitStack


def hybrid_decoder_layer(
    nc: bass.Bass,
    x, mem, norm_mix_g, norm_mem_g, w_in, conv_w, conv_b, w_rgate, b_rgate, w_igate, b_igate, lru_lambda,
    w_mem_kv, q_norm_g, k_norm_g, g_out_sb, g_out_rg, g_out_ca, w_out, norm_ffn_g, w_router, router_bias,
    w_gate_e, w_up_e, w_down_e, w_gate_sh, w_up_sh, w_down_sh, out,
):
    F32, F32R, BF16, I32 = mybir.dt.float32, mybir.dt.float32r, mybir.dt.bfloat16, mybir.dt.int32
    ALU = mybir.AluOpType
    ACT = mybir.ActivationFunctionType
    AX = mybir.AxisListType

    P = 128
    _, SEQ, D = x.shape
    NT = SEQ // P
    KD = D // P
    HD = 64
    SB, RG, CA = 512, 256, 256
    SB_HEADS, CA_HEADS = SB // HD, CA // HD
    NE, GROUPS, DE = w_router.shape[2], 8, w_gate_e.shape[3]
    EG = NE // GROUPS
    KH = DE // P
    SLOTS = 64
    PAIRS = NE // 2
    EPS = 1e-6
    HUGE = 3.0e38
    SCALE = HD ** -0.5
    RING = 4

    KB = 1024
    base = (nc.sbuf_base + 31) // 32 * 32
    o_ring = base
    o_A = o_ring + 96 * KB
    o_R = o_A + 32 * KB
    o_V = o_R + 24 * KB
    o_O = o_V + 16 * KB

    def at(name, offset, shape, dt=F32):
        return nc.alloc_sbuf_tensor_at(name, shape, dt, offset=offset)

    class Space:
        def __init__(self, offset):
            self.offset = offset

        def __call__(self, name, shape, dt=F32):
            t = at(name, self.offset, shape, dt)
            n = 1
            for s in shape[1:]:
                n *= s
            self.offset += (n * (2 if dt == BF16 else 4) + 31) // 32 * 32
            return t

    ring_gu = [at(f"ring_gu{s}", o_ring + 24 * KB * s, [P, 2, KD, DE]) for s in range(RING)]
    ring_d = [at(f"ring_d{s}", o_ring + 24 * KB * s + 16 * KB, [P, KH, D]) for s in range(RING)]
    xn = at("xn", o_ring, [P, NT, D])
    memn = at("memn", o_ring + 8 * KB, [P, NT, D])
    x_in = at("x_in", o_ring + 24 * KB, [P, NT, D])
    hT = at("hT", o_ring + 48 * KB, [P, KD, SEQ])
    memT = at("memT", o_ring + 56 * KB, [P, KD, SEQ])
    w_kv = at("w_kv", o_ring + 72 * KB, [P, KD, 2 * CA])
    mem_in = at("mem_in", o_ring + 88 * KB, [P, NT, D])
    wA = [at(f"wA{g}", o_A + 8 * KB * g, [P, KD, 256]) for g in range(4)]
    wo = at("wo", o_A, [P, KD, D])
    xg = [at(f"xg{b}", o_A + 16 * KB * b, [P, KD, 512]) for b in range(2)]
    s_sg = at("s_sg", o_A + 24 * KB, [P, NT, DE])
    s_h = at("s_h", o_A + 26 * KB, [P, NT, KH, P])
    s_hT = at("s_hT", o_A + 28 * KB, [P, KH, SEQ])
    wR = [at(f"wR{g}", o_R + 8 * KB * g, [P, KD, 256]) for g in range(3)]
    r = Space(o_R)
    xc = r("xc", [P, 2, SEQ])
    rg_r = r("rg_r", [P, 2, SEQ])
    rg_i = r("rg_i", [P, 2, SEQ])
    rg_a = r("rg_a", [P, 2, SEQ])
    rg_t = r("rg_t", [P, 2, SEQ])
    rg_u = r("rg_u", [P, 2, SEQ])
    rg_g = r("rg_g", [P, 2, SEQ])
    ca_sq = r("ca_sq", [P, 2, 2 * SEQ])
    ca_rs = r("ca_rs", [P, 2, 2 * SEQ])
    y_sq = at("y_sq", o_R, [P, KD, SEQ])
    y_rs = at("y_rs", o_R + 8 * KB, [P, 3, SEQ])
    xhi = at("xhi", o_R, [P, NT, KD, P], F32R)
    xlo = at("xlo", o_R + 8 * KB, [P, NT, KD, P], F32R)
    xn2T = at("xn2T", o_R + 16 * KB, [P, KD, SEQ])
    yhi = at("yhi", o_R + 16 * KB, [P, D], F32R)
    ylo = at("ylo", o_R + 20 * KB, [P, D], F32R)
    wV = at("wV", o_V, [P, KD, SB])
    r = Space(o_V)
    NZ = 3 * P
    beta = [r(f"beta{b}", [P, NZ]) for b in range(2)]
    keep = [r(f"keep{b}", [P, NZ]) for b in range(2)]
    rest = [r(f"rest{b}", [P, NZ + 2]) for b in range(2)]
    wT = [r(f"wT{b}", [P, NZ]) for b in range(2)]
    ca_p = [at(f"ca_p{b}", o_V + 2 * KB * b, [P, NT, SEQ]) for b in range(2)]
    ca_pT = [at(f"ca_pT{b}", o_V + 4 * KB + 2 * KB * b, [P, 2, SEQ]) for b in range(2)]
    pick = [at(f"pick{b}", o_V + 4 * KB * b, [P, NT, 8 * SLOTS], F32R) for b in range(2)]
    xn2 = at("xn2", o_V + 8 * KB, [P, NT, KD, P])
    r = Space(o_O)
    qk = r("qk", [P, 8, SEQ])
    v_sb = r("v_sb", [P, NT, SB])
    xpad = r("xpad", [P, 2, SEQ + 3])
    gate = r("gate", [P, 2, SEQ])
    qkca = r("qkca", [P, 4, SEQ])
    v_ca = r("v_ca", [P, NT, CA])
    yT = r("yT", [P, KD, SEQ])
    x1 = at("x1", o_O, [P, NT, D])
    ov_xg = at("ov_xg", o_O + 8 * KB, [P, KD, P])
    g_ffn = at("g_ffn", o_O + 12 * KB + 2080 + 2 * KB, [P, D])
    rt = Space(o_O + 8 * KB)
    w_rt = rt("w_rt", [P, KD, NE])
    rbias = rt("rbias", [P, NE])
    top8 = rt("top8", [P, NT, GROUPS, 8])
    gtop = rt("gtop", [P, NT, 8])
    grep = rt("grep", [P, NT, 16])
    rt = Space(o_O + 12 * KB)
    score = rt("score", [P, NT, NE])
    choice = rt("choice", [P, NT, NE])
    rt = Space(o_O + 12 * KB + 2080 + 6 * KB)
    cand = rt("cand", [P, NT, NE])
    repl = rt("repl", [P, NT, NE])
    gatew = rt("gatew", [P, NT, NE])
    rt = Space(o_O + 12 * KB + 2080 + 8 * KB)
    e_h = rt("e_h", [P, KH, P])
    e_sg = rt("e_sg", [P, DE])
    e_hT = rt("e_hT", [P, KH, P])
    S = [rt(f"S{b}", [P, SEQ], F32R) for b in range(2)]
    ov_pick = rt("ov_pick", [P, NT, P], F32R)
    ov_S = rt("ov_S", [P, SEQ], F32R)
    ov_h = rt("ov_h", [P, KH, P])
    ident = r("ident", [P, P])
    ones = r("ones", [P, P])
    upper = r("upper", [P, P], BF16)
    ones_b = r("ones_b", [P, P], BF16)
    block_ones = r("block_ones", [P, P])
    vecs = r("vecs", [42, P])
    vec = r("vec", [P, 42])
    zeros = r("zeros", [P, SEQ])
    iota1 = r("iota1", [P, SEQ + SLOTS])
    wg_r = r("wg_r", [P, 2, HD])
    wg_i = r("wg_i", [P, 2, HD])
    picked = r("picked", [P, NT, NE], BF16)
    posm = r("posm", [P, NT, NE])
    gates2 = r("gates2", [P, NT, PAIRS, 4], F32R)
    stat = r("stat", [P, 16])
    gslot = r("gslot", [P, 2])
    ov_gslot = r("ov_gslot", [P, 1])
    lam = r("lam", [P, 8, 2])
    mx = r("mx", [P, 2, 4])
    grp = r("grp", [P, NT, 16])
    cnt_row = r("cnt_row", [1, 4, NE + 1])
    cum = r("cum", [1, NE + 1], I32)
    assert r.offset <= nc.sbuf_usable_end, r.offset - nc.sbuf_usable_end

    MIX, MEM, GOUT, CW, CB, BR, BI, LAM, QN, KN = 0, 8, 16, 24, 32, 34, 36, 38, 40, 41

    with ExitStack() as ctx:
        ps = ctx.enter_context(nc.psum_tensor("ps", [P, 8, 512], F32))
        U, T, Y, ACC = 0, 1, (2, 3), (4, 5, 6, 7)
        (
            x_loaded, mem_loaded, vec_loaded, wg_loaded, wV_loaded, kv_loaded, wo_loaded, x1_loaded,
            gffn_loaded, rt_loaded, rb_loaded, consts, zeroed, ssq_act, std_act, xn_dve, vec_ps, vec_dve,
            xT_ps, xT_act, xT_dve, memT_ps, memT_act, memT_dve, unit_ps, unit_act, unit_dve, conv_dve, z_ps,
            bc_act, mask_pool, w_dve, wT_ps, wT_act, o_ps, yT_dve, lam_act, lam_dve, gelu_dve, gelu_act,
            rg_act, rg_dve, sq_act, car_act, can_dve, camax_dve, cap_dve, oca_ps, oca_dve, yrg_dve, ysq_act,
            yrs_dve, yrs_act, yn_dve, wo_ps, x1_dve, x2T_ps, x2T_act, x2T_dve, split_act, split_dve, rt_ps,
            score_act, route_dve, count_ps, cum_dve, s_gu_ps, s_sg_act, s_h_dve, s_hT_ps, s_hT_dve,
            s_down_ps, pick_dve, gather_ps, xg_act, xg_dve, gu_ps, sg_act, h_dve, hT_ps, hTs_dve, pt_ps,
            S_act, gslot_dve, y_ps, yhi_act, ylo_dve, scatter_ps, ov_pick_dve, ov_gather_ps, ov_xg_act,
            ov_xg_dve, ov_pt_ps, ov_S_act, ov_gslot_dve, ov_gu_ps, ov_sg_act, ov_h_dve, ov_hT_ps,
            ov_hTs_dve, ov_y_ps, ov_yhi_act, ov_ylo_dve, ov_scatter_ps, last_ps, out_dve, stored, act_chain,
            dve_chain, pool_chain,
        ) = [ctx.enter_context(nc.semaphore(name)) for name in """
            x_loaded mem_loaded vec_loaded wg_loaded wV_loaded kv_loaded wo_loaded x1_loaded gffn_loaded
            rt_loaded rb_loaded consts zeroed ssq_act std_act xn_dve vec_ps vec_dve xT_ps xT_act xT_dve
            memT_ps memT_act memT_dve unit_ps unit_act unit_dve conv_dve z_ps bc_act mask_pool w_dve
            wT_ps wT_act o_ps yT_dve lam_act lam_dve gelu_dve gelu_act rg_act rg_dve sq_act car_act
            can_dve camax_dve cap_dve oca_ps oca_dve yrg_dve ysq_act yrs_dve yrs_act yn_dve wo_ps x1_dve
            x2T_ps x2T_act x2T_dve split_act split_dve rt_ps score_act route_dve count_ps cum_dve
            s_gu_ps s_sg_act s_h_dve s_hT_ps s_hT_dve s_down_ps pick_dve gather_ps xg_act xg_dve gu_ps
            sg_act h_dve hT_ps hTs_dve pt_ps S_act gslot_dve y_ps yhi_act ylo_dve scatter_ps ov_pick_dve
            ov_gather_ps ov_xg_act ov_xg_dve ov_pt_ps ov_S_act ov_gslot_dve ov_gu_ps ov_sg_act ov_h_dve
            ov_hT_ps ov_hTs_dve ov_y_ps ov_yhi_act ov_ylo_dve ov_scatter_ps last_ps out_dve stored
            act_chain dve_chain pool_chain
        """.split()]
        wA_loaded = [ctx.enter_context(nc.semaphore(f"wA_loaded{g}")) for g in range(4)]
        wR_loaded = [ctx.enter_context(nc.semaphore(f"wR_loaded{g}")) for g in range(3)]
        gu_loaded = [ctx.enter_context(nc.semaphore(f"gu_loaded{i}")) for i in range(RING)]
        d_loaded = [ctx.enter_context(nc.semaphore(f"d_loaded{i}")) for i in range(RING)]
        block = ctx.enter_context(nc.Block())

        owner = ["act" if n % 2 == 0 else "dve" for n in range(20)]
        owner += ["act", "act", "dve", "dve"] + ["act"] * 4 + ["dve"] * 4 + ["dve"] * 5
        walk = [("unit", n) for n in range(8)] + [("memT", 0), ("unit", 8), ("unit", 9)]
        for i in range(1, 13):
            walk.append(("unit", 9 + i))
            if i <= 8:
                walk.append(("z", i - 1))
            if 3 <= i <= 10:
                walk.append(("t", i - 3))
            if 4 <= i <= 11:
                walk.append(("av", i - 4))
            if i == 7:
                walk.append(("conv", 0))

        ACT_K, DVE_K = [0, 1, 4, 5], [2, 3, 6, 7]

        def freed(eng, n):
            count = owner[:n + 1].count(owner[n])
            eng.wait_ge(unit_act if owner[n] == "act" else unit_dve, count)

        def slot(j):
            return (j + 1) % RING

        def fills(it, j):
            return 4 * it + (j + 1) // RING + 1

        def load_expert(sp, n_slot, gate_src, up_src, down_src):
            sp.dma_start(ring_gu[n_slot][:, 0], gate_src.rearrange("(p k) n -> p k n", k=KD)).then_inc(gu_loaded[n_slot], 16)
            sp.dma_start(ring_gu[n_slot][:, 1], up_src.rearrange("(p k) n -> p k n", k=KD)).then_inc(gu_loaded[n_slot], 16)
            sp.dma_start(ring_d[n_slot][:], down_src.rearrange("(p k) n -> p k n", k=KH)).then_inc(d_loaded[n_slot], 16)

        @block.sync
        def _(sp):
            def cols(c, n):
                return w_in[0][:, c:c + n].rearrange("(k p) n -> p k n", p=P)

            sp.dma_start(x_in[:], x[0].rearrange("(t p) d -> p t d", p=P)).then_inc(x_loaded, 16)
            for g in range(4):
                sp.dma_start(wA[g][:], cols(256 * g, 256)).then_inc(wA_loaded[g], 16)
                if g == 0:
                    sp.wait_ge(vec_loaded, 16 * 14)
            sp.dma_start(mem_in[:], mem[0].rearrange("(t p) d -> p t d", p=P)).then_inc(mem_loaded, 16)
            sp.dma_start(wV[:], cols(2 * SB, SB)).then_inc(wV_loaded, 16)
            for g in range(3):
                sp.dma_start(wR[g][:], cols(3 * SB + 256 * g, 256)).then_inc(wR_loaded[g], 16)
            sp.dma_start(w_kv[:], w_mem_kv[0].rearrange("(k p) n -> p k n", p=P)).then_inc(kv_loaded, 16)
            sp.wait_ge(unit_ps, 8)
            sp.dma_start(wo[:], w_out[0].rearrange("(k p) n -> p k n", p=P)).then_inc(wo_loaded, 16)
            sp.wait_ge(memT_ps, 4)
            load_expert(sp, 0, w_gate_sh[0], w_up_sh[0], w_down_sh[0])
            load_expert(sp, 1, w_gate_e[0, 0], w_up_e[0, 0], w_down_e[0, 0])
            sp.wait_ge(unit_ps, 20)
            for e in (1, 2):
                load_expert(sp, slot(e), w_gate_e[0, e], w_up_e[0, e], w_down_e[0, e])
            sp.wait_ge(s_down_ps, 1)
            load_expert(sp, slot(3), w_gate_e[0, 3], w_up_e[0, 3], w_down_e[0, 3])
            sp.wait_ge(cum_dve, 1)
            with sp.Fori(0, (NE - 4) // 4) as i:
                for half in range(2):
                    p = 2 * i + half
                    done = nc.sync.value_load(cum[0:1, bass.ds(2 * p + 2, 1)], min_val=0, max_val=NE)
                    sp.wait_ge(ov_gu_ps, 2 * done + 1)
                    sp.wait_ge(gu_ps, 2 * p + 2)
                    for side in range(2):
                        e = 4 * i + 2 * half + side + 4
                        n = slot(2 * half + side)
                        sp.dma_start(ring_gu[n][:, 0], w_gate_e[0, bass.ds(e, 1)].rearrange("o (p k) n -> p (o k) n", k=KD)).then_inc(gu_loaded[n], 16)
                        sp.dma_start(ring_gu[n][:, 1], w_up_e[0, bass.ds(e, 1)].rearrange("o (p k) n -> p (o k) n", k=KD)).then_inc(gu_loaded[n], 16)
                    sp.wait_ge(y_ps, 2 * p + 2)
                    for side in range(2):
                        e = 4 * i + 2 * half + side + 4
                        n = slot(2 * half + side)
                        sp.dma_start(ring_d[n][:], w_down_e[0, bass.ds(e, 1)].rearrange("o (p k) n -> p (o k) n", k=KH)).then_inc(d_loaded[n], 16)
            for c in range(NT):
                sp.wait_ge(out_dve, 2 * c + 2)
                sp.dma_start(out[0, c * P:(c + 1) * P, :], x1[:, c, :]).then_inc(stored, 16)
            sp.wait_ge(stored, 16 * NT)

        @block.gpsimd
        def _(pool):
            chain = [0]

            def link(ins):
                chain[0] += 1
                ins.then_inc(pool_chain, 1)
                pool.wait_ge(pool_chain, chain[0])

            def diagonal(t, value_off, cmp, lo, n):
                return pool.affine_select(out=t, in_=t, compare_op=cmp, fill=value_off, base=lo, pattern=[[-1, n]],
                                          channel_multiplier=1)

            link(pool.memset(ident[:], 0.0))
            diagonal(ident[:], 1.0, ALU.not_equal, 0, P).then_inc(consts, 1)
            link(pool.memset(ones[:], 1.0))
            link(pool.memset(ones_b[:], 1.0))
            link(pool.memset(block_ones[:], 0.0))
            link(pool.memset(block_ones[0:HD, 0:HD], 1.0))
            link(pool.memset(block_ones[HD:P, HD:P], 1.0))
            link(pool.memset(zeros[:], 0.0))
            link(pool.memset(xpad[:, :, 0:3], 0.0))
            link(pool.memset(cnt_row[:], 0.0))
            link(pool.memset(upper[:], 1.0))
            link(pool.affine_select(out=upper[:], in_=upper[:], compare_op=ALU.is_gt, fill=0.0, base=0,
                                    pattern=[[1, P]], channel_multiplier=-1))
            link(pool.iota(iota1[:], pattern=[[1, SEQ + SLOTS]], base=1, channel_multiplier=0,
                           allow_small_or_imprecise_dtypes=True))
            pool.memset(grp[:], HUGE).then_inc(consts, 1)
            pool.wait_ge(unit_ps, 10)
            for b in range(2):
                link(pool.memset(rest[b][:, P:P + 1], 1.0))
                last = pool.memset(rest[b][:, NZ + 1:NZ + 2], 1.0)
                link(last)
            pool.memset(stat[:, 15:16], 0.0).then_inc(zeroed, 1)
            for kind, h in walk:
                if kind != "z":
                    continue
                pool.wait_ge(bc_act, 2 * h + 2)
                for t, off in ((keep[h % 2], 1.0), (beta[h % 2], 0.0)):
                    for c in (0, 2):
                        last = pool.affine_select(out=t[:, c * P:(c + 1) * P], in_=t[:, c * P:(c + 1) * P],
                                                  compare_op=ALU.is_gt, fill=off, base=0, pattern=[[-1, P]],
                                                  channel_multiplier=1)
                        last.then_inc(mask_pool, 1)
            pool.wait_ge(z_ps, SB_HEADS)
            pool.wait_ge(o_ps, SB_HEADS)
            pool.dma_start(x1[:], x[0].rearrange("(t p) d -> p t d", p=P)).then_inc(x1_loaded, 16)
            pool.dma_start(w_rt[:], w_router[0].rearrange("(p k) e -> p k e", k=KD)).then_inc(rt_loaded, 16)
            pool.dma_start(rbias[:], router_bias[0].partition_broadcast(P)).then_inc(rb_loaded, 16)
            pool.wait_ge(unit_ps, 28)
            pool.wait_ge(yrg_dve, 2)
            pool.dma_start(g_ffn[:], norm_ffn_g[0].partition_broadcast(P)).then_inc(gffn_loaded, 16)
            pool.wait_ge(s_gu_ps, 2)
            link(pool.memset(yhi[:].bitcast(F32), 0.0))
            link(pool.memset(ylo[:].bitcast(F32), 0.0))
            pool.memset(S[1][:].bitcast(F32), 0.0).then_inc(zeroed, 1)

        @block.scalar
        def _(act):
            chain = [0]

            def link(ins):
                chain[0] += 1
                ins.then_inc(act_chain, 1)
                act.wait_ge(act_chain, chain[0])

            def rows(v, n):
                return v.rearrange("(a p) -> a p", a=n)

            at_row = 0
            vlist = [(norm_mix_g[0], 8), (norm_mem_g[0], 8), (g_out_sb[0], 4), (g_out_rg[0], 2), (g_out_ca[0], 2),
                     (conv_w[0].rearrange("t c -> (t c)"), 8), (conv_b[0], 2), (b_rgate[0], 2), (b_igate[0], 2),
                     (lru_lambda[0], 2)]
            for v, n in vlist:
                act.dma_start(vecs[at_row:at_row + n, :], rows(v, n)).then_inc(vec_loaded, 16)
                at_row += n
            for i, v in enumerate((q_norm_g[0], k_norm_g[0])):
                for half in range(2):
                    act.dma_start(vecs[QN + i:QN + i + 1, half * HD:(half + 1) * HD], rows(v, 1)).then_inc(vec_loaded, 16)
            for w, t in ((w_rgate, wg_r), (w_igate, wg_i)):
                wv = w[0].rearrange("(j two) c d -> two c j d", two=2)
                for half in range(2):
                    act.dma_start(t[half * HD:(half + 1) * HD], wv[half]).then_inc(wg_loaded, 16)

            def squares(src, col, n0):
                for t in range(NT):
                    if n0 + t:
                        act.wait_ge(ssq_act, n0 + t)
                    nc.scalar.activation(ps[:, 6:8, :], src[:, t, :].rearrange("p (a b) -> p a b", a=2), ACT.Square,
                                         accum_out=stat[:, col + t:col + t + 1]).then_inc(ssq_act, 1)

            def root(col, n):
                act.wait_ge(xn_dve, n)
                nc.scalar.activation(stat[:, col + 2:col + 4], stat[:, col + 2:col + 4], ACT.Sqrt).then_inc(std_act, 1)

            act.wait_ge(x_loaded, 16)
            squares(x_in, 0, 0)
            root(0, 1)
            act.wait_ge(vec_dve, 1)
            for k in ACT_K:
                act.wait_ge(xT_ps, k // 2 + 1)
                nc.scalar.mul(hT[:, k, :], ps[:, k // 2, k % 2 * SEQ:(k % 2 + 1) * SEQ], vec[:, MIX + k:MIX + k + 1]).then_inc(xT_act, 1)
            act.wait_ge(mem_loaded, 16)
            squares(mem_in, 4, 2)
            root(4, 4)
            act.wait_ge(lam_dve, 1)
            nc.scalar.activation(lam[:, 1, :], lam[:, 0, :], ACT.Exp).then_inc(lam_act, 1)

            def evac(n):
                act.wait_ge(unit_ps, n + 1)
                b = ps[:, n % 4, :]
                if n < 8:
                    nc.scalar.copy(qk[:, n, :], b[:, 0:SEQ]).then_inc(unit_act, 1)
                elif n < 10:
                    nc.scalar.copy(v_sb[:, n - 8, :], b).then_inc(unit_act, 1)
                elif n < 12:
                    nc.scalar.copy(xpad[:, n - 10, 3:3 + SEQ], b[:, 0:SEQ]).then_inc(unit_act, 1)
                elif n < 14:
                    nc.scalar.copy(gate[:, n - 12, :], b[:, 0:SEQ]).then_inc(unit_act, 1)
                elif n < 18:
                    nc.scalar.copy(qkca[:, n - 14, :], b[:, 0:SEQ]).then_inc(unit_act, 1)
                elif n < 20:
                    nc.scalar.copy(v_ca[:, n - 18, :], b[:, 0:SEQ]).then_inc(unit_act, 1)
                else:
                    dst, bias = (rg_r, BR) if n == 20 else (rg_i, BI)
                    link(nc.scalar.activation(dst[:, 0, :], b[:, 0:SEQ], ACT.Sigmoid, bias=vec[:, bias:bias + 1]))
                    nc.scalar.activation(dst[:, 1, :], b[:, SEQ:2 * SEQ], ACT.Sigmoid,
                                         bias=vec[:, bias + 1:bias + 2]).then_inc(unit_act, 1)

            for kind, n in walk:
                if kind == "unit" and owner[n] == "act":
                    evac(n)
                elif kind == "memT":
                    for k in ACT_K:
                        act.wait_ge(memT_ps, k // 2 + 1)
                        nc.scalar.mul(memT[:, k, :], ps[:, 4 + k // 2, k % 2 * SEQ:(k % 2 + 1) * SEQ],
                                      vec[:, MEM + k:MEM + k + 1]).then_inc(memT_act, 1)
                elif kind == "z":
                    act.wait_ge(z_ps, n + 1)
                    if n >= 2:
                        act.wait_ge(wT_ps, n - 1)
                    zb = ps[:, 4 + n % 2, 0:NZ]
                    nc.scalar.activation(beta[n % 2][:], zb, ACT.Sigmoid, scale=SCALE).then_inc(bc_act, 1)
                    nc.scalar.activation(keep[n % 2][:], zb, ACT.Sigmoid, scale=-SCALE).then_inc(bc_act, 1)
                elif kind == "t":
                    act.wait_ge(wT_ps, n + 1)
                    nc.scalar.copy(wT[n % 2][:], ps[:, 6, 0:NZ]).then_inc(wT_act, 1)
            freed(act, 17)
            freed(act, 16)
            for i in range(2):
                nc.scalar.activation(ca_sq[:, i, :], qkca[:, 2 * i:2 * i + 2, :].rearrange("p a b -> p (a b)"),
                                     ACT.Square).then_inc(sq_act, 1)
            act.wait_ge(gelu_dve, 1)
            nc.scalar.activation(rg_g[:], rg_g[:], ACT.Sigmoid, scale=2.0 * 0.7978845608028654).then_inc(gelu_act, 1)
            act.wait_ge(lam_dve, 2)
            act.wait_ge(unit_act, owner[:22].count("act"))
            for c in range(2):
                nc.scalar.activation(rg_t[:, c, :], rg_r[:, c, :], ACT.Tanh, scale=lam[:, 7, c:c + 1]).then_inc(rg_act, 1)
            for c in range(2):
                nc.scalar.activation(rg_a[:, c, :], rg_r[:, c, :], ACT.Exp, scale=lam[:, 7, c:c + 1]).then_inc(rg_act, 1)
            freed(act, 23)
            for i in range(2):
                nc.scalar.activation(ca_rs[:, i, :], ca_rs[:, i, :], ACT.Sqrt).then_inc(car_act, 1)
            act.wait_ge(rg_dve, 1)
            nc.scalar.activation(rg_t[:], rg_t[:], ACT.Sqrt, scale=-2.0).then_inc(rg_act, 1)
            for h in range(CA_HEADS):
                act.wait_ge(camax_dve, h + 1)
                if h >= 2:
                    act.wait_ge(unit_ps, 28 + h - 2 + 1)
                for t in range(NT):
                    ins = nc.scalar.activation(ca_p[h % 2][:, t, :], ps[:, h % 4, t * SEQ:(t + 1) * SEQ], ACT.Exp,
                                               bias=mx[:, t, h:h + 1], scale=SCALE,
                                               accum_out=stat[:, 8 + 2 * (h % 2) + t:9 + 2 * (h % 2) + t])
                    if t == 0:
                        link(ins)
                    else:
                        ins.then_inc(unit_act, 1)
            for k, (sem, n) in enumerate([(yT_dve, 1), (yT_dve, 2), (yT_dve, 3), (yT_dve, 4),
                                          (yrg_dve, 1), (yrg_dve, 2), (oca_dve, 1), (oca_dve, 2)]):
                act.wait_ge(sem, n)
                if k == 0:
                    act.wait_ge(yrg_dve, 2)
                    act.wait_ge(oca_dve, 2)
                nc.scalar.activation(y_sq[:, k, :], yT[:, k, :], ACT.Square).then_inc(ysq_act, 1)
            act.wait_ge(yrs_dve, 3)
            nc.scalar.activation(y_rs[:], y_rs[:], ACT.Sqrt).then_inc(yrs_act, 1)
            act.wait_ge(x1_dve, 4)
            squares(x1, 0, 4)
            root(0, 7)
            for k in ACT_K:
                act.wait_ge(x2T_ps, k // 2 + 1)
                nc.scalar.copy(xn2T[:, k, :], ps[:, k // 2, k % 2 * SEQ:(k % 2 + 1) * SEQ]).then_inc(x2T_act, 1)
            for t in range(NT):
                act.wait_ge(xn_dve, 9)
                nc.scalar.copy(xhi[:, t], xn2[:, t]).then_inc(split_act, 1)
            act.wait_ge(rt_ps, 1)
            nc.scalar.activation(score[:], ps[:, 4, 0:NT * NE].rearrange("p (t e) -> p t e", t=NT),
                                 ACT.Sigmoid).then_inc(score_act, 1)
            for t in range(NT):
                act.wait_ge(s_gu_ps, t + 1)
                nc.scalar.activation(s_sg[:, t, :], ps[:, t, 0:DE], ACT.Silu).then_inc(s_sg_act, 1)
            for i in range(KD // 2):
                act.wait_ge(gather_ps, 2 * i + 1)
                nc.scalar.copy(xg[0][:, 2 * i, :], ps[:, Y[0], :]).then_inc(xg_act, 1)

            def overflow(p):
                lo = nc.scalar.value_load(cum[0:1, bass.ds(2 * p, 1)], min_val=0, max_val=NE)
                hi = nc.scalar.value_load(cum[0:1, bass.ds(2 * p + 2, 1)], min_val=0, max_val=NE)
                with nc.scalar.If(hi > lo):
                    with nc.scalar.Fori(lo, hi) as j:
                        act.wait_ge(ov_gather_ps, 2 * j + 1)
                        nc.scalar.copy(ov_xg[:, 0:4, :], ps[:, Y[0], :].rearrange("p (a b) -> p a b", a=4)).then_inc(ov_xg_act, 1)
                        act.wait_ge(ov_pt_ps, j + 1)
                        nc.scalar.copy(ov_S[:], ps[:, T, 0:SEQ]).then_inc(ov_S_act, 1)
                        act.wait_ge(ov_gu_ps, 2 * j + 3)
                        act.wait_ge(h_dve, p + 1)
                        nc.scalar.activation(e_sg[:], ps[:, U, 0:DE], ACT.Silu).then_inc(ov_sg_act, 1)
                        act.wait_ge(ov_gslot_dve, 2 * j + 2)
                        for half in range(2):
                            act.wait_ge(ov_y_ps, 2 * j + half + 1)
                            nc.scalar.mul(yhi[:, half * 512:(half + 1) * 512], ps[:, Y[half], :],
                                          ov_gslot[:]).then_inc(ov_yhi_act, 1)

            def octets(it, gather_last):
                for j in range(8):
                    p, o, q, ob = 8 * it + j, 2 * it + j // 4, j % 4, j // 4
                    act.wait_ge(gu_ps, 2 * p + 2)
                    nc.scalar.activation(e_sg[:], ps[:, U, 0:DE], ACT.Silu).then_inc(sg_act, 1)
                    overflow(p)
                    if ob == 0 or gather_last:
                        act.wait_ge(gather_ps, 8 * (o + 1) + 2 * q + 1)
                        nc.scalar.copy(xg[1 - ob][:, 2 * q, :], ps[:, Y[0], :]).then_inc(xg_act, 1)
                    act.wait_ge(pt_ps, p + 2)
                    nc.scalar.copy(S[j % 2][:], ps[:, T, 0:SEQ]).then_inc(S_act, 1)
                    act.wait_ge(gslot_dve, 2 * p + 2)
                    for half in range(2):
                        act.wait_ge(y_ps, 2 * p + half + 1)
                        nc.scalar.mul(yhi[:, half * 512:(half + 1) * 512], ps[:, Y[half], :],
                                      gslot[:, j % 2:j % 2 + 1]).then_inc(yhi_act, 1)

            act.sem_inc(S_act, 1)
            act.sem_inc(yhi_act, 1)
            act.wait_ge(cum_dve, 1)
            with act.Fori(0, PAIRS // 8 - 1) as it:
                octets(it, True)
            octets(PAIRS // 8 - 1, False)

        @block.vector
        def _(dve):
            chain = [0]

            def link(ins):
                chain[0] += 1
                ins.then_inc(dve_chain, 1)
                dve.wait_ge(dve_chain, chain[0])

            def mean_eps(col, n_ssq):
                dve.wait_ge(ssq_act, n_ssq)
                nc.vector.tensor_scalar(stat[:, col + 2:col + 4], stat[:, col:col + 2], 1.0 / D, EPS, ALU.mult,
                                        ALU.add).then_inc(xn_dve, 1)

            def scale_rows(src, dst, col, n_std):
                dve.wait_ge(std_act, n_std)
                link(nc.vector.reciprocal(stat[:, col + 2:col + 4], stat[:, col + 2:col + 4]))
                for t in range(NT):
                    nc.vector.tensor_scalar(dst[:, t, :], src[:, t, :], stat[:, col + 2 + t:col + 3 + t], None,
                                            ALU.mult).then_inc(xn_dve, 1)

            mean_eps(0, 2)
            scale_rows(x_in, xn, 0, 1)
            dve.wait_ge(vec_ps, 1)
            nc.vector.tensor_copy(vec[:], ps[:, 5, 0:42]).then_inc(vec_dve, 1)
            dve.wait_ge(vec_dve, 1)
            for k in DVE_K:
                dve.wait_ge(xT_ps, k // 2 + 1)
                nc.vector.tensor_scalar(hT[:, k, :], ps[:, k // 2, k % 2 * SEQ:(k % 2 + 1) * SEQ], vec[:, MIX + k:MIX + k + 1], None,
                                        ALU.mult).then_inc(xT_dve, 1)
            mean_eps(4, 4)
            scale_rows(mem_in, memn, 4, 2)
            link(nc.vector.tensor_scalar(lam[:, 2, :], vec[:, LAM:LAM + 2], -1.0, None, ALU.mult))
            nc.vector.tensor_tensor(lam[:, 0, :], vec[:, LAM:LAM + 2], lam[:, 2, :], ALU.min).then_inc(lam_dve, 1)

            def log1p():
                dve.wait_ge(lam_act, 1)
                e = lam[:, 1, :]
                link(nc.vector.tensor_scalar(lam[:, 3, :], e, 2.0, None, ALU.add))
                link(nc.vector.reciprocal(lam[:, 3, :], lam[:, 3, :]))
                link(nc.vector.tensor_tensor(lam[:, 3, :], e, lam[:, 3, :], ALU.mult))
                link(nc.vector.tensor_tensor(lam[:, 4, :], lam[:, 3, :], lam[:, 3, :], ALU.mult))
                terms = 9
                link(nc.vector.tensor_scalar(lam[:, 5, :], lam[:, 4, :], 2.0 / (2 * terms + 1), 2.0 / (2 * terms - 1),
                                             ALU.mult, ALU.add))
                for n in range(terms - 2, -1, -1):
                    link(nc.vector.tensor_tensor(lam[:, 5, :], lam[:, 5, :], lam[:, 4, :], ALU.mult))
                    link(nc.vector.tensor_scalar(lam[:, 5, :], lam[:, 5, :], 2.0 / (2 * n + 1), None, ALU.add))
                link(nc.vector.tensor_tensor(lam[:, 5, :], lam[:, 5, :], lam[:, 3, :], ALU.mult))
                link(nc.vector.tensor_scalar(lam[:, 6, :], lam[:, 2, :], 0.0, None, ALU.max))
                link(nc.vector.tensor_tensor(lam[:, 6, :], lam[:, 6, :], lam[:, 5, :], ALU.add))
                nc.vector.tensor_scalar(lam[:, 7, :], lam[:, 6, :], -8.0, None, ALU.mult).then_inc(lam_dve, 1)

            def evac(n):
                dve.wait_ge(unit_ps, n + 1)
                b = ps[:, n % 4, :]
                if n < 8:
                    dst, src = qk[:, n, :], b[:, 0:SEQ]
                elif n < 10:
                    dst, src = v_sb[:, n - 8, :], b
                elif n < 12:
                    dst, src = xpad[:, n - 10, 3:3 + SEQ], b[:, 0:SEQ]
                elif n < 14:
                    dst, src = gate[:, n - 12, :], b[:, 0:SEQ]
                elif n < 18:
                    dst, src = qkca[:, n - 14, :], b[:, 0:SEQ]
                else:
                    dst, src = v_ca[:, n - 18, :], b[:, 0:SEQ]
                nc.vector.tensor_copy(dst, src).then_inc(unit_dve, 1)

            def conv():
                dve.wait_ge(unit_ps, 16)
                freed(dve, 10)
                freed(dve, 11)
                freed(dve, 12)
                freed(dve, 13)
                for c in range(2):
                    link(nc.vector.tensor_scalar(xc[:, c, :], xpad[:, c, 3:3 + SEQ], vec[:, CW + 6 + c:CW + 7 + c],
                                                 vec[:, CB + c:CB + c + 1], ALU.mult, ALU.add))
                    for tap in range(3):
                        ins = nc.vector.scalar_tensor_tensor(xc[:, c, :], xpad[:, c, tap:tap + SEQ],
                                                             vec[:, CW + 2 * tap + c:CW + 2 * tap + c + 1], xc[:, c, :],
                                                             ALU.mult, ALU.add)
                        if tap < 2:
                            link(ins)
                        else:
                            ins.then_inc(conv_dve, 1)
                link(nc.vector.tensor_tensor(rg_g[:], gate[:], gate[:], ALU.mult))
                link(nc.vector.tensor_scalar(rg_g[:], rg_g[:], 0.044715, 1.0, ALU.mult, ALU.add))
                nc.vector.tensor_tensor(rg_g[:], rg_g[:], gate[:], ALU.mult).then_inc(gelu_dve, 1)

            for kind, n in walk:
                if kind == "unit" and owner[n] == "dve":
                    evac(n)
                    if n == 7:
                        log1p()
                elif kind == "memT":
                    for k in DVE_K:
                        dve.wait_ge(memT_ps, k // 2 + 1)
                        nc.vector.tensor_scalar(memT[:, k, :], ps[:, 4 + k // 2, k % 2 * SEQ:(k % 2 + 1) * SEQ],
                                                vec[:, MEM + k:MEM + k + 1], None, ALU.mult).then_inc(memT_dve, 1)
                elif kind == "z":
                    if n == 0:
                        dve.wait_ge(zeroed, 1)
                    dve.wait_ge(mask_pool, 4 * n + 4)
                    b = n % 2
                    kp, rs = keep[b], rest[b]
                    nc.vector.tensor_tensor_scan(rs[:, 0:P][:, ::-1], kp[:, 0:P][:, ::-1], zeros[:, 0:P], 1.0,
                                                 ALU.mult, ALU.add).then_inc(dve_chain, 1)
                    nc.vector.tensor_tensor_scan(rs[:, P + 1:NZ + 1][:, ::-1], kp[:, P:NZ][:, ::-1], zeros[:], 1.0,
                                                 ALU.mult, ALU.add).then_inc(dve_chain, 1)
                    chain[0] += 2
                    dve.wait_ge(dve_chain, chain[0])
                    nc.vector.tensor_tensor(beta[b][:, 0:P], beta[b][:, 0:P], rs[:, 1:P + 1], ALU.mult).then_inc(w_dve, 1)
                    nc.vector.tensor_tensor(beta[b][:, P:NZ], beta[b][:, P:NZ], rs[:, P + 2:NZ + 2],
                                            ALU.mult).then_inc(w_dve, 1)
                elif kind == "av":
                    if n % 2:
                        dve.wait_ge(o_ps, n + 1)
                        c = (n // 2) % 2 * SEQ
                        nc.vector.tensor_copy(yT[:, n // 2, :], ps[:, 7, c:c + SEQ]).then_inc(yT_dve, 1)
                elif kind == "conv":
                    conv()
            for i in range(2):
                dve.wait_ge(unit_ps, 23 + i)
                nc.vector.tensor_scalar(ca_rs[:, i, :], ps[:, (22 + i) % 4, :], 1.0 / HD, EPS, ALU.mult,
                                        ALU.add).then_inc(unit_dve, 1)
            dve.wait_ge(rg_act, 2)
            link(nc.vector.tensor_scalar(rg_u[:], rg_t[:], -1.0, 1.0, ALU.mult, ALU.add))
            link(nc.vector.reciprocal(rg_u[:], rg_u[:]))
            nc.vector.tensor_tensor(rg_t[:], rg_t[:], rg_u[:], ALU.mult).then_inc(rg_dve, 1)
            dve.wait_ge(car_act, 2)
            link(nc.vector.reciprocal(ca_rs[:], ca_rs[:]))
            for i in range(4):
                nc.vector.scalar_tensor_tensor(qkca[:, i, :], qkca[:, i, :], vec[:, QN + i // 2:QN + i // 2 + 1],
                                               ca_rs[:, i // 2, (i % 2) * SEQ:(i % 2 + 1) * SEQ], ALU.mult,
                                               ALU.mult).then_inc(can_dve, 1)

            def ca_max(h):
                dve.wait_ge(unit_ps, 25 + h)
                link(nc.vector.reduce_max(mx[:, :, h], ps[:, h % 4, :].rearrange("p (t m) -> p t m", t=NT), AX.X))
                nc.vector.tensor_scalar(mx[:, :, h], mx[:, :, h], -SCALE, None, ALU.mult).then_inc(camax_dve, 1)

            def ca_norm(h):
                b = h % 2
                dve.wait_ge(unit_act, owner[:24 + h + 1].count("act"))
                sums = stat[:, 8 + 2 * b:10 + 2 * b]
                link(nc.vector.reciprocal(sums, sums))
                for t in range(NT):
                    nc.vector.tensor_scalar(ca_p[b][:, t, :], ca_p[b][:, t, :], stat[:, 8 + 2 * b + t:9 + 2 * b + t],
                                            None, ALU.mult).then_inc(cap_dve, 1)

            def ca_evac(h):
                dve.wait_ge(unit_ps, 29 + h)
                if h == 2:
                    dve.wait_ge(oca_ps, 1)
                if h == 3:
                    dve.wait_ge(unit_ps, 33)
                nc.vector.tensor_copy(ca_pT[h % 2][:], ps[:, h % 4, :].rearrange("p (m q) -> p m q", m=2)).then_inc(unit_dve, 1)

            for h in range(CA_HEADS):
                ca_max(h)
            dve.wait_ge(rg_act, 5)
            link(nc.vector.tensor_tensor(rg_u[:], rg_i[:], xc[:], ALU.mult))
            link(nc.vector.tensor_tensor(rg_u[:], rg_u[:], rg_t[:], ALU.mult))
            for c in range(2):
                link(nc.vector.tensor_tensor_scan(rg_r[:, c, :], rg_a[:, c, :], rg_u[:, c, :], 0.0, ALU.mult, ALU.add))
            dve.wait_ge(gelu_act, 1)
            link(nc.vector.tensor_tensor(rg_g[:], rg_g[:], gate[:], ALU.mult))
            for c in range(2):
                nc.vector.tensor_tensor(yT[:, 4 + c, :], rg_g[:, c, :], rg_r[:, c, :], ALU.mult).then_inc(yrg_dve, 1)
            for h in range(CA_HEADS):
                ca_norm(h)
                if h >= 1:
                    ca_evac(h - 1)
            ca_evac(CA_HEADS - 1)
            for j in range(2):
                dve.wait_ge(unit_ps, 33 + j)
                nc.vector.tensor_copy(yT[:, 6 + j, :], ps[:, (32 + j) % 4, 0:SEQ]).then_inc(oca_dve, 1)
            for g, width in enumerate((SB, RG, CA)):
                dve.wait_ge(unit_ps, 35 + g)
                nc.vector.tensor_scalar(y_rs[:, g, :], ps[:, (34 + g) % 4, 0:SEQ], 1.0 / width, EPS, ALU.mult,
                                        ALU.add).then_inc(yrs_dve, 1)
            dve.wait_ge(yrs_act, 1)
            link(nc.vector.reciprocal(y_rs[:], y_rs[:]))
            for k in range(KD):
                g = 0 if k < 4 else 1 if k < 6 else 2
                nc.vector.scalar_tensor_tensor(yT[:, k, :], yT[:, k, :], vec[:, GOUT + k:GOUT + k + 1], y_rs[:, g, :],
                                               ALU.mult, ALU.mult).then_inc(yn_dve, 1)
            dve.wait_ge(x1_loaded, 16)
            for t in range(NT):
                for half in range(2):
                    dve.wait_ge(wo_ps, 2 * t + half + 1)
                    c = slice(half * 512, (half + 1) * 512)
                    nc.vector.tensor_tensor(x1[:, t, c], x1[:, t, c], ps[:, ACC[2 * t + half], :], ALU.add).then_inc(x1_dve, 1)
            mean_eps(0, 6)
            dve.wait_ge(std_act, 3)
            link(nc.vector.reciprocal(stat[:, 2:4], stat[:, 2:4]))
            dve.wait_ge(gffn_loaded, 16)
            for t in range(NT):
                nc.vector.scalar_tensor_tensor(xn2[:, t], x1[:, t, :].rearrange("q (p k) -> q k p", k=KD),
                                               stat[:, 2 + t:3 + t], g_ffn[:].rearrange("q (p k) -> q k p", k=KD),
                                               ALU.mult, ALU.mult).then_inc(xn_dve, 1)
            for k in DVE_K:
                dve.wait_ge(x2T_ps, k // 2 + 1)
                nc.vector.tensor_copy(xn2T[:, k, :], ps[:, k // 2, k % 2 * SEQ:(k % 2 + 1) * SEQ]).then_inc(x2T_dve, 1)
            dve.wait_ge(score_act, 1)
            dve.wait_ge(rb_loaded, 16)
            dve.wait_ge(consts, 2)
            link(nc.vector.tensor_tensor(choice[:], score[:], rbias[:].unsqueeze(1).to_broadcast([P, NT, NE]), ALU.add))
            for t in range(NT):
                for g in range(GROUPS):
                    link(nc.vector.max(top8[:, t, g, :], choice[:, t, g * EG:(g + 1) * EG]))
            for t in range(NT):
                link(nc.vector.tensor_tensor(grp[:, t, 0:GROUPS], top8[:, t, :, 0], top8[:, t, :, 1], ALU.add))
                link(nc.vector.memset(grp[:, t, 12:16], -HUGE))
                link(nc.vector.max(gtop[:, t, :], grp[:, t, :]))
                link(nc.vector.match_replace(grep[:, t, :], gtop[:, t, :], grp[:, t, :], -HUGE))
                link(nc.vector.tensor_tensor(grep[:, t, 0:GROUPS], grep[:, t, 0:GROUPS], grp[:, t, 0:GROUPS], ALU.is_equal))
                m = grep[:, t, 0:GROUPS].unsqueeze(2).to_broadcast([P, GROUPS, EG])
                cg = cand[:, t, :].rearrange("p (g e) -> p g e", g=GROUPS)
                link(nc.vector.tensor_scalar(grp[:, t, 0:GROUPS], grep[:, t, 0:GROUPS], -1.0, 1.0, ALU.mult, ALU.add))
                link(nc.vector.tensor_scalar(grep[:, t, 0:GROUPS], grep[:, t, 0:GROUPS], -HUGE, None, ALU.mult))
                m1 = grp[:, t, 0:GROUPS].unsqueeze(2).to_broadcast([P, GROUPS, EG])
                link(nc.vector.tensor_tensor(cg, choice[:, t, :].rearrange("p (g e) -> p g e", g=GROUPS), m1, ALU.mult))
                link(nc.vector.tensor_tensor(cg, cg, m, ALU.add))
                link(nc.vector.max(gtop[:, t, :], cand[:, t, :]))
                link(nc.vector.match_replace(repl[:, t, :], gtop[:, t, :], cand[:, t, :], HUGE))
            link(nc.vector.tensor_scalar(repl[:], repl[:], HUGE, None, ALU.is_equal))
            nc.vector.tensor_copy(picked[:], repl[:]).then_inc(route_dve, 1)
            link(nc.vector.tensor_tensor(gatew[:], repl[:], score[:], ALU.mult))
            link(nc.vector.reduce_sum(stat[:, 4:6], gatew[:], AX.X))
            link(nc.vector.tensor_scalar(stat[:, 4:6], stat[:, 4:6], 1e-20, None, ALU.add))
            link(nc.vector.reciprocal(stat[:, 4:6], stat[:, 4:6]))
            for t in range(NT):
                link(nc.vector.tensor_scalar(gatew[:, t, :], gatew[:, t, :], stat[:, 4 + t:5 + t], 2.5, ALU.mult, ALU.mult))
            g4 = gatew[:].rearrange("p t (n two) -> p t n two", two=2)
            link(nc.vector.tensor_copy(gates2[:, :, :, 0:2], g4))
            link(nc.vector.tensor_tensor(gates2[:, :, :, 2:4], g4, gates2[:, :, :, 0:2].bitcast(F32), ALU.subtract))
            dve.wait_ge(count_ps, 1)
            link(nc.vector.scalar_tensor_tensor(posm[:], ps[:, 5, 0:NT * NE].rearrange("p (t e) -> p t e", t=NT), 1.0,
                                                repl[:], ALU.add, ALU.mult))

            def build_pick(o, buf):
                for t in range(NT):
                    nc.vector.tensor_tensor(
                        pick[buf][:, t, :].rearrange("p (e s) -> p e s", s=SLOTS),
                        iota1[:, 0:SLOTS].unsqueeze(1).to_broadcast([P, 8, SLOTS]),
                        posm[:, t, bass.ds(8 * o, 8)].unsqueeze(2).to_broadcast([P, 8, SLOTS]),
                        ALU.is_equal).then_inc(pick_dve, 1)

            dve.wait_ge(unit_ps, 37)
            build_pick(0, 0)
            cr = cnt_row
            link(nc.vector.tensor_scalar(cr[:, 1, 0:NE], ps[0:1, 5, 2 * NE:3 * NE], float(SLOTS), None, ALU.is_gt))
            link(nc.vector.tensor_scalar(cr[:, 2, 0:NE], ps[0:1, 5, 2 * NE:3 * NE], float(SLOTS + P), None, ALU.is_gt))
            link(nc.vector.tensor_tensor(cr[:, 1, 0:NE], cr[:, 1, 0:NE], cr[:, 2, 0:NE], ALU.add))
            link(nc.vector.tensor_tensor_scan(cr[:, 0, 1:NE + 1], cr[:, 1, 0:NE], cr[:, 3, 0:NE], 0.0, ALU.add, ALU.add))
            nc.vector.tensor_copy(cum[:], cr[:, 0, :]).then_inc(cum_dve, 1)
            for t in range(NT):
                dve.wait_ge(split_act, t + 1)
                nc.vector.tensor_tensor(xlo[:, t], xn2[:, t], xhi[:, t].bitcast(F32), ALU.subtract).then_inc(split_dve, 1)
            for t in range(NT):
                dve.wait_ge(s_sg_act, t + 1)
                nc.vector.tensor_tensor(s_h[:, t].rearrange("q k p -> q p k"), s_sg[:, t, :].rearrange("q (p k) -> q p k", k=KH),
                                        ps[:, t, DE:2 * DE].rearrange("q (p k) -> q p k", k=KH), ALU.mult).then_inc(s_h_dve, 1)
            dve.wait_ge(s_hT_ps, 1)
            nc.vector.tensor_copy(s_hT[:], ps[:, 2, :].rearrange("p (k t) -> p k t", k=KH)).then_inc(s_hT_dve, 1)
            for i in range(KD // 2):
                dve.wait_ge(gather_ps, 2 * i + 2)
                nc.vector.tensor_copy(xg[0][:, 2 * i + 1, :], ps[:, Y[1], :]).then_inc(xg_dve, 1)
            dve.wait_ge(cum_dve, 1)

            def slot_gates(dst, sem, sides=(0, 1)):
                for part, side in enumerate(sides):
                    rws = slice(part * SLOTS, (part + 1) * SLOTS)
                    nc.vector.reduce_sum(dst[rws], ps[rws, T, SEQ + side:SEQ + side + 3:2], AX.X).then_inc(sem, 1)

            def hidden(dst, sem):
                nc.vector.tensor_tensor(dst[:].rearrange("q k p -> q p k"), e_sg[:].rearrange("q (p k) -> q p k", k=KH),
                                        ps[:, U, DE:2 * DE].rearrange("q (p k) -> q p k", k=KH), ALU.mult).then_inc(sem, 1)

            def hidden_T(sem):
                nc.vector.tensor_copy(e_hT[:], ps[:, U, 0:2 * P].rearrange("p (k t) -> p k t", k=KH)).then_inc(sem, 1)

            def overflow(p):
                c0 = nc.vector.value_load(cum[0:1, bass.ds(2 * p, 1)], min_val=0, max_val=NE)
                c2 = nc.vector.value_load(cum[0:1, bass.ds(2 * p + 2, 1)], min_val=0, max_val=NE)
                with nc.vector.If(c2 > c0):
                    c1 = nc.vector.value_load(cum[0:1, bass.ds(2 * p + 1, 1)], min_val=0, max_val=NE)
                    for side, lo, hi in ((0, c0, c1), (1, c1, c2)):
                        with nc.vector.If(hi > lo):
                            with nc.vector.Fori(lo, hi) as j:
                                overflow_item(2 * p + side, side, j, j - lo)

            def overflow_item(e, side, j, c):
                dve.wait_ge(ov_scatter_ps, j + 1)
                first = nc.s_assert_within(
                    c * P + SLOTS, SLOTS, SLOTS + P,
                    skip_runtime_bounds_check_because="an expert has at most 256 tokens, so at most two items")
                for t in range(NT):
                    nc.vector.tensor_tensor(ov_pick[:, t, :], iota1[:, bass.ds(first, P)],
                                            posm[:, t, bass.ds(e, 1)].to_broadcast([P, P]),
                                            ALU.is_equal).then_inc(ov_pick_dve, 1)
                dve.wait_ge(ov_gather_ps, 2 * j + 2)
                nc.vector.tensor_copy(ov_xg[:, 4:8, :], ps[:, Y[1], :].rearrange("p (a b) -> p a b", a=4)).then_inc(ov_xg_dve, 1)
                dve.wait_ge(ov_S_act, j + 1)
                slot_gates(ov_gslot[:], ov_gslot_dve, (side, side))
                dve.wait_ge(ov_sg_act, j + 1)
                hidden(ov_h, ov_h_dve)
                dve.wait_ge(ov_hT_ps, j + 1)
                hidden_T(ov_hTs_dve)
                dve.wait_ge(ov_gslot_dve, 2 * j + 2)
                for half in range(2):
                    dve.wait_ge(ov_yhi_act, 2 * j + half + 1)
                    c = slice(half * 512, (half + 1) * 512)
                    nc.vector.scalar_tensor_tensor(ylo[:, c], ps[:, Y[half], :], ov_gslot[:], yhi[:, c].bitcast(F32),
                                                   ALU.mult, ALU.subtract).then_inc(ov_ylo_dve, 1)

            def octets(it, gather_last):
                for j in range(8):
                    p, o, q, ob = 8 * it + j, 2 * it + j // 4, j % 4, j // 4
                    more = ob == 0 or gather_last
                    if q == 0 and more:
                        dve.wait_ge(pt_ps, p + 1)
                        build_pick(o + 1, 1 - ob)
                    dve.wait_ge(sg_act, p + 1)
                    hidden(e_h, h_dve)
                    overflow(p)
                    if more:
                        dve.wait_ge(gather_ps, 8 * (o + 1) + 2 * q + 2)
                        nc.vector.tensor_copy(xg[1 - ob][:, 2 * q + 1, :], ps[:, Y[1], :]).then_inc(xg_dve, 1)
                    dve.wait_ge(hT_ps, p + 1)
                    hidden_T(hTs_dve)
                    dve.wait_ge(S_act, p + 2)
                    slot_gates(gslot[:, j % 2:j % 2 + 1], gslot_dve)
                    dve.wait_ge(gslot_dve, 2 * p + 2)
                    for half in range(2):
                        dve.wait_ge(yhi_act, 2 * p + half + 2)
                        c = slice(half * 512, (half + 1) * 512)
                        nc.vector.scalar_tensor_tensor(ylo[:, c], ps[:, Y[half], :], gslot[:, j % 2:j % 2 + 1],
                                                       yhi[:, c].bitcast(F32), ALU.mult, ALU.subtract).then_inc(ylo_dve, 1)

            dve.sem_inc(hTs_dve, 1)
            dve.sem_inc(ylo_dve, 1)
            with dve.Fori(0, PAIRS // 8 - 1) as it:
                octets(it, True)
            octets(PAIRS // 8 - 1, False)
            for t in range(NT):
                for half in range(2):
                    dve.wait_ge(last_ps, 2 * t + half + 1)
                    c = slice(half * 512, (half + 1) * 512)
                    nc.vector.tensor_tensor(x1[:, t, c], x1[:, t, c], ps[:, ACC[2 * t + half], :], ALU.add).then_inc(out_dve, 1)

        @block.tensor
        def _(pe):
            mm = nc.tensor.matmul

            pe.wait_ge(consts, 1)
            pe.wait_ge(vec_loaded, 16 * 14)
            nc.tensor.transpose(ps[:, 5, 0:42], vecs[:], ident[0:42, 0:42]).then_inc(vec_ps, 1)

            def transposes(src, b0, sem):
                for k in range(KD):
                    for t in range(NT):
                        c = (k % 2) * SEQ + t * P
                        last = nc.tensor.transpose(ps[:, b0 + k // 2, c:c + P], src(t, k), ident[:])
                    if k % 2:
                        last.then_inc(sem, 1)

            pe.wait_ge(xn_dve, 3)
            transposes(lambda t, k: xn[:, t, k * P:(k + 1) * P], 0, xT_ps)
            pe.wait_ge(xT_act, KD // 2)
            pe.wait_ge(xT_dve, KD // 2)

            def unit(n):
                if n >= 4:
                    freed(pe, n - 4)
                b = ps[:, n % 4, :]
                if n < 8 or 10 <= n < 18:
                    if n < 8:
                        pe.wait_ge(wA_loaded[n // 2], 16)
                        w, c, act_T = wA[n // 2], n % 2 * P, hT
                    elif n < 16:
                        pe.wait_ge(wR_loaded[(n - 10) // 2], 16)
                        w, c, act_T = wR[(n - 10) // 2], n % 2 * P, hT
                    else:
                        pe.wait_ge(kv_loaded, 16)
                        pe.wait_ge(memT_act, KD // 2)
                        pe.wait_ge(memT_dve, KD // 2)
                        w, c, act_T = w_kv, n % 2 * P, memT
                    for k in range(KD):
                        last = mm(b[:, 0:SEQ], w[:, k, c:c + P], act_T[:, k, :], start=k == 0, stop=k == KD - 1)
                elif n < 10:
                    pe.wait_ge(wV_loaded, 16)
                    for k in range(KD):
                        last = mm(b, hT[:, k, (n - 8) * P:(n - 7) * P], wV[:, k, :], start=k == 0, stop=k == KD - 1)
                elif n < 20:
                    for k in range(KD):
                        last = mm(b[:, 0:CA], memT[:, k, (n - 18) * P:(n - 17) * P], w_kv[:, k, CA:2 * CA],
                                  start=k == 0, stop=k == KD - 1)
                elif n < 22:
                    pe.wait_ge(conv_dve, 2)
                    pe.wait_ge(wg_loaded, 64)
                    w = wg_r if n == 20 else wg_i
                    for c in range(2):
                        for half in range(2):
                            rws = slice(half * HD, (half + 1) * HD)
                            last = mm(b[rws, c * SEQ:(c + 1) * SEQ], w[rws, c, :], xc[rws, c, :], start=True, stop=True)
                elif n < 24:
                    pe.wait_ge(sq_act, n - 21)
                    last = mm(b, block_ones[:], ca_sq[:, n - 22, :], start=True, stop=True)
                elif n < 28:
                    h = n - 24
                    rws = slice(h % 2 * HD, (h % 2 + 1) * HD)
                    pe.wait_ge(can_dve, 4)
                    for t in range(NT):
                        last = mm(b[:, t * SEQ:(t + 1) * SEQ], qkca[rws, h // 2, t * P:(t + 1) * P],
                                  qkca[rws, 2 + h // 2, :], start=True, stop=True)
                elif n < 32:
                    h = n - 28
                    pe.wait_ge(cap_dve, 2 * h + 2)
                    for m in range(2):
                        for t in range(NT):
                            c = m * SEQ + t * P
                            last = nc.tensor.transpose(b[:, c:c + P], ca_p[h % 2][:, t, m * P:(m + 1) * P], ident[:])
                last.then_inc(unit_ps, 1)

            for kind, n in walk:
                if kind == "unit":
                    unit(n)
                elif kind == "memT":
                    pe.wait_ge(xn_dve, 6)
                    transposes(lambda t, k: memn[:, t, k * P:(k + 1) * P], 4, memT_ps)
                    pe.wait_ge(memT_act, KD // 2)
                    pe.wait_ge(memT_dve, KD // 2)
                elif kind == "z":
                    if n == 0:
                        freed(pe, 6)
                        freed(pe, 7)
                    if n >= 2:
                        pe.wait_ge(bc_act, 2 * n - 2)
                    rws = slice(n % 2 * HD, (n % 2 + 1) * HD)
                    q, k = qk[rws, n // 2, :], qk[rws, 4 + n // 2, :]
                    mm(ps[:, 4 + n % 2, 0:P], q[:, 0:P], k[:, 0:P], start=True, stop=True)
                    mm(ps[:, 4 + n % 2, P:NZ], q[:, P:SEQ], k, start=True, stop=True).then_inc(z_ps, 1)
                elif kind == "t":
                    if n >= 1:
                        pe.wait_ge(wT_act, n)
                    pe.wait_ge(w_dve, 2 * n + 2)
                    for c in range(3):
                        last = nc.tensor.transpose(ps[:, 6, c * P:(c + 1) * P], beta[n % 2][:, c * P:(c + 1) * P], ident[:])
                    last.then_inc(wT_ps, 1)
                elif kind == "av":
                    if n == 0:
                        freed(pe, 8)
                        freed(pe, 9)
                    if n >= 2 and n % 2 == 0:
                        pe.wait_ge(yT_dve, n // 2)
                    pe.wait_ge(wT_act, n + 1)
                    c = n // 2 % 2 * SEQ
                    o = ps[n % 2 * HD:(n % 2 + 1) * HD, 7, c:c + SEQ]
                    mm(o, v_sb[:, 0, n * HD:(n + 1) * HD], wT[n % 2][:, 0:SEQ], start=True, stop=False)
                    mm(o[:, P:SEQ], v_sb[:, 1, n * HD:(n + 1) * HD], wT[n % 2][:, SEQ:NZ], start=False,
                       stop=True).then_inc(o_ps, 1)
            for n in range(22, 28):
                unit(n)

            def ca_out(h):
                if h == 0:
                    freed(pe, 18)
                    freed(pe, 19)
                freed(pe, 28 + h)
                n = 32 + h // 2
                if h % 2 == 0:
                    freed(pe, n - 4)
                o = ps[h % 2 * HD:(h % 2 + 1) * HD, n % 4, 0:SEQ]
                for m in range(2):
                    last = mm(o, v_ca[:, m, h * HD:(h + 1) * HD], ca_pT[h % 2][:, m, :], start=m == 0, stop=m == 1)
                last.then_inc(unit_ps if h % 2 else oca_ps, 1)

            for n in range(28, 32):
                unit(n)
            for h in range(CA_HEADS):
                ca_out(h)
            k = 0
            for g, blocks in enumerate((4, 2, 2)):
                n = 34 + g
                if g == 2:
                    pe.wait_ge(oca_dve, 2)
                for i in range(blocks):
                    pe.wait_ge(ysq_act, k + 1)
                    last = mm(ps[:, n % 4, 0:SEQ], ones[:], y_sq[:, k, :], start=i == 0, stop=i == blocks - 1)
                    k += 1
                last.then_inc(unit_ps, 1)
            pe.wait_ge(wo_loaded, 16)
            for t in range(NT):
                for half in range(2):
                    for k in range(KD):
                        if t == 0 and half == 0:
                            pe.wait_ge(yn_dve, k + 1)
                        last = mm(ps[:, ACC[2 * t + half], :], yT[:, k, t * P:(t + 1) * P],
                                  wo[:, k, half * 512:(half + 1) * 512], start=k == 0, stop=k == KD - 1)
                    last.then_inc(wo_ps, 1)
            pe.wait_ge(xn_dve, 9)
            transposes(lambda t, k: xn2[:, t, k, :], 0, x2T_ps)
            pe.wait_ge(x2T_act, KD // 2)
            pe.wait_ge(x2T_dve, KD // 2)
            pe.wait_ge(rt_loaded, 16)
            for t in range(NT):
                for k in range(KD):
                    last = mm(ps[:, 4, t * NE:(t + 1) * NE], xn2T[:, k, t * P:(t + 1) * P], w_rt[:, k, :],
                              start=k == 0, stop=k == KD - 1)
            last.then_inc(rt_ps, 1)
            pe.wait_ge(gu_loaded[0], 32)
            for t in range(NT):
                for k in range(KD):
                    last = mm(ps[:, t, :], xn2T[:, k, t * P:(t + 1) * P], ring_gu[0][:, :, k, :],
                              start=k == 0, stop=k == KD - 1)
                last.then_inc(s_gu_ps, 1)
            pe.wait_ge(route_dve, 1)
            pb = ps[:, 5, :]
            mm(pb[:, 0:NE], upper[:], picked[:, 0, :], start=True, stop=True)
            mm(pb[:, NE:2 * NE], upper[:], picked[:, 1, :], start=True, stop=False)
            mm(pb[:, NE:2 * NE], ones_b[:], picked[:, 0, :], start=False, stop=True)
            mm(pb[:, 2 * NE:3 * NE], ones_b[:], picked[:, 0, :], start=True, stop=False)
            mm(pb[:, 2 * NE:3 * NE], ones_b[:], picked[:, 1, :], start=False, stop=True).then_inc(count_ps, 1)
            pe.wait_ge(s_h_dve, 2)
            for t in range(NT):
                for kk in range(KH):
                    c = kk * SEQ + t * P
                    last = nc.tensor.transpose(ps[:, 2, c:c + P], s_h[:, t, kk, :], ident[:])
            last.then_inc(s_hT_ps, 1)
            pe.wait_ge(d_loaded[0], 16)
            pe.wait_ge(s_hT_dve, 1)
            pe.wait_ge(cum_dve, 1)
            for t in range(NT):
                for half in range(2):
                    for kk in range(KH):
                        last = mm(ps[:, ACC[2 * t + half], :], s_hT[:, kk, t * P:(t + 1) * P],
                                  ring_d[0][:, kk, half * 512:(half + 1) * 512], start=kk == 0, stop=False,
                                  skip_group_check=True)
            last.then_inc(s_down_ps, 1)

            def gather_chunk(k, buf, bank):
                for i, (part, t) in enumerate(((xhi, 0), (xhi, 1), (xlo, 0), (xlo, 1))):
                    last = mm(ps[:, bank, :], part[:, t, k, :], pick[buf][:, t, :], start=i == 0, stop=i == 3)
                last.then_inc(gather_ps, 1)

            pe.wait_ge(split_dve, 2)
            pe.wait_ge(pick_dve, 2)
            for k in range(KD):
                if k >= 2:
                    pe.wait_ge(xg_act if k % 2 == 0 else xg_dve, k // 2)
                gather_chunk(k, 0, Y[k % 2])

            def gate_up(rows_a, rows_b, na, nb, sem):
                for k in range(KD):
                    for side, (lhs, n) in enumerate(((rows_a, na), (rows_b, nb))):
                        last = mm(ps[side * SLOTS:(side + 1) * SLOTS, U, :], lhs(k), ring_gu[n][:, :, k, :],
                                  start=k == 0, stop=k == KD - 1)
                last.then_inc(sem, 2)

            def hidden_T(h, sem):
                for kk in range(KH):
                    last = nc.tensor.transpose(ps[:, U, kk * P:(kk + 1) * P], h[:, kk, :], ident[:])
                last.then_inc(sem, 1)

            def slots_T(picks, gate_cols, sem):
                for t in range(NT):
                    nc.tensor.transpose(ps[:, T, t * P:(t + 1) * P], picks(t).bitcast(F32), ident[:])
                for t in range(NT):
                    last = mm(ps[:, T, SEQ:SEQ + 4], picks(t), gate_cols(t), start=t == 0, stop=t == NT - 1)
                last.then_inc(sem, 1)

            def down(na, nb, sem):
                for half in range(2):
                    for kk in range(KH):
                        for side, n in enumerate((na, nb)):
                            last = mm(ps[side * SLOTS:(side + 1) * SLOTS, Y[half], :],
                                      e_hT[:, kk, side * SLOTS:(side + 1) * SLOTS],
                                      ring_d[n][:, kk, half * 512:(half + 1) * 512], start=kk == 0, stop=kk == KH - 1)
                    last.then_inc(sem, 1)

            def scatter(to_token, hi, lo, sem, final=False):
                for t in range(NT):
                    for half in range(2):
                        for i, y in enumerate((hi, lo)):
                            last = mm(ps[:, ACC[2 * t + half], :], to_token[:, t * P:(t + 1) * P],
                                      y[:, half * 512:(half + 1) * 512], start=False, stop=final and i == 1,
                                      skip_group_check=True)
                        if final:
                            last.then_inc(sem, 1)
                if not final:
                    last.then_inc(sem, 1)

            def overflow_item(p, j, n, d_fill):
                pe.wait_ge(ov_pick_dve, 2 * j + 2)
                for k in range(KD):
                    for t in range(NT):
                        last = mm(ps[:, Y[k // 4], k % 4 * P:(k % 4 + 1) * P], xn2[:, t, k, :],
                                  ov_pick[:, t, :].bitcast(F32), start=t == 0, stop=t == NT - 1)
                    if k % 4 == 3:
                        last.then_inc(ov_gather_ps, 1)
                slots_T(lambda t: ov_pick[:, t, :], lambda t: gates2[:, t, bass.ds(p, 1), :], ov_pt_ps)
                pe.wait_ge(h_dve, p + 1)
                pe.wait_ge(ov_xg_act, j + 1)
                pe.wait_ge(ov_xg_dve, j + 1)
                gate_up(lambda k: ov_xg[:, k, 0:SLOTS], lambda k: ov_xg[:, k, SLOTS:P], n, n, ov_gu_ps)
                pe.wait_ge(ov_h_dve, j + 1)
                hidden_T(ov_h, ov_hT_ps)
                pe.wait_ge(d_loaded[n], d_fill)
                pe.wait_ge(ov_hTs_dve, j + 1)
                down(n, n, ov_y_ps)
                pe.wait_ge(ov_yhi_act, 2 * j + 2)
                pe.wait_ge(ov_ylo_dve, 2 * j + 2)
                pe.wait_ge(ov_S_act, j + 1)
                scatter(ov_S, yhi, ylo, ov_scatter_ps)

            def octets(it, gather_last):
                for j in range(8):
                    p, o, q, ob = 8 * it + j, 2 * it + j // 4, j % 4, j // 4
                    na, nb = slot(2 * j), slot(2 * j + 1)
                    more = ob == 0 or gather_last
                    if q == 0:
                        pe.wait_ge(xg_act, 4 * (o + 1))
                        pe.wait_ge(xg_dve, 4 * (o + 1))
                    pe.wait_ge(gu_loaded[na], 32 * fills(it, 2 * j))
                    pe.wait_ge(gu_loaded[nb], 32 * fills(it, 2 * j + 1))
                    pe.wait_ge(hTs_dve, p + 1)
                    c = 2 * q * SLOTS
                    gate_up(lambda k: xg[ob][:, k, c:c + SLOTS], lambda k: xg[ob][:, k, c + SLOTS:c + 2 * SLOTS],
                            na, nb, gu_ps)
                    pe.wait_ge(yhi_act, 2 * p + 1)
                    pe.wait_ge(ylo_dve, 2 * p + 1)
                    pe.wait_ge(S_act, p + 1)
                    if j == 0:
                        pe.wait_ge(zeroed, 2)
                    scatter(S[(j + 1) % 2], yhi, ylo, scatter_ps)
                    c0 = nc.tensor.value_load(cum[0:1, bass.ds(2 * p, 1)], min_val=0, max_val=NE)
                    c2 = nc.tensor.value_load(cum[0:1, bass.ds(2 * p + 2, 1)], min_val=0, max_val=NE)
                    with nc.tensor.If(c2 > c0):
                        c1 = nc.tensor.value_load(cum[0:1, bass.ds(2 * p + 1, 1)], min_val=0, max_val=NE)
                        for side, (lo, hi) in enumerate(((c0, c1), (c1, c2))):
                            with nc.tensor.If(hi > lo):
                                with nc.tensor.Fori(lo, hi) as item:
                                    overflow_item(p, item, (na, nb)[side], 16 * fills(it, 2 * j + side))
                    if more:
                        if q == 0:
                            pe.wait_ge(pick_dve, 2 * (o + 2))
                        gather_chunk(2 * q, 1 - ob, Y[0])
                        gather_chunk(2 * q + 1, 1 - ob, Y[1])
                    pe.wait_ge(h_dve, p + 1)
                    hidden_T(e_h, hT_ps)
                    slots_T(lambda t: pick[ob][:, t, c:c + 2 * SLOTS], lambda t: gates2[:, t, bass.ds(p, 1), :], pt_ps)
                    pe.wait_ge(d_loaded[na], 16 * fills(it, 2 * j))
                    pe.wait_ge(d_loaded[nb], 16 * fills(it, 2 * j + 1))
                    pe.wait_ge(hTs_dve, p + 2)
                    if more:
                        pe.wait_ge(xg_act, 4 * (o + 1) + q + 1)
                        pe.wait_ge(xg_dve, 4 * (o + 1) + q + 1)
                    down(na, nb, y_ps)

            pe.sem_inc(pt_ps, 1)
            pe.sem_inc(ov_scatter_ps, 1)
            pe.sem_inc(ov_gu_ps, 1)
            with pe.Fori(0, PAIRS // 8 - 1) as it:
                octets(it, True)
            octets(PAIRS // 8 - 1, False)
            pe.wait_ge(yhi_act, 2 * PAIRS + 1)
            pe.wait_ge(ylo_dve, 2 * PAIRS + 1)
            pe.wait_ge(S_act, PAIRS + 1)
            scatter(S[(PAIRS + 1) % 2], yhi, ylo, last_ps, final=True)


_INS = ['x', 'mem', 'norm_mix_g', 'norm_mem_g', 'w_in', 'conv_w', 'conv_b', 'w_rgate', 'b_rgate', 'w_igate', 'b_igate',
        'lru_lambda', 'w_mem_kv', 'q_norm_g', 'k_norm_g', 'g_out_sb', 'g_out_rg', 'g_out_ca', 'w_out', 'norm_ffn_g',
        'w_router', 'router_bias', 'w_gate_e', 'w_up_e', 'w_down_e', 'w_gate_sh', 'w_up_sh', 'w_down_sh']


def kernel(**inputs):
    import numpy as _np
    import concourse.bacc as _bacc
    from concourse import mybir as _mybir
    from concourse.bass_utils import run_bass_kernel_spmd as _run

    nc = _bacc.Bacc("TRN2", target_bir_lowering=False, num_devices=1)
    arrays, args = {}, []
    for name in _INS:
        a = _np.ascontiguousarray(inputs[name])
        arrays[f"in_{name}"] = a
        args.append(nc.dram_tensor(f"in_{name}", a.shape, _mybir.dt.from_np(a.dtype), kind="ExternalInput").ap())
    o = nc.dram_tensor("out_0", inputs["x"].shape, _mybir.dt.float32, kind="ExternalOutput").ap()
    hybrid_decoder_layer(nc, *args, o)
    r = _run(nc, [arrays], core_ids=[0])
    return r.results[0]["out_0"]
```

```python
import concourse.bass as bass
from concourse import mybir
from contextlib import ExitStack


def hybrid_decoder_layer(
    nc: bass.Bass,
    x, mem, norm_mix_g, norm_mem_g, w_in, conv_w, conv_b, w_rgate, b_rgate, w_igate, b_igate, lru_lambda,
    w_mem_kv, q_norm_g, k_norm_g, g_out_sb, g_out_rg, g_out_ca, w_out, norm_ffn_g, w_router, router_bias,
    w_gate_e, w_up_e, w_down_e, w_gate_sh, w_up_sh, w_down_sh, out,
):
    F32, F32R, BF16, I32 = mybir.dt.float32, mybir.dt.float32r, mybir.dt.bfloat16, mybir.dt.int32
    ALU = mybir.AluOpType
    ACT = mybir.ActivationFunctionType
    AX = mybir.AxisListType

    P = 128
    _, SEQ, D = x.shape
    NT = SEQ // P
    KD = D // P
    HD = 64
    SB, RG, CA = 512, 256, 256
    SB_HEADS, CA_HEADS = SB // HD, CA // HD
    NE, GROUPS, DE = w_router.shape[2], 8, w_gate_e.shape[3]
    EG = NE // GROUPS
    KH = DE // P
    SLOTS = 64
    PAIRS = NE // 2
    EPS = 1e-6
    HUGE = 3.0e38
    SCALE = HD ** -0.5
    RING = 4

    KB = 1024
    base = (nc.sbuf_base + 31) // 32 * 32
    o_ring = base
    o_A = o_ring + 96 * KB
    o_R = o_A + 32 * KB
    o_V = o_R + 24 * KB
    o_O = o_V + 16 * KB

    def at(name, offset, shape, dt=F32):
        return nc.alloc_sbuf_tensor_at(name, shape, dt, offset=offset)

    class Space:
        def __init__(self, offset):
            self.offset = offset

        def __call__(self, name, shape, dt=F32):
            t = at(name, self.offset, shape, dt)
            n = 1
            for s in shape[1:]:
                n *= s
            self.offset += (n * (2 if dt == BF16 else 4) + 31) // 32 * 32
            return t

    ring_gu = [at(f"ring_gu{s}", o_ring + 24 * KB * s, [P, 2, KD, DE]) for s in range(RING)]
    ring_d = [at(f"ring_d{s}", o_ring + 24 * KB * s + 16 * KB, [P, KH, D]) for s in range(RING)]
    xn = at("xn", o_ring, [P, NT, D])
    memn = at("memn", o_ring + 8 * KB, [P, NT, D])
    x_in = at("x_in", o_ring + 24 * KB, [P, NT, D])
    hT = at("hT", o_ring + 48 * KB, [P, KD, SEQ])
    memT = at("memT", o_ring + 56 * KB, [P, KD, SEQ])
    w_kv = at("w_kv", o_ring + 72 * KB, [P, KD, 2 * CA])
    ca_raw = at("ca_raw", o_ring + 64 * KB, [P, 2, NT, CA])
    ca_sq = at("ca_sq", o_ring + 68 * KB, [P, 2, NT, CA])
    mem_in = at("mem_in", o_ring + 88 * KB, [P, NT, D])
    wA = [at(f"wA{g}", o_A + 8 * KB * g, [P, KD, 256]) for g in range(4)]
    wo = at("wo", o_A, [P, KD, D])
    xg = [at(f"xg{b}", o_A + 16 * KB * b, [P, KD, 512]) for b in range(2)]
    s_sg = at("s_sg", o_A + 24 * KB, [P, NT, DE])
    s_h = at("s_h", o_A + 26 * KB, [P, NT, KH, P])
    s_hT = at("s_hT", o_A + 28 * KB, [P, KH, SEQ])
    wR = [at(f"wR{g}", o_R + 8 * KB * g, [P, KD, 256]) for g in range(3)]
    r = Space(o_R)
    rg_r = r("rg_r", [P, 2, SEQ])
    rg_i = r("rg_i", [P, 2, SEQ])
    rg_a = r("rg_a", [P, 2, SEQ])
    rg_t = r("rg_t", [P, 2, SEQ])
    rg_u = r("rg_u", [P, 2, SEQ])
    y_sq = at("y_sq", o_R + 16 * KB, [P, KD, SEQ])
    xhi = at("xhi", o_R, [P, NT, KD, P], F32R)
    xlo = at("xlo", o_R + 8 * KB, [P, NT, KD, P], F32R)
    xn2T = at("xn2T", o_R + 16 * KB, [P, KD, SEQ])
    yhi = at("yhi", o_R + 16 * KB, [P, D], F32R)
    ylo = at("ylo", o_R + 20 * KB, [P, D], F32R)
    wV = at("wV", o_V, [P, KD, SB])
    r = Space(o_ring)
    NZ = 3 * P
    beta = [r(f"beta{b}", [P, NZ]) for b in range(2)]
    keep = [r(f"keep{b}", [P, NZ]) for b in range(2)]
    rest = [r(f"rest{b}", [P, NZ + 2]) for b in range(2)]
    wT = [r(f"wT{b}", [P, NZ]) for b in range(2)]
    ca_p = [at(f"ca_p{b}", o_V + 2 * KB * b, [P, NT, SEQ]) for b in range(2)]
    ca_pT = [at(f"ca_pT{b}", o_V + 4 * KB + 2 * KB * b, [P, 2, SEQ]) for b in range(2)]
    pick = [at(f"pick{b}", o_V + 4 * KB * b, [P, NT, 8 * SLOTS], F32R) for b in range(2)]
    xc = at("xc", o_V + 8 * KB, [P, 2, SEQ])
    rg_g = at("rg_g", o_V + 10 * KB, [P, 2, SEQ])
    xn2 = at("xn2", o_V + 8 * KB, [P, NT, KD, P])
    r = Space(o_O)
    qk = r("qk", [P, 8, SEQ])
    v_sb = r("v_sb", [P, NT, SB])
    xpad = r("xpad", [P, 2, SEQ + 3])
    gate = r("gate", [P, 2, SEQ])
    qkca = r("qkca", [P, 4, SEQ])
    v_ca = r("v_ca", [P, NT, CA])
    yT = r("yT", [P, KD, SEQ])
    x1 = at("x1", o_O, [P, NT, D])
    ov_xg = at("ov_xg", o_O + 8 * KB, [P, KD, P])
    g_ffn = at("g_ffn", o_O + 12 * KB + 2080 + 2 * KB, [P, D])
    rt = Space(o_O + 8 * KB)
    w_rt = rt("w_rt", [P, KD, NE])
    rbias = rt("rbias", [P, NE])
    top8 = rt("top8", [P, NT, GROUPS, 8])
    gtop = rt("gtop", [P, NT, 8])
    grep = rt("grep", [P, NT, 16])
    rt = Space(o_O + 12 * KB)
    score = rt("score", [P, NT, NE])
    choice = rt("choice", [P, NT, NE])
    rt = Space(o_O + 12 * KB + 2080 + 6 * KB)
    cand = rt("cand", [P, NT, NE])
    repl = rt("repl", [P, NT, NE])
    gatew = rt("gatew", [P, NT, NE])
    rt = Space(o_O + 12 * KB + 2080 + 8 * KB)
    e_h = rt("e_h", [P, KH, P])
    e_sg = rt("e_sg", [P, DE])
    e_hT = rt("e_hT", [P, KH, P])
    S = [rt(f"S{b}", [P, SEQ], F32R) for b in range(2)]
    ov_pick = rt("ov_pick", [P, NT, P], F32R)
    ov_S = rt("ov_S", [P, SEQ], F32R)
    ov_h = rt("ov_h", [P, KH, P])
    ident = r("ident", [P, P])
    ones = r("ones", [P, P])
    upper = r("upper", [P, P], BF16)
    ones_b = r("ones_b", [P, P], BF16)
    vecs = r("vecs", [42, P])
    vec = r("vec", [P, 42])
    zeros = r("zeros", [P, SEQ])
    iota1 = r("iota1", [P, SEQ + SLOTS])
    wg_r = r("wg_r", [P, 2, HD])
    wg_i = r("wg_i", [P, 2, HD])
    picked = r("picked", [P, NT, NE], BF16)
    posm = r("posm", [P, NT, NE])
    gates2 = r("gates2", [P, NT, PAIRS, 4], F32R)
    stat = r("stat", [P, 16])
    gslot = r("gslot", [P, 2])
    ov_gslot = r("ov_gslot", [P, 1])
    lam = r("lam", [P, 8, 2])
    mx = r("mx", [P, 2, 4])
    ca_rs = r("ca_rs", [P, 2, NT, CA_HEADS])
    g_rs = r("g_rs", [P, 3, NT])
    grp = r("grp", [P, NT, 16])
    cnt_row = r("cnt_row", [1, 4, NE + 1])
    cum = r("cum", [1, NE + 1], I32)
    assert r.offset <= nc.sbuf_usable_end, r.offset - nc.sbuf_usable_end

    MIX, MEM, GOUT, CW, CB, BR, BI, LAM, QN, KN = 0, 8, 16, 24, 32, 34, 36, 38, 40, 41

    with ExitStack() as ctx:
        ps = ctx.enter_context(nc.psum_tensor("ps", [P, 8, 512], F32))
        U, T, Y, ACC = 0, 1, (2, 3), (4, 5, 6, 7)
        (
            x_loaded, mem_loaded, vec_loaded, wg_loaded, wV_loaded, kv_loaded, wo_loaded, x1_loaded,
            gffn_loaded, rt_loaded, rb_loaded, consts, zeroed, ssq_act, std_act, xn_dve, vec_ps, vec_dve,
            xT_ps, xT_act, xT_dve, memT_ps, memT_act, memT_dve, unit_ps, unit_act, unit_dve, conv_dve, z_ps,
            bc_act, mask_pool, w_dve, wT_ps, wT_act, o_ps, yT_dve, lam_act, lam_dve, gelu_dve, gelu_act,
            rg_act, camax_dve, cap_dve, oca_ps, oca_dve, yrg_dve, ysq_act, wo_ps, x1_dve, x2T_ps, x2T_act,
            x2T_dve, split_act, split_dve, rt_ps, score_act, route_dve, count_ps, cum_dve, s_gu_ps,
            s_sg_act, s_h_dve, s_hT_ps, s_hT_dve, s_down_ps, pick_dve, gather_ps, xg_act, xg_dve, gu_ps,
            sg_act, h_dve, hT_ps, hTs_dve, pt_ps, S_act, gslot_dve, y_ps, yhi_act, ylo_dve, scatter_ps,
            ov_pick_dve, ov_gather_ps, ov_xg_act, ov_xg_dve, ov_pt_ps, ov_S_act, ov_gslot_dve, ov_gu_ps,
            ov_sg_act, ov_h_dve, ov_hT_ps, ov_hTs_dve, ov_y_ps, ov_yhi_act, ov_ylo_dve, ov_scatter_ps,
            last_ps, out_dve, stored, act_chain, dve_chain, pool_chain, rg_dve, ca_ss_dve, ca_rt_act,
            ca_rs_dve, yg_act, ysum_pool, g_rt_act,
        ) = [ctx.enter_context(nc.semaphore(name)) for name in """
            x_loaded mem_loaded vec_loaded wg_loaded wV_loaded kv_loaded wo_loaded x1_loaded gffn_loaded
            rt_loaded rb_loaded consts zeroed ssq_act std_act xn_dve vec_ps vec_dve xT_ps xT_act xT_dve
            memT_ps memT_act memT_dve unit_ps unit_act unit_dve conv_dve z_ps bc_act mask_pool w_dve
            wT_ps wT_act o_ps yT_dve lam_act lam_dve gelu_dve gelu_act rg_act camax_dve cap_dve oca_ps
            oca_dve yrg_dve ysq_act wo_ps x1_dve x2T_ps x2T_act x2T_dve split_act split_dve rt_ps
            score_act route_dve count_ps cum_dve s_gu_ps s_sg_act s_h_dve s_hT_ps s_hT_dve s_down_ps
            pick_dve gather_ps xg_act xg_dve gu_ps sg_act h_dve hT_ps hTs_dve pt_ps S_act gslot_dve y_ps
            yhi_act ylo_dve scatter_ps ov_pick_dve ov_gather_ps ov_xg_act ov_xg_dve ov_pt_ps ov_S_act
            ov_gslot_dve ov_gu_ps ov_sg_act ov_h_dve ov_hT_ps ov_hTs_dve ov_y_ps ov_yhi_act ov_ylo_dve
            ov_scatter_ps last_ps out_dve stored act_chain dve_chain pool_chain rg_dve ca_ss_dve
            ca_rt_act ca_rs_dve yg_act ysum_pool g_rt_act
        """.split()]
        wA_loaded = [ctx.enter_context(nc.semaphore(f"wA_loaded{g}")) for g in range(4)]
        wR_loaded = [ctx.enter_context(nc.semaphore(f"wR_loaded{g}")) for g in range(3)]
        gu_loaded = [ctx.enter_context(nc.semaphore(f"gu_loaded{i}")) for i in range(RING)]
        d_loaded = [ctx.enter_context(nc.semaphore(f"d_loaded{i}")) for i in range(RING)]
        block = ctx.enter_context(nc.Block())

        owner = ["act" if n % 2 == 0 else "dve" for n in range(18)]
        owner += ["dve", "dve", "act", "act"] + ["act"] * 4 + ["dve"] * 5 + [None, None] + ["dve"] * 2
        walk = [("unit", n) for n in range(8)] + [("memT", 0)]
        for i in range(1, 15):
            walk.append(("unit", 7 + i))
            if i <= 8:
                walk.append(("z", i - 1))
            if 3 <= i <= 10:
                walk.append(("t", i - 3))
            if 4 <= i <= 11:
                walk.append(("av", i - 4))
            walk += {2: [("log1p", 0)], 7: [("ca_square", 0)], 8: [("ca_norm", 0)], 9: [("conv", 0)],
                     11: [("gelu", 0)]}.get(i, [])

        rg_cols = {14: (0, 0), 15: (0, P), 16: (1, 0), 17: (1, P)}

        SUMS = (26, 33, 34)
        projections = [(g, t, half) for gs, ts in (((0,), (0, 1)), ((1, 2), (0,)), ((1, 2), (1,)))
                       for g in gs for t in ts for half in range(2)]

        ACT_K, DVE_K = [0, 1, 4, 5], [2, 3, 6, 7]

        def freed(eng, n):
            count = owner[:n + 1].count(owner[n])
            eng.wait_ge(unit_act if owner[n] == "act" else unit_dve, count)

        def slot(j):
            return (j + 1) % RING

        def fills(it, j):
            return 4 * it + (j + 1) // RING + 1

        def load_expert(sp, n_slot, gate_src, up_src, down_src):
            sp.dma_start(ring_gu[n_slot][:, 0], gate_src.rearrange("(p k) n -> p k n", k=KD)).then_inc(gu_loaded[n_slot], 16)
            sp.dma_start(ring_gu[n_slot][:, 1], up_src.rearrange("(p k) n -> p k n", k=KD)).then_inc(gu_loaded[n_slot], 16)
            sp.dma_start(ring_d[n_slot][:], down_src.rearrange("(p k) n -> p k n", k=KH)).then_inc(d_loaded[n_slot], 16)

        @block.sync
        def _(sp):
            def cols(c, n):
                return w_in[0][:, c:c + n].rearrange("(k p) n -> p k n", p=P)

            sp.dma_start(x_in[:], x[0].rearrange("(t p) d -> p t d", p=P)).then_inc(x_loaded, 16)
            def rows(v, n):
                return v.rearrange("(a p) -> a p", a=n)

            at_row = 0
            for v, n in ((norm_mix_g[0], 8), (norm_mem_g[0], 8), (g_out_sb[0], 4), (g_out_rg[0], 2), (g_out_ca[0], 2),
                         (conv_w[0].rearrange("t c -> (t c)"), 8), (conv_b[0], 2), (b_rgate[0], 2), (b_igate[0], 2),
                         (lru_lambda[0], 2)):
                sp.dma_start(vecs[at_row:at_row + n, :], rows(v, n)).then_inc(vec_loaded, 16)
                at_row += n
            for i, v in enumerate((q_norm_g[0], k_norm_g[0])):
                for half in range(2):
                    sp.dma_start(vecs[QN + i:QN + i + 1, half * HD:(half + 1) * HD], rows(v, 1)).then_inc(vec_loaded, 16)
            for g in range(4):
                sp.dma_start(wA[g][:], cols(256 * g, 256)).then_inc(wA_loaded[g], 16)
            sp.dma_start(mem_in[:], mem[0].rearrange("(t p) d -> p t d", p=P)).then_inc(mem_loaded, 16)
            sp.dma_start(wV[:], cols(2 * SB, SB)).then_inc(wV_loaded, 16)
            for g in (2, 0, 1):
                if g == 0:
                    sp.dma_start(w_kv[:], w_mem_kv[0].rearrange("(k p) n -> p k n", p=P)).then_inc(kv_loaded, 16)
                sp.dma_start(wR[g][:], cols(3 * SB + 256 * g, 256)).then_inc(wR_loaded[g], 16)
            sp.wait_ge(unit_ps, 8)
            sp.dma_start(wo[:], w_out[0].rearrange("(k p) n -> p k n", p=P)).then_inc(wo_loaded, 16)
            sp.wait_ge(xT_ps, 4)
            load_expert(sp, 1, w_gate_e[0, 0], w_up_e[0, 0], w_down_e[0, 0])
            sp.wait_ge(o_ps, SB_HEADS)
            load_expert(sp, 0, w_gate_sh[0], w_up_sh[0], w_down_sh[0])
            sp.wait_ge(unit_ps, 20)
            for e in (1, 2):
                load_expert(sp, slot(e), w_gate_e[0, e], w_up_e[0, e], w_down_e[0, e])
            sp.wait_ge(s_down_ps, 1)
            load_expert(sp, slot(3), w_gate_e[0, 3], w_up_e[0, 3], w_down_e[0, 3])
            sp.wait_ge(cum_dve, 1)
            with sp.Fori(0, (NE - 4) // 4) as i:
                for half in range(2):
                    p = 2 * i + half
                    done = nc.sync.value_load(cum[0:1, bass.ds(2 * p + 2, 1)], min_val=0, max_val=NE)
                    sp.wait_ge(ov_gu_ps, 2 * done + 1)
                    sp.wait_ge(gu_ps, 2 * p + 2)
                    for side in range(2):
                        e = 4 * i + 2 * half + side + 4
                        n = slot(2 * half + side)
                        sp.dma_start(ring_gu[n][:, 0], w_gate_e[0, bass.ds(e, 1)].rearrange("o (p k) n -> p (o k) n", k=KD)).then_inc(gu_loaded[n], 16)
                        sp.dma_start(ring_gu[n][:, 1], w_up_e[0, bass.ds(e, 1)].rearrange("o (p k) n -> p (o k) n", k=KD)).then_inc(gu_loaded[n], 16)
                    sp.wait_ge(y_ps, 2 * p + 2)
                    for side in range(2):
                        e = 4 * i + 2 * half + side + 4
                        n = slot(2 * half + side)
                        sp.dma_start(ring_d[n][:], w_down_e[0, bass.ds(e, 1)].rearrange("o (p k) n -> p (o k) n", k=KH)).then_inc(d_loaded[n], 16)
            for c in range(NT):
                sp.wait_ge(out_dve, 2 * c + 2)
                sp.dma_start(out[0, c * P:(c + 1) * P, :], x1[:, c, :]).then_inc(stored, 16)
            sp.wait_ge(stored, 16 * NT)

        @block.gpsimd
        def _(pool):
            chain = [0]

            def link(ins):
                chain[0] += 1
                ins.then_inc(pool_chain, 1)
                pool.wait_ge(pool_chain, chain[0])

            def diagonal(t, value_off, cmp, lo, n):
                return pool.affine_select(out=t, in_=t, compare_op=cmp, fill=value_off, base=lo, pattern=[[-1, n]],
                                          channel_multiplier=1)

            link(pool.memset(ident[:], 0.0))
            diagonal(ident[:], 1.0, ALU.not_equal, 0, P).then_inc(consts, 1)
            link(pool.memset(ones[:], 1.0))
            link(pool.memset(ones_b[:], 1.0))
            link(pool.memset(zeros[:], 0.0))
            link(pool.memset(xpad[:, :, 0:3], 0.0))
            link(pool.memset(cnt_row[:], 0.0))
            link(pool.memset(upper[:], 1.0))
            link(pool.affine_select(out=upper[:], in_=upper[:], compare_op=ALU.is_gt, fill=0.0, base=0,
                                    pattern=[[1, P]], channel_multiplier=-1))
            link(pool.iota(iota1[:], pattern=[[1, SEQ + SLOTS]], base=1, channel_multiplier=0,
                           allow_small_or_imprecise_dtypes=True))
            pool.memset(grp[:], HUGE).then_inc(consts, 1)
            pool.wait_ge(memT_ps, 4)
            for b in range(2):
                link(pool.memset(rest[b][:, P:P + 1], 1.0))
                last = pool.memset(rest[b][:, NZ + 1:NZ + 2], 1.0)
                link(last)
            pool.memset(stat[:, 15:16], 0.0).then_inc(zeroed, 1)
            for kind, h in walk:
                if kind != "z":
                    continue
                pool.wait_ge(bc_act, 2 * h + 2)
                for t, off in ((keep[h % 2], 1.0), (beta[h % 2], 0.0)):
                    for c in (0, 2):
                        last = pool.affine_select(out=t[:, c * P:(c + 1) * P], in_=t[:, c * P:(c + 1) * P],
                                                  compare_op=ALU.is_gt, fill=off, base=0, pattern=[[-1, P]],
                                                  channel_multiplier=1)
                        last.then_inc(mask_pool, 1)
            pool.wait_ge(z_ps, SB_HEADS)
            pool.dma_start(x1[:], x[0].rearrange("(t p) d -> p t d", p=P)).then_inc(x1_loaded, 16)
            pool.wait_ge(o_ps, SB_HEADS)
            pool.dma_start(w_rt[:], w_router[0].rearrange("(p k) e -> p k e", k=KD)).then_inc(rt_loaded, 16)
            pool.dma_start(rbias[:], router_bias[0].partition_broadcast(P)).then_inc(rb_loaded, 16)
            pool.wait_ge(ysq_act, 4)
            link(pool.tensor_tensor(y_sq[:, 0:2, :], y_sq[:, 0:2, :], y_sq[:, 2:4, :], ALU.add))
            pool.tensor_tensor(y_sq[:, 0, :], y_sq[:, 0, :], y_sq[:, 1, :], ALU.add).then_inc(ysum_pool, 1)
            pool.wait_ge(unit_ps, 26)
            pool.dma_start(g_ffn[:], norm_ffn_g[0].partition_broadcast(P)).then_inc(gffn_loaded, 16)
            for k in (4, 6):
                pool.wait_ge(ysq_act, k + 2)
                pool.tensor_tensor(y_sq[:, k, :], y_sq[:, k, :], y_sq[:, k + 1, :], ALU.add).then_inc(ysum_pool, 1)
            pool.wait_ge(s_gu_ps, 2)
            link(pool.memset(yhi[:].bitcast(F32), 0.0))
            link(pool.memset(ylo[:].bitcast(F32), 0.0))
            pool.memset(S[1][:].bitcast(F32), 0.0).then_inc(zeroed, 1)

        @block.scalar
        def _(act):
            chain = [0]

            def link(ins):
                chain[0] += 1
                ins.then_inc(act_chain, 1)
                act.wait_ge(act_chain, chain[0])

            def squares(src, col, n0):
                for t in range(NT):
                    if n0 + t:
                        act.wait_ge(ssq_act, n0 + t)
                    nc.scalar.activation(ps[:, 6:8, :], src[:, t, :].rearrange("p (a b) -> p a b", a=2), ACT.Square,
                                         accum_out=stat[:, col + t:col + t + 1]).then_inc(ssq_act, 1)

            def root(col, n):
                act.wait_ge(xn_dve, n)
                nc.scalar.activation(stat[:, col + 2:col + 4], stat[:, col + 2:col + 4], ACT.Sqrt).then_inc(std_act, 1)

            act.wait_ge(x_loaded, 16)
            squares(x_in, 0, 0)
            root(0, 1)
            for w, t in ((w_rgate, wg_r), (w_igate, wg_i)):
                wv = w[0].rearrange("(j two) c d -> two c j d", two=2)
                for half in range(2):
                    act.dma_start(t[half * HD:(half + 1) * HD], wv[half]).then_inc(wg_loaded, 16)
            act.wait_ge(vec_dve, 1)
            for k in ACT_K:
                act.wait_ge(xT_ps, k // 2 + 1)
                nc.scalar.mul(hT[:, k, :], ps[:, k // 2, k % 2 * SEQ:(k % 2 + 1) * SEQ], vec[:, MIX + k:MIX + k + 1]).then_inc(xT_act, 1)
            act.wait_ge(mem_loaded, 16)
            squares(mem_in, 4, 2)
            root(4, 4)
            act.wait_ge(lam_dve, 1)
            nc.scalar.activation(lam[:, 1, :], lam[:, 0, :], ACT.Exp).then_inc(lam_act, 1)

            def evac(n):
                act.wait_ge(unit_ps, n + 1)
                b = ps[:, n % 4, :]
                if n < 8:
                    nc.scalar.copy(qk[:, n, :], b[:, 0:SEQ]).then_inc(unit_act, 1)
                elif n < 10:
                    nc.scalar.copy(v_sb[:, n - 8, :], b).then_inc(unit_act, 1)
                elif n < 12:
                    nc.scalar.copy(ca_raw[:, 0, n - 10, :], b[:, 0:CA]).then_inc(unit_act, 1)
                elif n < 14:
                    link(nc.scalar.copy(v_ca[:, n - 12, :], b[:, CA:2 * CA]))
                    nc.scalar.copy(ca_raw[:, 1, n - 12, :], b[:, 0:CA]).then_inc(unit_act, 1)
                elif n < 16:
                    nc.scalar.copy(xpad[:, n - 14, 3:3 + SEQ], b[:, 0:SEQ]).then_inc(unit_act, 1)
                elif n < 18:
                    nc.scalar.copy(gate[:, n - 16, :], b[:, 0:SEQ]).then_inc(unit_act, 1)
                else:
                    dst, bias = (rg_r, BR) if n == 20 else (rg_i, BI)
                    link(nc.scalar.activation(dst[:, 0, :], b[:, 0:SEQ], ACT.Sigmoid, bias=vec[:, bias:bias + 1]))
                    nc.scalar.activation(dst[:, 1, :], b[:, SEQ:2 * SEQ], ACT.Sigmoid,
                                         bias=vec[:, bias + 1:bias + 2]).then_inc(unit_act, 1)

            def evac_x2T(t):
                act.wait_ge(x2T_ps, 2 * t + 1)
                nc.scalar.copy(xn2T[:, 0:4, t * P:(t + 1) * P],
                               ps[:, 2 * t, :].rearrange("p (k q) -> p k q", k=4)).then_inc(x2T_act, 1)

            def square_and_gain(k):
                nc.scalar.activation(y_sq[:, k, :], yT[:, k, :], ACT.Square).then_inc(ysq_act, 1)
                nc.scalar.mul(yT[:, k, :], yT[:, k, :], vec[:, GOUT + k:GOUT + k + 1]).then_inc(yg_act, 1)

            for kind, n in walk:
                if kind == "unit" and owner[n] == "act":
                    evac(n)
                elif kind == "memT":
                    for k in ACT_K:
                        act.wait_ge(memT_ps, k // 2 + 1)
                        nc.scalar.mul(memT[:, k, :], ps[:, 4 + k // 2, k % 2 * SEQ:(k % 2 + 1) * SEQ],
                                      vec[:, MEM + k:MEM + k + 1]).then_inc(memT_act, 1)
                elif kind == "z":
                    act.wait_ge(z_ps, n + 1)
                    if n >= 2:
                        act.wait_ge(wT_ps, n - 1)
                    zb = ps[:, 4 + n % 2, 0:NZ]
                    nc.scalar.activation(beta[n % 2][:], zb, ACT.Sigmoid, scale=SCALE).then_inc(bc_act, 1)
                    nc.scalar.activation(keep[n % 2][:], zb, ACT.Sigmoid, scale=-SCALE).then_inc(bc_act, 1)
                elif kind == "t":
                    act.wait_ge(wT_ps, n + 1)
                    nc.scalar.copy(wT[n % 2][:], ps[:, 6, 0:NZ]).then_inc(wT_act, 1)
                elif kind == "ca_norm":
                    act.wait_ge(ca_ss_dve, 1)
                    nc.scalar.activation(ca_rs[:], ca_rs[:], ACT.Sqrt).then_inc(ca_rt_act, 1)
                elif kind == "gelu":
                    act.wait_ge(unit_ps, 18)
                    for k in range(3):
                        act.wait_ge(yT_dve, k + 1)
                        square_and_gain(k)
            act.wait_ge(yT_dve, 4)
            square_and_gain(3)
            act.wait_ge(gelu_dve, 1)
            nc.scalar.activation(rg_g[:], rg_g[:], ACT.Sigmoid, scale=2.0 * 0.7978845608028654).then_inc(gelu_act, 1)
            act.wait_ge(lam_dve, 2)
            act.wait_ge(unit_act, owner[:22].count("act"))
            for c in range(2):
                nc.scalar.activation(rg_t[:, c, :], rg_r[:, c, :], ACT.Tanh, scale=lam[:, 7, c:c + 1]).then_inc(rg_act, 1)
            for c in range(2):
                nc.scalar.activation(rg_a[:, c, :], rg_r[:, c, :], ACT.Exp, scale=lam[:, 7, c:c + 1]).then_inc(rg_act, 1)
            for h in range(CA_HEADS):
                act.wait_ge(camax_dve, h + 1)
                if h >= 2:
                    act.wait_ge(unit_ps, 27 + h - 2 + 1)
                for t in range(NT):
                    ins = nc.scalar.activation(ca_p[h % 2][:, t, :], ps[:, (22 + h) % 4, t * SEQ:(t + 1) * SEQ], ACT.Exp,
                                               bias=mx[:, t, h:h + 1], scale=SCALE,
                                               accum_out=stat[:, 8 + 2 * (h % 2) + t:9 + 2 * (h % 2) + t])
                    if t == 0:
                        link(ins)
                    else:
                        ins.then_inc(unit_act, 1)
            act.wait_ge(rg_dve, 1)
            nc.scalar.activation(rg_t[:], rg_t[:], ACT.Sqrt, scale=-1.0).then_inc(rg_act, 1)
            for g in range(3):
                if g:
                    for i in range(2):
                        act.wait_ge(yrg_dve if g == 1 else oca_dve, i + 1)
                        square_and_gain(2 + 2 * g + i)
                freed(act, SUMS[g])
                nc.scalar.activation(g_rs[:, g, :], g_rs[:, g, :], ACT.Sqrt).then_inc(g_rt_act, 1)
            for t in range(NT):
                act.wait_ge(x1_dve, 8 + 4 * t)
                act.wait_ge(ssq_act, 4 + t)
                nc.scalar.activation(ps[:, 4 + 2 * t:6 + 2 * t, :], x1[:, t, :].rearrange("p (a b) -> p a b", a=2),
                                     ACT.Square, accum_out=stat[:, t:t + 1]).then_inc(ssq_act, 1)
                act.wait_ge(xn_dve, 7 + 2 * t)
                nc.scalar.activation(stat[:, 2 + t:3 + t], stat[:, 2 + t:3 + t], ACT.Sqrt).then_inc(std_act, 1)
                if t == 1:
                    evac_x2T(0)
            evac_x2T(1)
            for t in range(NT):
                nc.scalar.copy(xhi[:, t], xn2[:, t]).then_inc(split_act, 1)
            act.wait_ge(rt_ps, 2)
            for t in range(NT):
                nc.scalar.activation(score[:, t, :], ps[:, 4 + t, 0:NE], ACT.Sigmoid).then_inc(score_act, 1)
            for t in range(NT):
                act.wait_ge(s_gu_ps, t + 1)
                nc.scalar.activation(s_sg[:, t, :], ps[:, t, 0:DE], ACT.Silu).then_inc(s_sg_act, 1)
            for i in range(KD // 2):
                act.wait_ge(gather_ps, 2 * i + 1)
                nc.scalar.copy(xg[0][:, 2 * i, :], ps[:, Y[0], :]).then_inc(xg_act, 1)

            def overflow(p):
                lo = nc.scalar.value_load(cum[0:1, bass.ds(2 * p, 1)], min_val=0, max_val=NE)
                hi = nc.scalar.value_load(cum[0:1, bass.ds(2 * p + 2, 1)], min_val=0, max_val=NE)
                with nc.scalar.If(hi > lo):
                    with nc.scalar.Fori(lo, hi) as j:
                        act.wait_ge(ov_gather_ps, 2 * j + 1)
                        nc.scalar.copy(ov_xg[:, 0:4, :], ps[:, Y[0], :].rearrange("p (a b) -> p a b", a=4)).then_inc(ov_xg_act, 1)
                        act.wait_ge(ov_pt_ps, j + 1)
                        nc.scalar.copy(ov_S[:], ps[:, T, 0:SEQ]).then_inc(ov_S_act, 1)
                        act.wait_ge(ov_gu_ps, 2 * j + 3)
                        act.wait_ge(h_dve, p + 1)
                        nc.scalar.activation(e_sg[:], ps[:, U, 0:DE], ACT.Silu).then_inc(ov_sg_act, 1)
                        act.wait_ge(ov_gslot_dve, 2 * j + 2)
                        for half in range(2):
                            act.wait_ge(ov_y_ps, 2 * j + half + 1)
                            nc.scalar.mul(yhi[:, half * 512:(half + 1) * 512], ps[:, Y[half], :],
                                          ov_gslot[:]).then_inc(ov_yhi_act, 1)

            def octets(it, gather_last):
                for j in range(8):
                    p, o, q, ob = 8 * it + j, 2 * it + j // 4, j % 4, j // 4
                    act.wait_ge(gu_ps, 2 * p + 2)
                    nc.scalar.activation(e_sg[:], ps[:, U, 0:DE], ACT.Silu).then_inc(sg_act, 1)
                    overflow(p)
                    if ob == 0 or gather_last:
                        act.wait_ge(gather_ps, 8 * (o + 1) + 2 * q + 1)
                        nc.scalar.copy(xg[1 - ob][:, 2 * q, :], ps[:, Y[0], :]).then_inc(xg_act, 1)
                    act.wait_ge(pt_ps, p + 2)
                    nc.scalar.copy(S[j % 2][:], ps[:, T, 0:SEQ]).then_inc(S_act, 1)
                    act.wait_ge(gslot_dve, 2 * p + 2)
                    for half in range(2):
                        act.wait_ge(y_ps, 2 * p + half + 1)
                        nc.scalar.mul(yhi[:, half * 512:(half + 1) * 512], ps[:, Y[half], :],
                                      gslot[:, j % 2:j % 2 + 1]).then_inc(yhi_act, 1)

            act.sem_inc(S_act, 1)
            act.sem_inc(yhi_act, 1)
            act.wait_ge(cum_dve, 1)
            with act.Fori(0, PAIRS // 8 - 1) as it:
                octets(it, True)
            octets(PAIRS // 8 - 1, False)

        @block.vector
        def _(dve):
            chain = [0]

            def link(ins):
                chain[0] += 1
                ins.then_inc(dve_chain, 1)
                dve.wait_ge(dve_chain, chain[0])

            def mean_eps(col, n_ssq):
                dve.wait_ge(ssq_act, n_ssq)
                nc.vector.tensor_scalar(stat[:, col + 2:col + 4], stat[:, col:col + 2], 1.0 / D, EPS, ALU.mult,
                                        ALU.add).then_inc(xn_dve, 1)

            def scale_rows(src, dst, col, n_std):
                dve.wait_ge(std_act, n_std)
                link(nc.vector.reciprocal(stat[:, col + 2:col + 4], stat[:, col + 2:col + 4]))
                for t in range(NT):
                    nc.vector.tensor_scalar(dst[:, t, :], src[:, t, :], stat[:, col + 2 + t:col + 3 + t], None,
                                            ALU.mult).then_inc(xn_dve, 1)

            mean_eps(0, 2)
            scale_rows(x_in, xn, 0, 1)
            dve.wait_ge(vec_ps, 1)
            nc.vector.tensor_copy(vec[:], ps[:, 5, 0:42]).then_inc(vec_dve, 1)
            dve.wait_ge(vec_dve, 1)
            for k in DVE_K:
                dve.wait_ge(xT_ps, k // 2 + 1)
                nc.vector.tensor_scalar(hT[:, k, :], ps[:, k // 2, k % 2 * SEQ:(k % 2 + 1) * SEQ], vec[:, MIX + k:MIX + k + 1], None,
                                        ALU.mult).then_inc(xT_dve, 1)
            mean_eps(4, 4)
            scale_rows(mem_in, memn, 4, 2)
            link(nc.vector.tensor_scalar(lam[:, 2, :], vec[:, LAM:LAM + 2], -1.0, None, ALU.mult))
            nc.vector.tensor_tensor(lam[:, 0, :], vec[:, LAM:LAM + 2], lam[:, 2, :], ALU.min).then_inc(lam_dve, 1)

            def log1p():
                dve.wait_ge(lam_act, 1)
                e = lam[:, 1, :]
                link(nc.vector.tensor_scalar(lam[:, 3, :], e, 2.0, None, ALU.add))
                link(nc.vector.reciprocal(lam[:, 3, :], lam[:, 3, :]))
                link(nc.vector.tensor_tensor(lam[:, 3, :], e, lam[:, 3, :], ALU.mult))
                link(nc.vector.tensor_tensor(lam[:, 4, :], lam[:, 3, :], lam[:, 3, :], ALU.mult))
                terms = 9
                link(nc.vector.tensor_scalar(lam[:, 5, :], lam[:, 4, :], 2.0 / (2 * terms + 1), 2.0 / (2 * terms - 1),
                                             ALU.mult, ALU.add))
                for n in range(terms - 2, -1, -1):
                    link(nc.vector.tensor_tensor(lam[:, 5, :], lam[:, 5, :], lam[:, 4, :], ALU.mult))
                    link(nc.vector.tensor_scalar(lam[:, 5, :], lam[:, 5, :], 2.0 / (2 * n + 1), None, ALU.add))
                link(nc.vector.tensor_tensor(lam[:, 5, :], lam[:, 5, :], lam[:, 3, :], ALU.mult))
                link(nc.vector.tensor_scalar(lam[:, 6, :], lam[:, 2, :], 0.0, None, ALU.max))
                link(nc.vector.tensor_tensor(lam[:, 6, :], lam[:, 6, :], lam[:, 5, :], ALU.add))
                nc.vector.tensor_scalar(lam[:, 7, :], lam[:, 6, :], -8.0, None, ALU.mult).then_inc(lam_dve, 1)

            def evac(n):
                dve.wait_ge(unit_ps, n + 1)
                b = ps[:, n % 4, :]
                if n < 8:
                    dst, src = qk[:, n, :], b[:, 0:SEQ]
                elif n < 10:
                    dst, src = v_sb[:, n - 8, :], b
                elif n < 12:
                    dst, src = ca_raw[:, 0, n - 10, :], b[:, 0:CA]
                elif n < 14:
                    link(nc.vector.tensor_copy(v_ca[:, n - 12, :], b[:, CA:2 * CA]))
                    dst, src = ca_raw[:, 1, n - 12, :], b[:, 0:CA]
                elif n < 16:
                    dst, src = xpad[:, n - 14, 3:3 + SEQ], b[:, 0:SEQ]
                elif n < 18:
                    dst, src = gate[:, n - 16, :], b[:, 0:SEQ]
                else:
                    j = n - 18
                    nc.vector.tensor_scalar(qkca[:, 2 * j:2 * j + 2, :], b.rearrange("p (c q) -> p c q", c=2),
                                            vec[:, QN + j:QN + j + 1], None, ALU.mult).then_inc(unit_dve, 1)
                    return
                nc.vector.tensor_copy(dst, src).then_inc(unit_dve, 1)

            def conv():
                freed(dve, 14)
                freed(dve, 15)
                for c in range(2):
                    link(nc.vector.tensor_scalar(xc[:, c, :], xpad[:, c, 3:3 + SEQ], vec[:, CW + 6 + c:CW + 7 + c],
                                                 vec[:, CB + c:CB + c + 1], ALU.mult, ALU.add))
                    for tap in range(3):
                        ins = nc.vector.scalar_tensor_tensor(xc[:, c, :], xpad[:, c, tap:tap + SEQ],
                                                             vec[:, CW + 2 * tap + c:CW + 2 * tap + c + 1], xc[:, c, :],
                                                             ALU.mult, ALU.add)
                        if tap < 2:
                            link(ins)
                        else:
                            ins.then_inc(conv_dve, 1)

            def gelu_argument():
                freed(dve, 16)
                freed(dve, 17)
                link(nc.vector.tensor_tensor(rg_g[:], gate[:], gate[:], ALU.mult))
                link(nc.vector.tensor_scalar(rg_g[:], rg_g[:], 0.044715, 1.0, ALU.mult, ALU.add))
                nc.vector.tensor_tensor(rg_g[:], rg_g[:], gate[:], ALU.mult).then_inc(gelu_dve, 1)

            for kind, n in walk:
                if kind == "unit" and owner[n] == "dve":
                    evac(n)
                elif kind == "memT":
                    for k in DVE_K:
                        dve.wait_ge(memT_ps, k // 2 + 1)
                        nc.vector.tensor_scalar(memT[:, k, :], ps[:, 4 + k // 2, k % 2 * SEQ:(k % 2 + 1) * SEQ],
                                                vec[:, MEM + k:MEM + k + 1], None, ALU.mult).then_inc(memT_dve, 1)
                elif kind == "z":
                    if n == 0:
                        dve.wait_ge(zeroed, 1)
                    dve.wait_ge(mask_pool, 4 * n + 4)
                    b = n % 2
                    kp, rs = keep[b], rest[b]
                    nc.vector.tensor_tensor_scan(rs[:, 0:P][:, ::-1], kp[:, 0:P][:, ::-1], zeros[:, 0:P], 1.0,
                                                 ALU.mult, ALU.add).then_inc(dve_chain, 1)
                    nc.vector.tensor_tensor_scan(rs[:, P + 1:NZ + 1][:, ::-1], kp[:, P:NZ][:, ::-1], zeros[:], 1.0,
                                                 ALU.mult, ALU.add).then_inc(dve_chain, 1)
                    chain[0] += 2
                    dve.wait_ge(dve_chain, chain[0])
                    nc.vector.tensor_tensor(beta[b][:, 0:P], beta[b][:, 0:P], rs[:, 1:P + 1], ALU.mult).then_inc(w_dve, 1)
                    nc.vector.tensor_tensor(beta[b][:, P:NZ], beta[b][:, P:NZ], rs[:, P + 2:NZ + 2],
                                            ALU.mult).then_inc(w_dve, 1)
                elif kind == "av":
                    if n % 2:
                        dve.wait_ge(o_ps, n + 1)
                        c = (n // 2) % 2 * SEQ
                        nc.vector.tensor_copy(yT[:, n // 2, :], ps[:, 7, c:c + SEQ]).then_inc(yT_dve, 1)
                elif kind == "conv":
                    conv()
                elif kind == "gelu":
                    gelu_argument()
                elif kind == "log1p":
                    log1p()
                elif kind == "ca_square":
                    for u in range(10, 14):
                        freed(dve, u)
                    link(nc.vector.tensor_tensor(ca_sq[:], ca_raw[:], ca_raw[:], ALU.mult))
                    link(nc.vector.reduce_sum(ca_rs[:].rearrange("p a t h -> p (a t h)"),
                                              ca_sq[:].rearrange("p a t (h d) -> p (a t h) d", d=HD), AX.X))
                    nc.vector.tensor_scalar(ca_rs[:], ca_rs[:], 1.0 / HD, EPS, ALU.mult, ALU.add).then_inc(ca_ss_dve, 1)
                elif kind == "ca_norm":
                    dve.wait_ge(ca_rt_act, 1)
                    link(nc.vector.reciprocal(ca_rs[:], ca_rs[:]))
                    heads = ca_raw[:].rearrange("p a t (h d) -> p (a t h) d", d=HD)
                    nc.vector.tensor_tensor(heads, heads, ca_rs[:].rearrange("p a t h -> p (a t h)").unsqueeze(2)
                                            .to_broadcast([P, 2 * NT * CA_HEADS, HD]), ALU.mult).then_inc(ca_rs_dve, 1)

            def ca_max(h):
                dve.wait_ge(unit_ps, 23 + h)
                link(nc.vector.reduce_max(mx[:, :, h], ps[:, (22 + h) % 4, :].rearrange("p (t m) -> p t m", t=NT), AX.X))
                nc.vector.tensor_scalar(mx[:, :, h], mx[:, :, h], -SCALE, None, ALU.mult).then_inc(camax_dve, 1)

            def ca_norm(h):
                b = h % 2
                freed(dve, 22 + h)
                sums = stat[:, 8 + 2 * b:10 + 2 * b]
                link(nc.vector.reciprocal(sums, sums))
                for t in range(NT):
                    nc.vector.tensor_scalar(ca_p[b][:, t, :], ca_p[b][:, t, :], stat[:, 8 + 2 * b + t:9 + 2 * b + t],
                                            None, ALU.mult).then_inc(cap_dve, 1)

            def ca_evac(h):
                dve.wait_ge(unit_ps, 28 + h)
                if h == 2:
                    dve.wait_ge(oca_ps, 1)
                if h == 3:
                    dve.wait_ge(unit_ps, 32)
                nc.vector.tensor_copy(ca_pT[h % 2][:], ps[:, (27 + h) % 4, :].rearrange("p (m q) -> p m q", m=2)).then_inc(unit_dve, 1)

            def ca_result(j):
                dve.wait_ge(unit_ps, 32 + j)
                nc.vector.tensor_copy(yT[:, 6 + j, :], ps[:, (31 + j) % 4, 0:SEQ]).then_inc(oca_dve, 1)

            def mean_square(g, width):
                dve.wait_ge(unit_ps, SUMS[g] + 1)
                nc.vector.tensor_scalar(g_rs[:, g, :], ps[:, SUMS[g] % 4, 0:NT], 1.0 / width, EPS, ALU.mult,
                                        ALU.add).then_inc(unit_dve, 1)

            def residual(u):
                g, t, half = projections[u]
                if t == 0 and half == 0:
                    dve.wait_ge(g_rt_act, g + 1)
                    link(nc.vector.reciprocal(g_rs[:, g, :], g_rs[:, g, :]))
                dve.wait_ge(wo_ps, u + 1)
                if g:
                    dve.wait_ge(x1_dve, projections.index((g - 1, t, half)) + 1)
                c = slice(half * 512, (half + 1) * 512)
                nc.vector.scalar_tensor_tensor(x1[:, t, c], ps[:, ACC[2 * t + half], :], g_rs[:, g, t:t + 1], x1[:, t, c],
                                               ALU.mult, ALU.add).then_inc(x1_dve, 1)

            for h in range(CA_HEADS):
                ca_max(h)
            dve.wait_ge(rg_act, 4)
            link(nc.vector.tensor_tensor(rg_u[:], rg_a[:], rg_a[:], ALU.mult))
            nc.vector.scalar_tensor_tensor(rg_t[:], rg_u[:], 1.0, rg_t[:], ALU.add, ALU.mult).then_inc(rg_dve, 1)
            ca_norm(0)
            ca_norm(1)
            mean_square(0, SB)
            ca_evac(0)
            ca_norm(2)
            ca_evac(1)
            ca_norm(3)
            link(nc.vector.tensor_tensor(rg_u[:], rg_i[:], xc[:], ALU.mult))
            dve.wait_ge(rg_act, 5)
            link(nc.vector.tensor_tensor(rg_u[:], rg_u[:], rg_t[:], ALU.mult))
            for c in range(2):
                link(nc.vector.tensor_tensor_scan(rg_r[:, c, :], rg_a[:, c, :], rg_u[:, c, :], 0.0, ALU.mult, ALU.add))
            dve.wait_ge(gelu_act, 1)
            link(nc.vector.tensor_tensor(rg_g[:], rg_g[:], gate[:], ALU.mult))
            for c in range(2):
                nc.vector.tensor_tensor(yT[:, 4 + c, :], rg_g[:, c, :], rg_r[:, c, :], ALU.mult).then_inc(yrg_dve, 1)
            ca_evac(2)
            ca_evac(3)
            ca_result(0)
            dve.wait_ge(x1_loaded, 16)
            for u in range(3):
                residual(u)
            ca_result(1)
            residual(3)
            mean_square(1, RG)
            residual(4)
            mean_square(2, CA)
            for u in range(5, 8):
                residual(u)
            for t in range(NT):
                if t == 1:
                    residual(10)
                    residual(11)
                dve.wait_ge(ssq_act, 5 + t)
                rms = stat[:, 2 + t:3 + t]
                nc.vector.tensor_scalar(rms, stat[:, t:t + 1], 1.0 / D, EPS, ALU.mult, ALU.add).then_inc(xn_dve, 1)
                dve.wait_ge(std_act, 3 + t)
                link(nc.vector.reciprocal(rms, rms))
                if t == 0:
                    dve.wait_ge(gffn_loaded, 16)
                nc.vector.scalar_tensor_tensor(xn2[:, t], x1[:, t, :].rearrange("q (p k) -> q k p", k=KD), rms,
                                               g_ffn[:].rearrange("q (p k) -> q k p", k=KD), ALU.mult,
                                               ALU.mult).then_inc(xn_dve, 1)
                if t == 0:
                    residual(8)
                    residual(9)
            for t in range(NT):
                dve.wait_ge(x2T_ps, 2 * t + 2)
                nc.vector.tensor_copy(xn2T[:, 4:8, t * P:(t + 1) * P],
                                      ps[:, 2 * t + 1, :].rearrange("p (k q) -> p k q", k=4)).then_inc(x2T_dve, 1)
            dve.wait_ge(score_act, 2)
            dve.wait_ge(rb_loaded, 16)
            dve.wait_ge(consts, 2)
            link(nc.vector.tensor_tensor(choice[:], score[:], rbias[:].unsqueeze(1).to_broadcast([P, NT, NE]), ALU.add))
            for t in range(NT):
                for g in range(GROUPS):
                    link(nc.vector.max(top8[:, t, g, :], choice[:, t, g * EG:(g + 1) * EG]))
            for t in range(NT):
                link(nc.vector.tensor_tensor(grp[:, t, 0:GROUPS], top8[:, t, :, 0], top8[:, t, :, 1], ALU.add))
                link(nc.vector.memset(grp[:, t, 12:16], -HUGE))
                link(nc.vector.max(gtop[:, t, :], grp[:, t, :]))
                link(nc.vector.match_replace(grep[:, t, :], gtop[:, t, :], grp[:, t, :], -HUGE))
                link(nc.vector.tensor_tensor(grep[:, t, 0:GROUPS], grep[:, t, 0:GROUPS], grp[:, t, 0:GROUPS], ALU.is_equal))
                m = grep[:, t, 0:GROUPS].unsqueeze(2).to_broadcast([P, GROUPS, EG])
                cg = cand[:, t, :].rearrange("p (g e) -> p g e", g=GROUPS)
                link(nc.vector.tensor_scalar(grp[:, t, 0:GROUPS], grep[:, t, 0:GROUPS], -1.0, 1.0, ALU.mult, ALU.add))
                link(nc.vector.tensor_scalar(grep[:, t, 0:GROUPS], grep[:, t, 0:GROUPS], -HUGE, None, ALU.mult))
                m1 = grp[:, t, 0:GROUPS].unsqueeze(2).to_broadcast([P, GROUPS, EG])
                link(nc.vector.tensor_tensor(cg, choice[:, t, :].rearrange("p (g e) -> p g e", g=GROUPS), m1, ALU.mult))
                link(nc.vector.tensor_tensor(cg, cg, m, ALU.add))
                link(nc.vector.max(gtop[:, t, :], cand[:, t, :]))
                link(nc.vector.match_replace(repl[:, t, :], gtop[:, t, :], cand[:, t, :], HUGE))
            link(nc.vector.tensor_scalar(repl[:], repl[:], HUGE, None, ALU.is_equal))
            nc.vector.tensor_copy(picked[:], repl[:]).then_inc(route_dve, 1)
            link(nc.vector.tensor_tensor(gatew[:], repl[:], score[:], ALU.mult))
            link(nc.vector.reduce_sum(stat[:, 4:6], gatew[:], AX.X))
            link(nc.vector.tensor_scalar(stat[:, 4:6], stat[:, 4:6], 1e-20, None, ALU.add))
            link(nc.vector.reciprocal(stat[:, 4:6], stat[:, 4:6]))
            for t in range(NT):
                link(nc.vector.tensor_scalar(gatew[:, t, :], gatew[:, t, :], stat[:, 4 + t:5 + t], 2.5, ALU.mult, ALU.mult))
            g4 = gatew[:].rearrange("p t (n two) -> p t n two", two=2)
            link(nc.vector.tensor_copy(gates2[:, :, :, 0:2], g4))
            link(nc.vector.tensor_tensor(gates2[:, :, :, 2:4], g4, gates2[:, :, :, 0:2].bitcast(F32), ALU.subtract))
            for t in range(NT):
                dve.wait_ge(s_sg_act, t + 1)
                nc.vector.tensor_tensor(s_h[:, t].rearrange("q k p -> q p k"), s_sg[:, t, :].rearrange("q (p k) -> q p k", k=KH),
                                        ps[:, t, DE:2 * DE].rearrange("q (p k) -> q p k", k=KH), ALU.mult).then_inc(s_h_dve, 1)
            dve.wait_ge(count_ps, 1)
            link(nc.vector.scalar_tensor_tensor(posm[:], ps[:, 3, 0:NT * NE].rearrange("p (t e) -> p t e", t=NT), 1.0,
                                                repl[:], ALU.add, ALU.mult))
            dve.wait_ge(s_hT_ps, 1)
            nc.vector.tensor_copy(s_hT[:], ps[:, 2, :].rearrange("p (k t) -> p k t", k=KH)).then_inc(s_hT_dve, 1)

            def build_pick(o, buf):
                for t in range(NT):
                    nc.vector.tensor_tensor(
                        pick[buf][:, t, :].rearrange("p (e s) -> p e s", s=SLOTS),
                        iota1[:, 0:SLOTS].unsqueeze(1).to_broadcast([P, 8, SLOTS]),
                        posm[:, t, bass.ds(8 * o, 8)].unsqueeze(2).to_broadcast([P, 8, SLOTS]),
                        ALU.is_equal).then_inc(pick_dve, 1)

            build_pick(0, 0)
            cr = cnt_row
            link(nc.vector.tensor_scalar(cr[:, 1, 0:NE], ps[0:1, 3, 2 * NE:3 * NE], float(SLOTS), None, ALU.is_gt))
            link(nc.vector.tensor_scalar(cr[:, 2, 0:NE], ps[0:1, 3, 2 * NE:3 * NE], float(SLOTS + P), None, ALU.is_gt))
            link(nc.vector.tensor_tensor(cr[:, 1, 0:NE], cr[:, 1, 0:NE], cr[:, 2, 0:NE], ALU.add))
            link(nc.vector.tensor_tensor_scan(cr[:, 0, 1:NE + 1], cr[:, 1, 0:NE], cr[:, 3, 0:NE], 0.0, ALU.add, ALU.add))
            nc.vector.tensor_copy(cum[:], cr[:, 0, :]).then_inc(cum_dve, 1)
            for t in range(NT):
                dve.wait_ge(split_act, t + 1)
                nc.vector.tensor_tensor(xlo[:, t], xn2[:, t], xhi[:, t].bitcast(F32), ALU.subtract).then_inc(split_dve, 1)
            for i in range(KD // 2):
                dve.wait_ge(gather_ps, 2 * i + 2)
                nc.vector.tensor_copy(xg[0][:, 2 * i + 1, :], ps[:, Y[1], :]).then_inc(xg_dve, 1)
            dve.wait_ge(cum_dve, 1)

            def slot_gates(dst, sem, sides=(0, 1)):
                for part, side in enumerate(sides):
                    rws = slice(part * SLOTS, (part + 1) * SLOTS)
                    nc.vector.reduce_sum(dst[rws], ps[rws, T, SEQ + side:SEQ + side + 3:2], AX.X).then_inc(sem, 1)

            def hidden(dst, sem):
                nc.vector.tensor_tensor(dst[:].rearrange("q k p -> q p k"), e_sg[:].rearrange("q (p k) -> q p k", k=KH),
                                        ps[:, U, DE:2 * DE].rearrange("q (p k) -> q p k", k=KH), ALU.mult).then_inc(sem, 1)

            def hidden_T(sem):
                nc.vector.tensor_copy(e_hT[:], ps[:, U, 0:2 * P].rearrange("p (k t) -> p k t", k=KH)).then_inc(sem, 1)

            def overflow(p):
                c0 = nc.vector.value_load(cum[0:1, bass.ds(2 * p, 1)], min_val=0, max_val=NE)
                c2 = nc.vector.value_load(cum[0:1, bass.ds(2 * p + 2, 1)], min_val=0, max_val=NE)
                with nc.vector.If(c2 > c0):
                    c1 = nc.vector.value_load(cum[0:1, bass.ds(2 * p + 1, 1)], min_val=0, max_val=NE)
                    for side, lo, hi in ((0, c0, c1), (1, c1, c2)):
                        with nc.vector.If(hi > lo):
                            with nc.vector.Fori(lo, hi) as j:
                                overflow_item(2 * p + side, side, j, j - lo)

            def overflow_item(e, side, j, c):
                dve.wait_ge(ov_scatter_ps, j + 1)
                first = nc.s_assert_within(
                    c * P + SLOTS, SLOTS, SLOTS + P,
                    skip_runtime_bounds_check_because="an expert has at most 256 tokens, so at most two items")
                for t in range(NT):
                    nc.vector.tensor_tensor(ov_pick[:, t, :], iota1[:, bass.ds(first, P)],
                                            posm[:, t, bass.ds(e, 1)].to_broadcast([P, P]),
                                            ALU.is_equal).then_inc(ov_pick_dve, 1)
                dve.wait_ge(ov_gather_ps, 2 * j + 2)
                nc.vector.tensor_copy(ov_xg[:, 4:8, :], ps[:, Y[1], :].rearrange("p (a b) -> p a b", a=4)).then_inc(ov_xg_dve, 1)
                dve.wait_ge(ov_S_act, j + 1)
                slot_gates(ov_gslot[:], ov_gslot_dve, (side, side))
                dve.wait_ge(ov_sg_act, j + 1)
                hidden(ov_h, ov_h_dve)
                dve.wait_ge(ov_hT_ps, j + 1)
                hidden_T(ov_hTs_dve)
                dve.wait_ge(ov_gslot_dve, 2 * j + 2)
                for half in range(2):
                    dve.wait_ge(ov_yhi_act, 2 * j + half + 1)
                    c = slice(half * 512, (half + 1) * 512)
                    nc.vector.scalar_tensor_tensor(ylo[:, c], ps[:, Y[half], :], ov_gslot[:], yhi[:, c].bitcast(F32),
                                                   ALU.mult, ALU.subtract).then_inc(ov_ylo_dve, 1)

            def octets(it, gather_last):
                for j in range(8):
                    p, o, q, ob = 8 * it + j, 2 * it + j // 4, j % 4, j // 4
                    more = ob == 0 or gather_last
                    if q == 0 and more:
                        dve.wait_ge(pt_ps, p + 1)
                        build_pick(o + 1, 1 - ob)
                    dve.wait_ge(sg_act, p + 1)
                    hidden(e_h, h_dve)
                    overflow(p)
                    if more:
                        dve.wait_ge(gather_ps, 8 * (o + 1) + 2 * q + 2)
                        nc.vector.tensor_copy(xg[1 - ob][:, 2 * q + 1, :], ps[:, Y[1], :]).then_inc(xg_dve, 1)
                    dve.wait_ge(hT_ps, p + 1)
                    hidden_T(hTs_dve)
                    dve.wait_ge(S_act, p + 2)
                    slot_gates(gslot[:, j % 2:j % 2 + 1], gslot_dve)
                    dve.wait_ge(gslot_dve, 2 * p + 2)
                    for half in range(2):
                        dve.wait_ge(yhi_act, 2 * p + half + 2)
                        c = slice(half * 512, (half + 1) * 512)
                        nc.vector.scalar_tensor_tensor(ylo[:, c], ps[:, Y[half], :], gslot[:, j % 2:j % 2 + 1],
                                                       yhi[:, c].bitcast(F32), ALU.mult, ALU.subtract).then_inc(ylo_dve, 1)

            dve.sem_inc(hTs_dve, 1)
            dve.sem_inc(ylo_dve, 1)
            with dve.Fori(0, PAIRS // 8 - 1) as it:
                octets(it, True)
            octets(PAIRS // 8 - 1, False)
            for t in range(NT):
                for half in range(2):
                    dve.wait_ge(last_ps, 2 * t + half + 1)
                    c = slice(half * 512, (half + 1) * 512)
                    nc.vector.tensor_tensor(x1[:, t, c], x1[:, t, c], ps[:, ACC[2 * t + half], :], ALU.add).then_inc(out_dve, 1)

        @block.tensor
        def _(pe):
            mm = nc.tensor.matmul

            pe.wait_ge(consts, 1)
            pe.wait_ge(vec_loaded, 16 * 14)
            nc.tensor.transpose(ps[:, 5, 0:42], vecs[:], ident[0:42, 0:42]).then_inc(vec_ps, 1)

            def transposes(src, b0, sem):
                for k in range(KD):
                    for t in range(NT):
                        c = (k % 2) * SEQ + t * P
                        last = nc.tensor.transpose(ps[:, b0 + k // 2, c:c + P], src(t, k), ident[:])
                    if k % 2:
                        last.then_inc(sem, 1)

            pe.wait_ge(xn_dve, 3)
            transposes(lambda t, k: xn[:, t, k * P:(k + 1) * P], 0, xT_ps)
            pe.wait_ge(xT_act, KD // 2)
            pe.wait_ge(xT_dve, KD // 2)

            def unit(n):
                if n >= 4:
                    freed(pe, n - 4)
                b = ps[:, n % 4, :]
                if n < 8 or 14 <= n < 18:
                    if n < 8:
                        pe.wait_ge(wA_loaded[n // 2], 16)
                        w, c = wA[n // 2], n % 2 * P
                    else:
                        g, c = rg_cols[n]
                        pe.wait_ge(wR_loaded[g], 16)
                        w = wR[g]
                    for k in range(KD):
                        last = mm(b[:, 0:SEQ], w[:, k, c:c + P], hT[:, k, :], start=k == 0, stop=k == KD - 1)
                elif n < 14:
                    first, act_T, w, out_n, loaded = (
                        (8, hT, wV, SB, wV_loaded) if n < 10 else
                        (10, hT, wR[2], CA, wR_loaded[2]) if n < 12 else (12, memT, w_kv, 2 * CA, kv_loaded))
                    pe.wait_ge(loaded, 16)
                    if n >= 12:
                        pe.wait_ge(memT_act, KD // 2)
                        pe.wait_ge(memT_dve, KD // 2)
                    c = (n - first) * P
                    for k in range(KD):
                        last = mm(b[:, 0:out_n], act_T[:, k, c:c + P], w[:, k, :], start=k == 0, stop=k == KD - 1)
                elif n < 20:
                    pe.wait_ge(ca_rs_dve, 1)
                    for m in range(2):
                        for t in range(NT):
                            c = m * SEQ + t * P
                            last = nc.tensor.transpose(b[:, c:c + P], ca_raw[:, n - 18, t, m * P:(m + 1) * P], ident[:])
                elif n < 22:
                    pe.wait_ge(conv_dve, 2)
                    pe.wait_ge(wg_loaded, 64)
                    w = wg_r if n == 20 else wg_i
                    for c in range(2):
                        for half in range(2):
                            rws = slice(half * HD, (half + 1) * HD)
                            last = mm(b[rws, c * SEQ:(c + 1) * SEQ], w[rws, c, :], xc[rws, c, :], start=True, stop=True)
                elif n < 26:
                    h = n - 22
                    rws = slice(h % 2 * HD, (h % 2 + 1) * HD)
                    freed(pe, 18)
                    freed(pe, 19)
                    for t in range(NT):
                        last = mm(b[:, t * SEQ:(t + 1) * SEQ], qkca[rws, h // 2, t * P:(t + 1) * P],
                                  qkca[rws, 2 + h // 2, :], start=True, stop=True)
                elif n in SUMS:
                    g = SUMS.index(n)
                    pe.wait_ge(ysum_pool, g + 1)
                    for t in range(NT):
                        last = mm(b[:, t:t + 1], y_sq[:, (0, 4, 6)[g], t * P:(t + 1) * P], ones[:, 0:1], start=True, stop=True)
                elif n < 31:
                    h = n - 27
                    pe.wait_ge(cap_dve, 2 * h + 2)
                    for m in range(2):
                        for t in range(NT):
                            c = m * SEQ + t * P
                            last = nc.tensor.transpose(b[:, c:c + P], ca_p[h % 2][:, t, m * P:(m + 1) * P], ident[:])
                last.then_inc(unit_ps, 1)

            for kind, n in walk:
                if kind == "unit":
                    unit(n)
                elif kind == "memT":
                    pe.wait_ge(xn_dve, 6)
                    transposes(lambda t, k: memn[:, t, k * P:(k + 1) * P], 4, memT_ps)
                elif kind == "z":
                    if n == 0:
                        freed(pe, 6)
                        freed(pe, 7)
                        pe.wait_ge(memT_act, KD // 2)
                        pe.wait_ge(memT_dve, KD // 2)
                    if n >= 2:
                        pe.wait_ge(bc_act, 2 * n - 2)
                    rws = slice(n % 2 * HD, (n % 2 + 1) * HD)
                    q, k = qk[rws, n // 2, :], qk[rws, 4 + n // 2, :]
                    mm(ps[:, 4 + n % 2, 0:P], q[:, 0:P], k[:, 0:P], start=True, stop=True)
                    mm(ps[:, 4 + n % 2, P:NZ], q[:, P:SEQ], k, start=True, stop=True).then_inc(z_ps, 1)
                elif kind == "t":
                    if n >= 1:
                        pe.wait_ge(wT_act, n)
                    pe.wait_ge(w_dve, 2 * n + 2)
                    for c in range(3):
                        last = nc.tensor.transpose(ps[:, 6, c * P:(c + 1) * P], beta[n % 2][:, c * P:(c + 1) * P], ident[:])
                    last.then_inc(wT_ps, 1)
                elif kind == "av":
                    if n == 0:
                        freed(pe, 8)
                        freed(pe, 9)
                    if n >= 2 and n % 2 == 0:
                        pe.wait_ge(yT_dve, n // 2)
                    pe.wait_ge(wT_act, n + 1)
                    c = n // 2 % 2 * SEQ
                    o = ps[n % 2 * HD:(n % 2 + 1) * HD, 7, c:c + SEQ]
                    mm(o, v_sb[:, 0, n * HD:(n + 1) * HD], wT[n % 2][:, 0:SEQ], start=True, stop=False)
                    mm(o[:, P:SEQ], v_sb[:, 1, n * HD:(n + 1) * HD], wT[n % 2][:, SEQ:NZ], start=False,
                       stop=True).then_inc(o_ps, 1)
            def ca_out(h):
                if h == 0:
                    freed(pe, 12)
                    freed(pe, 13)
                freed(pe, 27 + h)
                n = 31 + h // 2
                o = ps[h % 2 * HD:(h % 2 + 1) * HD, n % 4, 0:SEQ]
                for m in range(2):
                    last = mm(o, v_ca[:, m, h * HD:(h + 1) * HD], ca_pT[h % 2][:, m, :], start=m == 0, stop=m == 1)
                last.then_inc(unit_ps if h % 2 else oca_ps, 1)

            def project(u):
                g, t, half = projections[u]
                if u == 0:
                    pe.wait_ge(wo_loaded, 16)
                if g:
                    pe.wait_ge(x1_dve, projections.index((g - 1, t, half)) + 1)
                chunks = ((0, 1, 2, 3), (4, 5), (6, 7))[g]
                for k in chunks:
                    if t == 0 and half == 0:
                        pe.wait_ge(yg_act, k + 1)
                    last = mm(ps[:, ACC[2 * t + half], :], yT[:, k, t * P:(t + 1) * P],
                              wo[:, k, half * 512:(half + 1) * 512], start=k == chunks[0], stop=k == chunks[-1])
                last.then_inc(wo_ps, 1)

            for n in range(22, 26):
                unit(n)
            project(0)
            unit(26)
            project(1)
            unit(27)
            unit(28)
            project(2)
            unit(29)
            unit(30)
            ca_out(0)
            ca_out(1)
            project(3)
            ca_out(2)
            ca_out(3)
            unit(33)
            project(4)
            project(5)
            unit(34)
            for u in range(6, 12):
                project(u)
            pe.wait_ge(rt_loaded, 16)
            for t in range(NT):
                pe.wait_ge(xn_dve, 8 + 2 * t)
                for k in range(KD):
                    last = nc.tensor.transpose(ps[:, 2 * t + k // 4, k % 4 * P:(k % 4 + 1) * P], xn2[:, t, k, :], ident[:])
                    if k % 4 == 3:
                        last.then_inc(x2T_ps, 1)
                pe.wait_ge(x2T_act, t + 1)
                pe.wait_ge(x2T_dve, t + 1)
                for k in range(KD):
                    last = mm(ps[:, 4 + t, 0:NE], xn2T[:, k, t * P:(t + 1) * P], w_rt[:, k, :],
                              start=k == 0, stop=k == KD - 1)
                last.then_inc(rt_ps, 1)
            pe.wait_ge(gu_loaded[0], 32)
            for t in range(NT):
                for k in range(KD):
                    last = mm(ps[:, t, :], xn2T[:, k, t * P:(t + 1) * P], ring_gu[0][:, :, k, :],
                              start=k == 0, stop=k == KD - 1)
                last.then_inc(s_gu_ps, 1)
            pe.wait_ge(route_dve, 1)
            pb = ps[:, 3, :]
            mm(pb[:, 0:NE], upper[:], picked[:, 0, :], start=True, stop=True)
            mm(pb[:, NE:2 * NE], upper[:], picked[:, 1, :], start=True, stop=False)
            mm(pb[:, NE:2 * NE], ones_b[:], picked[:, 0, :], start=False, stop=True)
            mm(pb[:, 2 * NE:3 * NE], ones_b[:], picked[:, 0, :], start=True, stop=False)
            mm(pb[:, 2 * NE:3 * NE], ones_b[:], picked[:, 1, :], start=False, stop=True).then_inc(count_ps, 1)
            pe.wait_ge(s_h_dve, 2)
            for t in range(NT):
                for kk in range(KH):
                    c = kk * SEQ + t * P
                    last = nc.tensor.transpose(ps[:, 2, c:c + P], s_h[:, t, kk, :], ident[:])
            last.then_inc(s_hT_ps, 1)
            pe.wait_ge(d_loaded[0], 16)
            pe.wait_ge(s_hT_dve, 1)
            pe.wait_ge(score_act, 2)
            for t in range(NT):
                for half in range(2):
                    for kk in range(KH):
                        last = mm(ps[:, ACC[2 * t + half], :], s_hT[:, kk, t * P:(t + 1) * P],
                                  ring_d[0][:, kk, half * 512:(half + 1) * 512], start=kk == 0, stop=False,
                                  skip_group_check=True)
            last.then_inc(s_down_ps, 1)

            def gather_chunk(k, buf, bank):
                for i, (part, t) in enumerate(((xhi, 0), (xhi, 1), (xlo, 0), (xlo, 1))):
                    last = mm(ps[:, bank, :], part[:, t, k, :], pick[buf][:, t, :], start=i == 0, stop=i == 3)
                last.then_inc(gather_ps, 1)

            pe.wait_ge(split_dve, 2)
            pe.wait_ge(pick_dve, 2)
            pe.wait_ge(cum_dve, 1)
            for k in range(KD):
                if k >= 2:
                    pe.wait_ge(xg_act if k % 2 == 0 else xg_dve, k // 2)
                gather_chunk(k, 0, Y[k % 2])

            def gate_up(rows_a, rows_b, na, nb, sem):
                for k in range(KD):
                    for side, (lhs, n) in enumerate(((rows_a, na), (rows_b, nb))):
                        last = mm(ps[side * SLOTS:(side + 1) * SLOTS, U, :], lhs(k), ring_gu[n][:, :, k, :],
                                  start=k == 0, stop=k == KD - 1)
                last.then_inc(sem, 2)

            def hidden_T(h, sem):
                for kk in range(KH):
                    last = nc.tensor.transpose(ps[:, U, kk * P:(kk + 1) * P], h[:, kk, :], ident[:])
                last.then_inc(sem, 1)

            def slots_T(picks, gate_cols, sem):
                for t in range(NT):
                    nc.tensor.transpose(ps[:, T, t * P:(t + 1) * P], picks(t).bitcast(F32), ident[:])
                for t in range(NT):
                    last = mm(ps[:, T, SEQ:SEQ + 4], picks(t), gate_cols(t), start=t == 0, stop=t == NT - 1)
                last.then_inc(sem, 1)

            def down(na, nb, sem):
                for half in range(2):
                    for kk in range(KH):
                        for side, n in enumerate((na, nb)):
                            last = mm(ps[side * SLOTS:(side + 1) * SLOTS, Y[half], :],
                                      e_hT[:, kk, side * SLOTS:(side + 1) * SLOTS],
                                      ring_d[n][:, kk, half * 512:(half + 1) * 512], start=kk == 0, stop=kk == KH - 1)
                    last.then_inc(sem, 1)

            def scatter(to_token, hi, lo, sem, final=False):
                for t in range(NT):
                    for half in range(2):
                        for i, y in enumerate((hi, lo)):
                            last = mm(ps[:, ACC[2 * t + half], :], to_token[:, t * P:(t + 1) * P],
                                      y[:, half * 512:(half + 1) * 512], start=False, stop=final and i == 1,
                                      skip_group_check=True)
                        if final:
                            last.then_inc(sem, 1)
                if not final:
                    last.then_inc(sem, 1)

            def overflow_item(p, j, n, d_fill):
                pe.wait_ge(ov_pick_dve, 2 * j + 2)
                for k in range(KD):
                    for t in range(NT):
                        last = mm(ps[:, Y[k // 4], k % 4 * P:(k % 4 + 1) * P], xn2[:, t, k, :],
                                  ov_pick[:, t, :].bitcast(F32), start=t == 0, stop=t == NT - 1)
                    if k % 4 == 3:
                        last.then_inc(ov_gather_ps, 1)
                slots_T(lambda t: ov_pick[:, t, :], lambda t: gates2[:, t, bass.ds(p, 1), :], ov_pt_ps)
                pe.wait_ge(h_dve, p + 1)
                pe.wait_ge(ov_xg_act, j + 1)
                pe.wait_ge(ov_xg_dve, j + 1)
                gate_up(lambda k: ov_xg[:, k, 0:SLOTS], lambda k: ov_xg[:, k, SLOTS:P], n, n, ov_gu_ps)
                pe.wait_ge(ov_h_dve, j + 1)
                hidden_T(ov_h, ov_hT_ps)
                pe.wait_ge(d_loaded[n], d_fill)
                pe.wait_ge(ov_hTs_dve, j + 1)
                down(n, n, ov_y_ps)
                pe.wait_ge(ov_yhi_act, 2 * j + 2)
                pe.wait_ge(ov_ylo_dve, 2 * j + 2)
                pe.wait_ge(ov_S_act, j + 1)
                scatter(ov_S, yhi, ylo, ov_scatter_ps)

            def octets(it, gather_last):
                for j in range(8):
                    p, o, q, ob = 8 * it + j, 2 * it + j // 4, j % 4, j // 4
                    na, nb = slot(2 * j), slot(2 * j + 1)
                    more = ob == 0 or gather_last
                    if q == 0:
                        pe.wait_ge(xg_act, 4 * (o + 1))
                        pe.wait_ge(xg_dve, 4 * (o + 1))
                    pe.wait_ge(gu_loaded[na], 32 * fills(it, 2 * j))
                    pe.wait_ge(gu_loaded[nb], 32 * fills(it, 2 * j + 1))
                    pe.wait_ge(hTs_dve, p + 1)
                    c = 2 * q * SLOTS
                    gate_up(lambda k: xg[ob][:, k, c:c + SLOTS], lambda k: xg[ob][:, k, c + SLOTS:c + 2 * SLOTS],
                            na, nb, gu_ps)
                    pe.wait_ge(yhi_act, 2 * p + 1)
                    pe.wait_ge(ylo_dve, 2 * p + 1)
                    pe.wait_ge(S_act, p + 1)
                    if j == 0:
                        pe.wait_ge(zeroed, 2)
                    scatter(S[(j + 1) % 2], yhi, ylo, scatter_ps)
                    c0 = nc.tensor.value_load(cum[0:1, bass.ds(2 * p, 1)], min_val=0, max_val=NE)
                    c2 = nc.tensor.value_load(cum[0:1, bass.ds(2 * p + 2, 1)], min_val=0, max_val=NE)
                    with nc.tensor.If(c2 > c0):
                        c1 = nc.tensor.value_load(cum[0:1, bass.ds(2 * p + 1, 1)], min_val=0, max_val=NE)
                        for side, (lo, hi) in enumerate(((c0, c1), (c1, c2))):
                            with nc.tensor.If(hi > lo):
                                with nc.tensor.Fori(lo, hi) as item:
                                    overflow_item(p, item, (na, nb)[side], 16 * fills(it, 2 * j + side))
                    if more:
                        if q == 0:
                            pe.wait_ge(pick_dve, 2 * (o + 2))
                        gather_chunk(2 * q, 1 - ob, Y[0])
                        gather_chunk(2 * q + 1, 1 - ob, Y[1])
                    pe.wait_ge(h_dve, p + 1)
                    hidden_T(e_h, hT_ps)
                    slots_T(lambda t: pick[ob][:, t, c:c + 2 * SLOTS], lambda t: gates2[:, t, bass.ds(p, 1), :], pt_ps)
                    pe.wait_ge(d_loaded[na], 16 * fills(it, 2 * j))
                    pe.wait_ge(d_loaded[nb], 16 * fills(it, 2 * j + 1))
                    pe.wait_ge(hTs_dve, p + 2)
                    if more:
                        pe.wait_ge(xg_act, 4 * (o + 1) + q + 1)
                        pe.wait_ge(xg_dve, 4 * (o + 1) + q + 1)
                    down(na, nb, y_ps)

            pe.sem_inc(pt_ps, 1)
            pe.sem_inc(ov_scatter_ps, 1)
            pe.sem_inc(ov_gu_ps, 1)
            with pe.Fori(0, PAIRS // 8 - 1) as it:
                octets(it, True)
            octets(PAIRS // 8 - 1, False)
            pe.wait_ge(yhi_act, 2 * PAIRS + 1)
            pe.wait_ge(ylo_dve, 2 * PAIRS + 1)
            pe.wait_ge(S_act, PAIRS + 1)
            scatter(S[(PAIRS + 1) % 2], yhi, ylo, last_ps, final=True)


_INS = ['x', 'mem', 'norm_mix_g', 'norm_mem_g', 'w_in', 'conv_w', 'conv_b', 'w_rgate', 'b_rgate', 'w_igate', 'b_igate',
        'lru_lambda', 'w_mem_kv', 'q_norm_g', 'k_norm_g', 'g_out_sb', 'g_out_rg', 'g_out_ca', 'w_out', 'norm_ffn_g',
        'w_router', 'router_bias', 'w_gate_e', 'w_up_e', 'w_down_e', 'w_gate_sh', 'w_up_sh', 'w_down_sh']


def kernel(**inputs):
    import numpy as _np
    import concourse.bacc as _bacc
    from concourse import mybir as _mybir
    from concourse.bass_utils import run_bass_kernel_spmd as _run

    nc = _bacc.Bacc("TRN2", target_bir_lowering=False, num_devices=1)
    arrays, args = {}, []
    for name in _INS:
        a = _np.ascontiguousarray(inputs[name])
        arrays[f"in_{name}"] = a
        args.append(nc.dram_tensor(f"in_{name}", a.shape, _mybir.dt.from_np(a.dtype), kind="ExternalInput").ap())
    o = nc.dram_tensor("out_0", inputs["x"].shape, _mybir.dt.float32, kind="ExternalOutput").ap()
    hybrid_decoder_layer(nc, *args, o)
    r = _run(nc, [arrays], core_ids=[0])
    return r.results[0]["out_0"]
```

```python
import concourse.bass as bass
from concourse import mybir
from contextlib import ExitStack


def hybrid_decoder_layer(
    nc: bass.Bass,
    x, mem, norm_mix_g, norm_mem_g, w_in, conv_w, conv_b, w_rgate, b_rgate, w_igate, b_igate, lru_lambda,
    w_mem_kv, q_norm_g, k_norm_g, g_out_sb, g_out_rg, g_out_ca, w_out, norm_ffn_g, w_router, router_bias,
    w_gate_e, w_up_e, w_down_e, w_gate_sh, w_up_sh, w_down_sh, out,
):
    F32, F32R, BF16, I32 = mybir.dt.float32, mybir.dt.float32r, mybir.dt.bfloat16, mybir.dt.int32
    ALU = mybir.AluOpType
    ACT = mybir.ActivationFunctionType
    AX = mybir.AxisListType

    P = 128
    _, SEQ, D = x.shape
    NT = SEQ // P
    KD = D // P
    HD = 64
    SB, RG, CA = 512, 256, 256
    SB_HEADS, CA_HEADS = SB // HD, CA // HD
    NE, GROUPS, DE = w_router.shape[2], 8, w_gate_e.shape[3]
    EG = NE // GROUPS
    KH = DE // P
    SLOTS = 64
    PAIRS = NE // 2
    EPS = 1e-6
    HUGE = 3.0e38
    SCALE = HD ** -0.5
    RING = 4
    WARM_UP = 8

    KB = 1024
    base = (nc.sbuf_base + 31) // 32 * 32
    o_ring = base
    o_A = o_ring + 96 * KB
    o_R = o_A + 32 * KB
    o_V = o_R + 24 * KB
    o_O = o_V + 16 * KB

    def at(name, offset, shape, dt=F32):
        return nc.alloc_sbuf_tensor_at(name, shape, dt, offset=offset)

    class Space:
        def __init__(self, offset):
            self.offset = offset

        def __call__(self, name, shape, dt=F32):
            t = at(name, self.offset, shape, dt)
            n = 1
            for s in shape[1:]:
                n *= s
            self.offset += (n * (2 if dt == BF16 else 4) + 31) // 32 * 32
            return t

    ring_gu = [at(f"ring_gu{s}", o_ring + 24 * KB * s, [P, 2, KD, DE]) for s in range(RING)]
    ring_d = [at(f"ring_d{s}", o_ring + 24 * KB * s + 16 * KB, [P, KH, D]) for s in range(RING)]
    xn = at("xn", o_ring, [P, NT, D])
    memn = at("memn", o_ring + 8 * KB, [P, NT, D])
    x_in = at("x_in", o_ring + 24 * KB, [P, NT, D])
    hT = at("hT", o_ring + 48 * KB, [P, KD, SEQ])
    memT = at("memT", o_ring + 56 * KB, [P, KD, SEQ])
    hT_hi = at("hT_hi", o_ring + 16 * KB, [P, KD, SEQ], F32R)
    hT_lo = at("hT_lo", o_ring + 24 * KB, [P, KD, SEQ], F32R)
    wV_hi = at("wV_hi", o_ring + 32 * KB, [P, KD, 512], F32R)
    w_kv_hi = at("w_kv_hi", o_A, [P, KD, 512], F32R)
    memT_hi = at("memT_hi", o_A + 16 * KB, [P, KD, SEQ], F32R)
    memT_lo = at("memT_lo", o_A + 24 * KB, [P, KD, SEQ], F32R)
    w_kv_lo = at("w_kv_lo", o_ring + 72 * KB, [P, KD, 2 * CA], F32R)
    w_kv = at("w_kv", o_ring + 72 * KB, [P, KD, 2 * CA])
    ca_raw = at("ca_raw", o_ring + 64 * KB, [P, 2, NT, CA])
    ca_sq = at("ca_sq", o_ring + 68 * KB, [P, 2, NT, CA])
    mem_in = at("mem_in", o_ring + 88 * KB, [P, NT, D])
    wA = [at(f"wA{g}", o_A + 8 * KB * g, [P, KD, 256]) for g in range(4)]
    wo = at("wo", o_A, [P, KD, D])
    xg = [at(f"xg{b}", o_A + 16 * KB * b, [P, KD, 512]) for b in range(2)]
    s_sg = at("s_sg", o_A + 24 * KB, [P, NT, DE])
    s_h = at("s_h", o_A + 26 * KB, [P, NT, KH, P])
    s_hT = at("s_hT", o_A + 28 * KB, [P, KH, SEQ])
    wR = [at(f"wR{g}", o_R + 8 * KB * g, [P, KD, 256]) for g in range(3)]
    r = Space(o_R)
    rg_r = r("rg_r", [P, 2, SEQ])
    rg_i = r("rg_i", [P, 2, SEQ])
    rg_a = r("rg_a", [P, 2, SEQ])
    rg_t = r("rg_t", [P, 2, SEQ])
    rg_u = r("rg_u", [P, 2, SEQ])
    y_sq = at("y_sq", o_R + 16 * KB, [P, KD, SEQ])
    x1_sq = at("x1_sq", o_R + 8 * KB, [P, D])
    xhi = at("xhi", o_R, [P, NT, KD, P], F32R)
    xlo = at("xlo", o_R + 8 * KB, [P, NT, KD, P], F32R)
    xn2T = at("xn2T", o_R + 16 * KB, [P, KD, SEQ])
    yhi = at("yhi", o_R + 16 * KB, [P, D], F32R)
    ylo = at("ylo", o_R + 20 * KB, [P, D], F32R)
    wV = at("wV", o_V, [P, KD, SB])
    wV_lo = at("wV_lo", o_V, [P, KD, SB], F32R)
    r = Space(o_ring)
    NZ = 3 * P
    beta = [r(f"beta{b}", [P, NZ]) for b in range(2)]
    keep = [r(f"keep{b}", [P, NZ]) for b in range(2)]
    rest = [r(f"rest{b}", [P, NZ + 2]) for b in range(2)]
    wT = [r(f"wT{b}", [P, NZ]) for b in range(2)]
    ca_p = [at(f"ca_p{b}", o_V + 2 * KB * b, [P, NT, SEQ]) for b in range(2)]
    ca_pT = [at(f"ca_pT{b}", o_V + 4 * KB + 2 * KB * b, [P, 2, SEQ]) for b in range(2)]
    pick = [at(f"pick{b}", o_V + 4 * KB * b, [P, NT, 8 * SLOTS], F32R) for b in range(2)]
    xc = at("xc", o_V + 8 * KB, [P, 2, SEQ])
    rg_g = at("rg_g", o_V + 10 * KB, [P, 2, SEQ])
    xn2 = at("xn2", o_V + 8 * KB, [P, NT, KD, P])
    r = Space(o_O)
    qk = r("qk", [P, 8, SEQ])
    v_sb = r("v_sb", [P, NT, SB])
    xpad = r("xpad", [P, 2, SEQ + 3])
    gate = r("gate", [P, 2, SEQ])
    qkca = r("qkca", [P, 4, SEQ])
    v_ca = r("v_ca", [P, NT, CA])
    yT = r("yT", [P, KD, SEQ])
    x1 = at("x1", o_O, [P, NT, D])
    ov_xg = at("ov_xg", o_O + 8 * KB, [P, KD, P])
    g_ffn = at("g_ffn", o_O + 12 * KB + 2080 + 2 * KB, [P, D])
    rt = Space(o_O + 8 * KB)
    w_rt = rt("w_rt", [P, KD, NE])
    rbias = rt("rbias", [P, NE])
    top8 = rt("top8", [P, NT, GROUPS, 8])
    gtop = rt("gtop", [P, NT, 8])
    grep = rt("grep", [P, NT, 16])
    rt = Space(o_O + 12 * KB)
    score = rt("score", [P, NT, NE])
    choice = rt("choice", [P, NT, NE])
    rt = Space(o_O + 12 * KB + 2080 + 6 * KB)
    cand = rt("cand", [P, NT, NE])
    repl = rt("repl", [P, NT, NE])
    gatew = rt("gatew", [P, NT, NE])
    rt = Space(o_O + 12 * KB + 2080 + 8 * KB)
    e_h = rt("e_h", [P, KH, P])
    e_sg = rt("e_sg", [P, DE])
    e_hT = rt("e_hT", [P, KH, P])
    S = [rt(f"S{b}", [P, SEQ], F32R) for b in range(2)]
    ov_pick = rt("ov_pick", [P, NT, P], F32R)
    ov_S = rt("ov_S", [P, SEQ], F32R)
    ov_h = rt("ov_h", [P, KH, P])
    ident = r("ident", [P, P])
    ones = r("ones", [P, P])
    upper = r("upper", [P, P], BF16)
    ones_b = r("ones_b", [P, P], BF16)
    vecs = r("vecs", [42, P])
    vec = r("vec", [P, 42])
    zeros = r("zeros", [P, SEQ])
    iota1 = r("iota1", [P, SEQ + SLOTS])
    wg_r = r("wg_r", [P, 2, HD])
    wg_i = r("wg_i", [P, 2, HD])
    picked = r("picked", [P, NT, NE], BF16)
    posm = r("posm", [P, NT, NE])
    gates2 = r("gates2", [P, NT, PAIRS, 4], F32R)
    stat = r("stat", [P, 16])
    gslot = r("gslot", [P, 2])
    ov_gslot = r("ov_gslot", [P, 1])
    lam = r("lam", [P, 8, 2])
    mx = r("mx", [P, 2, 4])
    ca_rs = r("ca_rs", [P, 2, NT, CA_HEADS])
    g_rs = r("g_rs", [P, 3, NT])
    grp = r("grp", [P, NT, 16])
    cnt_row = r("cnt_row", [1, 4, NE + 1])
    cum = r("cum", [1, NE + 1], I32)
    assert r.offset <= nc.sbuf_usable_end, r.offset - nc.sbuf_usable_end

    MIX, MEM, GOUT, CW, CB, BR, BI, LAM, QN, KN = 0, 8, 16, 24, 32, 34, 36, 38, 40, 41

    with ExitStack() as ctx:
        ps = ctx.enter_context(nc.psum_tensor("ps", [P, 8, 512], F32))
        U, T, Y, ACC = 0, 1, (2, 3), (4, 5, 6, 7)
        (
            x_loaded, mem_loaded, vec_loaded, wg_loaded, wV_loaded, kv_loaded, wo_loaded, x1_loaded,
            gffn_loaded, rt_loaded, rb_loaded, consts, zeroed, ssq_act, std_act, xn_dve, vec_ps, vec_dve,
            xT_ps, xT_act, xT_dve, memT_ps, memT_act, memT_dve, unit_ps, unit_act, unit_dve, conv_dve, z_ps,
            bc_act, mask_pool, w_dve, wT_ps, wT_act, o_ps, yT_dve, lam_act, lam_dve, gelu_dve, gelu_act,
            rg_act, camax_dve, cap_dve, oca_ps, oca_dve, yrg_dve, ysq_act, wo_ps, x1_dve, x2T_ps, x2T_act,
            x2T_dve, split_act, split_dve, rt_ps, score_act, route_dve, count_ps, cum_dve, s_gu_ps,
            s_sg_act, s_h_dve, s_hT_ps, s_hT_dve, s_down_ps, pick_dve, gather_ps, xg_act, xg_dve, gu_ps,
            sg_act, h_dve, hT_ps, hTs_dve, pt_ps, S_act, gslot_dve, y_ps, yhi_act, ylo_dve,
            ov_pick_dve, ov_gather_ps, ov_xg_act, ov_xg_dve, ov_pt_ps, ov_S_act, ov_gslot_dve, ov_gu_ps,
            ov_sg_act, ov_h_dve, ov_hT_ps, ov_hTs_dve, ov_y_ps, ov_yhi_act, ov_ylo_dve, ov_scatter_ps,
            last_ps, out_dve, stored, act_chain, dve_chain, pool_chain, rg_dve, ca_ss_dve, ca_rt_act,
            ca_rs_dve, gates_dve, ahi_act, alo_dve, whi_act, wlo_dve, yg_act, ysum_pool, g_rt_act,
        ) = [ctx.enter_context(nc.semaphore(name)) for name in """
            x_loaded mem_loaded vec_loaded wg_loaded wV_loaded kv_loaded wo_loaded x1_loaded gffn_loaded
            rt_loaded rb_loaded consts zeroed ssq_act std_act xn_dve vec_ps vec_dve xT_ps xT_act xT_dve
            memT_ps memT_act memT_dve unit_ps unit_act unit_dve conv_dve z_ps bc_act mask_pool w_dve
            wT_ps wT_act o_ps yT_dve lam_act lam_dve gelu_dve gelu_act rg_act camax_dve cap_dve oca_ps
            oca_dve yrg_dve ysq_act wo_ps x1_dve x2T_ps x2T_act x2T_dve split_act split_dve rt_ps
            score_act route_dve count_ps cum_dve s_gu_ps s_sg_act s_h_dve s_hT_ps s_hT_dve s_down_ps
            pick_dve gather_ps xg_act xg_dve gu_ps sg_act h_dve hT_ps hTs_dve pt_ps S_act gslot_dve y_ps
            yhi_act ylo_dve ov_pick_dve ov_gather_ps ov_xg_act ov_xg_dve ov_pt_ps ov_S_act
            ov_gslot_dve ov_gu_ps ov_sg_act ov_h_dve ov_hT_ps ov_hTs_dve ov_y_ps ov_yhi_act ov_ylo_dve
            ov_scatter_ps last_ps out_dve stored act_chain dve_chain pool_chain rg_dve ca_ss_dve
            ca_rt_act ca_rs_dve gates_dve ahi_act alo_dve whi_act wlo_dve yg_act ysum_pool g_rt_act
        """.split()]
        wA_loaded = [ctx.enter_context(nc.semaphore(f"wA_loaded{g}")) for g in range(4)]
        wR_loaded = [ctx.enter_context(nc.semaphore(f"wR_loaded{g}")) for g in range(3)]
        gu_loaded = [ctx.enter_context(nc.semaphore(f"gu_loaded{i}")) for i in range(RING)]
        d_loaded = [ctx.enter_context(nc.semaphore(f"d_loaded{i}")) for i in range(RING)]
        block = ctx.enter_context(nc.Block())

        owner = ["act" if n % 2 == 0 else "dve" for n in range(18)]
        owner += ["dve", "dve", "act", "act"] + ["act"] * 4 + ["dve"] * 5 + [None, None] + ["dve"] * 2
        walk = [("unit", n) for n in range(4)] + [("mem_norm", 0)] + [
            ("unit", 4), ("split_w", 0), ("unit", 5), ("split_w", 1), ("unit", 6), ("unit", 7), ("memT", 0)]
        for i in range(1, 15):
            walk.append(("unit", 7 + i))
            if i <= 8:
                walk.append(("z", i - 1))
            if 3 <= i <= 10:
                walk.append(("t", i - 3))
            if 4 <= i <= 11:
                walk.append(("av", i - 4))
            walk += {1: [("split_a", 1)], 2: [("split_w", 2)], 3: [("split_w", 3)], 5: [("log1p", 0)], 7: [("ca_square", 0)], 8: [("ca_norm", 0)], 9: [("conv", 0)],
                     11: [("gelu", 0)]}.get(i, [])

        rg_cols = {14: (0, 0), 15: (0, P), 16: (1, 0), 17: (1, P)}

        SUMS = (26, 33, 34)
        projections = [(g, t, half) for gs, ts in (((0,), (0, 1)), ((1, 2), (0,)), ((1, 2), (1,)))
                       for g in gs for t in ts for half in range(2)]

        ACT_K, DVE_K = [0, 1, 4, 5], [2, 3, 6, 7]

        def freed(eng, n):
            count = owner[:n + 1].count(owner[n])
            eng.wait_ge(unit_act if owner[n] == "act" else unit_dve, count)

        def slot(j):
            return (j + 1) % RING

        def fills(it, j):
            return 4 * it + (j + 1) // RING + 1

        def load_expert(sp, n_slot, gate_src, up_src, down_src):
            sp.dma_start(ring_gu[n_slot][:, 0], gate_src.rearrange("(p k) n -> p k n", k=KD)).then_inc(gu_loaded[n_slot], 16)
            sp.dma_start(ring_gu[n_slot][:, 1], up_src.rearrange("(p k) n -> p k n", k=KD)).then_inc(gu_loaded[n_slot], 16)
            sp.dma_start(ring_d[n_slot][:], down_src.rearrange("(p k) n -> p k n", k=KH)).then_inc(d_loaded[n_slot], 16)

        @block.sync
        def _(sp):
            def cols(c, n):
                return w_in[0][:, c:c + n].rearrange("(k p) n -> p k n", p=P)

            sp.dma_start(x_in[:], x[0].rearrange("(t p) d -> p t d", p=P)).then_inc(x_loaded, 16)
            def rows(v, n):
                return v.rearrange("(a p) -> a p", a=n)

            at_row = 0
            for v, n in ((norm_mix_g[0], 8), (norm_mem_g[0], 8), (g_out_sb[0], 4), (g_out_rg[0], 2), (g_out_ca[0], 2),
                         (conv_w[0].rearrange("t c -> (t c)"), 8), (conv_b[0], 2), (b_rgate[0], 2), (b_igate[0], 2),
                         (lru_lambda[0], 2)):
                sp.dma_start(vecs[at_row:at_row + n, :], rows(v, n)).then_inc(vec_loaded, 16)
                at_row += n
            for i, v in enumerate((q_norm_g[0], k_norm_g[0])):
                for half in range(2):
                    sp.dma_start(vecs[QN + i:QN + i + 1, half * HD:(half + 1) * HD], rows(v, 1)).then_inc(vec_loaded, 16)
            for g in range(4):
                sp.dma_start(wA[g][:], cols(256 * g, 256)).then_inc(wA_loaded[g], 16)
            sp.dma_start(mem_in[:], mem[0].rearrange("(t p) d -> p t d", p=P)).then_inc(mem_loaded, 16)
            sp.dma_start(wV[:], cols(2 * SB, SB)).then_inc(wV_loaded, 16)
            for g in (2, 0, 1):
                if g == 0:
                    sp.dma_start(w_kv[:], w_mem_kv[0].rearrange("(k p) n -> p k n", p=P)).then_inc(kv_loaded, 16)
                sp.dma_start(wR[g][:], cols(3 * SB + 256 * g, 256)).then_inc(wR_loaded[g], 16)
            sp.wait_ge(unit_ps, 10)
            load_expert(sp, 1, w_gate_e[0, 0], w_up_e[0, 0], w_down_e[0, 0])
            sp.wait_ge(unit_ps, 14)
            sp.dma_start(wo[:], w_out[0].rearrange("(k p) n -> p k n", p=P)).then_inc(wo_loaded, 16)
            sp.wait_ge(o_ps, SB_HEADS)
            load_expert(sp, 0, w_gate_sh[0], w_up_sh[0], w_down_sh[0])
            sp.wait_ge(unit_ps, 20)
            for e in (1, 2):
                load_expert(sp, slot(e), w_gate_e[0, e], w_up_e[0, e], w_down_e[0, e])
            sp.wait_ge(s_down_ps, 1)
            load_expert(sp, slot(3), w_gate_e[0, 3], w_up_e[0, 3], w_down_e[0, 3])
            sp.wait_ge(cum_dve, 1)
            with sp.Fori(0, (NE - 4) // 4) as i:
                for half in range(2):
                    p = 2 * i + half
                    done = nc.sync.value_load(cum[0:1, bass.ds(2 * p + 2, 1)], min_val=0, max_val=NE)
                    sp.wait_ge(ov_gu_ps, 2 * done + 1)
                    sp.wait_ge(gu_ps, 2 * p + 2)
                    for side in range(2):
                        e = 4 * i + 2 * half + side + 4
                        n = slot(2 * half + side)
                        sp.dma_start(ring_gu[n][:, 0], w_gate_e[0, bass.ds(e, 1)].rearrange("o (p k) n -> p (o k) n", k=KD)).then_inc(gu_loaded[n], 16)
                        sp.dma_start(ring_gu[n][:, 1], w_up_e[0, bass.ds(e, 1)].rearrange("o (p k) n -> p (o k) n", k=KD)).then_inc(gu_loaded[n], 16)
                    sp.wait_ge(y_ps, 2 * p + 2)
                    for side in range(2):
                        e = 4 * i + 2 * half + side + 4
                        n = slot(2 * half + side)
                        sp.dma_start(ring_d[n][:], w_down_e[0, bass.ds(e, 1)].rearrange("o (p k) n -> p (o k) n", k=KH)).then_inc(d_loaded[n], 16)
            for t in range(NT):
                for half in range(2):
                    sp.wait_ge(out_dve, 2 * t + half + 1)
                    c = slice(half * 512, (half + 1) * 512)
                    sp.dma_start(out[0, t * P:(t + 1) * P, c], x1[:, t, c]).then_inc(stored, 16)
            sp.wait_ge(stored, 16 * 2 * NT)

        @block.gpsimd
        def _(pool):
            chain = [0]

            def link(ins):
                chain[0] += 1
                ins.then_inc(pool_chain, 1)
                pool.wait_ge(pool_chain, chain[0])

            def diagonal(t, value_off, cmp, lo, n):
                return pool.affine_select(out=t, in_=t, compare_op=cmp, fill=value_off, base=lo, pattern=[[-1, n]],
                                          channel_multiplier=1)

            pool.memset(stat[:, 14:15], 0.0).then_inc(consts, 1)
            link(pool.memset(ident[:], 0.0))
            link(pool.memset(zeros[:], 0.0))
            link(pool.memset(ones[:], 1.0))
            diagonal(ident[:], 1.0, ALU.not_equal, 0, P).then_inc(consts, 1)
            link(pool.memset(ones_b[:], 1.0))
            link(pool.memset(xpad[:, :, 0:3], 0.0))
            link(pool.memset(cnt_row[:], 0.0))
            link(pool.memset(upper[:], 1.0))
            link(pool.affine_select(out=upper[:], in_=upper[:], compare_op=ALU.is_gt, fill=0.0, base=0,
                                    pattern=[[1, P]], channel_multiplier=-1))
            link(pool.iota(iota1[:], pattern=[[1, SEQ + SLOTS]], base=1, channel_multiplier=0,
                           allow_small_or_imprecise_dtypes=True))
            pool.memset(grp[:], HUGE).then_inc(consts, 1)
            pool.wait_ge(memT_ps, 4)
            for b in range(2):
                link(pool.memset(rest[b][:, P:P + 1], 1.0))
                last = pool.memset(rest[b][:, NZ + 1:NZ + 2], 1.0)
                link(last)
            pool.memset(stat[:, 15:16], 0.0).then_inc(zeroed, 1)
            for kind, h in walk:
                if kind != "z":
                    continue
                pool.wait_ge(bc_act, 2 * h + 2)
                for t, off in ((keep[h % 2], 1.0), (beta[h % 2], 0.0)):
                    for c in (0, 2):
                        last = pool.affine_select(out=t[:, c * P:(c + 1) * P], in_=t[:, c * P:(c + 1) * P],
                                                  compare_op=ALU.is_gt, fill=off, base=0, pattern=[[-1, P]],
                                                  channel_multiplier=1)
                        last.then_inc(mask_pool, 1)
            pool.wait_ge(z_ps, SB_HEADS)
            pool.dma_start(x1[:], x[0].rearrange("(t p) d -> p t d", p=P)).then_inc(x1_loaded, 16)
            pool.wait_ge(o_ps, SB_HEADS)
            pool.dma_start(w_rt[:], w_router[0].rearrange("(p k) e -> p k e", k=KD)).then_inc(rt_loaded, 16)
            pool.dma_start(rbias[:], router_bias[0].partition_broadcast(P)).then_inc(rb_loaded, 16)
            pool.wait_ge(ysq_act, 4)
            link(pool.tensor_tensor(y_sq[:, 0:2, :], y_sq[:, 0:2, :], y_sq[:, 2:4, :], ALU.add))
            pool.tensor_tensor(y_sq[:, 0, :], y_sq[:, 0, :], y_sq[:, 1, :], ALU.add).then_inc(ysum_pool, 1)
            pool.wait_ge(unit_ps, 26)
            pool.dma_start(g_ffn[:], norm_ffn_g[0].partition_broadcast(P)).then_inc(gffn_loaded, 16)
            for k in (4, 6):
                pool.wait_ge(ysq_act, k + 2)
                pool.tensor_tensor(y_sq[:, k, :], y_sq[:, k, :], y_sq[:, k + 1, :], ALU.add).then_inc(ysum_pool, 1)
            pool.wait_ge(s_gu_ps, 2)
            link(pool.memset(yhi[:].bitcast(F32), 0.0))
            link(pool.memset(ylo[:].bitcast(F32), 0.0))
            pool.memset(S[1][:].bitcast(F32), 0.0).then_inc(zeroed, 1)

        @block.scalar
        def _(act):
            chain = [0]

            def link(ins):
                chain[0] += 1
                ins.then_inc(act_chain, 1)
                act.wait_ge(act_chain, chain[0])

            def squares(src, col, n0):
                for t in range(NT):
                    if n0 + t:
                        act.wait_ge(ssq_act, n0 + t)
                    nc.scalar.activation(ca_sq[:].rearrange("p a t c -> p (a t c)"), src[:, t, :], ACT.Square,
                                         accum_out=stat[:, col + t:col + t + 1]).then_inc(ssq_act, 1)

            def root(col, n):
                act.wait_ge(xn_dve, n)
                nc.scalar.activation(stat[:, col + 2:col + 4], stat[:, col + 2:col + 4], ACT.Sqrt).then_inc(std_act, 1)

            act.wait_ge(consts, 1)
            nc.scalar.activation(stat[:, 14:15], stat[:, 14:15], ACT.Sqrt).then_inc(act_chain, 1)
            chain[0] += 1
            act.wait_ge(x_loaded, 16)
            squares(x_in, 0, 0)
            root(0, 1)
            for w, t in ((w_rgate, wg_r), (w_igate, wg_i)):
                wv = w[0].rearrange("(j two) c d -> two c j d", two=2)
                for half in range(2):
                    act.dma_start(t[half * HD:(half + 1) * HD], wv[half]).then_inc(wg_loaded, 16)
            act.wait_ge(vec_dve, 1)
            for k in ACT_K:
                act.wait_ge(xT_ps, k // 2 + 1)
                nc.scalar.mul(hT[:, k, :], ps[:, 4 + k // 2, k % 2 * SEQ:(k % 2 + 1) * SEQ], vec[:, MIX + k:MIX + k + 1]).then_inc(xT_act, 1)
            act.wait_ge(lam_dve, 1)
            nc.scalar.activation(lam[:, 1, :], lam[:, 0, :], ACT.Exp).then_inc(lam_act, 1)

            def evac(n):
                act.wait_ge(unit_ps, n + 1)
                b = ps[:, n % 4, :]
                if n < 8:
                    nc.scalar.copy(qk[:, n, :], b[:, 0:SEQ]).then_inc(unit_act, 1)
                elif n < 10:
                    nc.scalar.copy(v_sb[:, n - 8, :], b).then_inc(unit_act, 1)
                elif n < 12:
                    nc.scalar.copy(ca_raw[:, 0, n - 10, :], b[:, 0:CA]).then_inc(unit_act, 1)
                elif n < 14:
                    link(nc.scalar.copy(v_ca[:, n - 12, :], b[:, CA:2 * CA]))
                    nc.scalar.copy(ca_raw[:, 1, n - 12, :], b[:, 0:CA]).then_inc(unit_act, 1)
                elif n < 16:
                    nc.scalar.copy(xpad[:, n - 14, 3:3 + SEQ], b[:, 0:SEQ]).then_inc(unit_act, 1)
                elif n < 18:
                    nc.scalar.copy(gate[:, n - 16, :], b[:, 0:SEQ]).then_inc(unit_act, 1)
                else:
                    dst, bias = (rg_r, BR) if n == 20 else (rg_i, BI)
                    link(nc.scalar.activation(dst[:, 0, :], b[:, 0:SEQ], ACT.Sigmoid, bias=vec[:, bias:bias + 1]))
                    nc.scalar.activation(dst[:, 1, :], b[:, SEQ:2 * SEQ], ACT.Sigmoid,
                                         bias=vec[:, bias + 1:bias + 2]).then_inc(unit_act, 1)

            def evac_x2T(t):
                act.wait_ge(x2T_ps, 2 * t + 1)
                nc.scalar.copy(xn2T[:, 0:4, t * P:(t + 1) * P],
                               ps[:, 2 * t, :].rearrange("p (k q) -> p k q", k=4)).then_inc(x2T_act, 1)

            def split_a(i):
                if i:
                    act.wait_ge(unit_ps, 8)
                    act.wait_ge(memT_act, KD // 2)
                    act.wait_ge(memT_dve, KD // 2)
                else:
                    act.wait_ge(xT_act, KD // 2)
                    act.wait_ge(xT_dve, KD // 2)
                nc.scalar.copy((hT_hi, memT_hi)[i][:], (hT, memT)[i][:]).then_inc(ahi_act, 1)

            def split_w(i):
                act.wait_ge((wV_loaded, kv_loaded)[i // 2], 16)
                c = slice(i % 2 * 4, i % 2 * 4 + 4)
                nc.scalar.copy((wV_hi, w_kv_hi)[i // 2][:, c, :], (wV, w_kv)[i // 2][:, c, :]).then_inc(whi_act, 1)

            split_a(0)

            def square_and_gain(k):
                nc.scalar.activation(y_sq[:, k, :], yT[:, k, :], ACT.Square).then_inc(ysq_act, 1)
                nc.scalar.mul(yT[:, k, :], yT[:, k, :], vec[:, GOUT + k:GOUT + k + 1]).then_inc(yg_act, 1)

            for kind, n in walk:
                if kind == "unit" and owner[n] == "act":
                    evac(n)
                elif kind == "split_a":
                    split_a(n)
                elif kind == "split_w":
                    split_w(n)
                elif kind == "mem_norm":
                    act.wait_ge(mem_loaded, 16)
                    squares(mem_in, 4, 2)
                    root(4, 4)
                elif kind == "memT":
                    for k in ACT_K:
                        act.wait_ge(memT_ps, k // 2 + 1)
                        nc.scalar.mul(memT[:, k, :], ps[:, 4 + k // 2, k % 2 * SEQ:(k % 2 + 1) * SEQ],
                                      vec[:, MEM + k:MEM + k + 1]).then_inc(memT_act, 1)
                elif kind == "z":
                    act.wait_ge(z_ps, n + 1)
                    if n >= 2:
                        act.wait_ge(wT_ps, n - 1)
                    zb = ps[:, 4 + n % 2, 0:NZ]
                    nc.scalar.activation(beta[n % 2][:], zb, ACT.Sigmoid, scale=SCALE).then_inc(bc_act, 1)
                    nc.scalar.activation(keep[n % 2][:], zb, ACT.Sigmoid, scale=-SCALE).then_inc(bc_act, 1)
                elif kind == "t":
                    act.wait_ge(wT_ps, n + 1)
                    nc.scalar.copy(wT[n % 2][:], ps[:, 6, 0:NZ]).then_inc(wT_act, 1)
                elif kind == "ca_norm":
                    act.wait_ge(ca_ss_dve, 1)
                    nc.scalar.activation(ca_rs[:], ca_rs[:], ACT.Sqrt).then_inc(ca_rt_act, 1)
                elif kind == "gelu":
                    act.wait_ge(unit_ps, 18)
                    for k in range(3):
                        act.wait_ge(yT_dve, k + 1)
                        square_and_gain(k)
            act.wait_ge(yT_dve, 4)
            square_and_gain(3)
            act.wait_ge(gelu_dve, 1)
            nc.scalar.activation(rg_g[:], rg_g[:], ACT.Sigmoid, scale=2.0 * 0.7978845608028654).then_inc(gelu_act, 1)
            act.wait_ge(lam_dve, 2)
            act.wait_ge(unit_act, owner[:22].count("act"))
            for c in range(2):
                nc.scalar.activation(rg_t[:, c, :], rg_r[:, c, :], ACT.Tanh, scale=lam[:, 7, c:c + 1]).then_inc(rg_act, 1)
            for c in range(2):
                nc.scalar.activation(rg_a[:, c, :], rg_r[:, c, :], ACT.Exp, scale=lam[:, 7, c:c + 1]).then_inc(rg_act, 1)
            for h in range(CA_HEADS):
                act.wait_ge(camax_dve, h + 1)
                if h >= 2:
                    act.wait_ge(unit_ps, 27 + h - 2 + 1)
                for t in range(NT):
                    ins = nc.scalar.activation(ca_p[h % 2][:, t, :], ps[:, (22 + h) % 4, t * SEQ:(t + 1) * SEQ], ACT.Exp,
                                               bias=mx[:, t, h:h + 1], scale=SCALE,
                                               accum_out=stat[:, 8 + 2 * (h % 2) + t:9 + 2 * (h % 2) + t])
                    if t == 0:
                        link(ins)
                    else:
                        ins.then_inc(unit_act, 1)
            act.wait_ge(rg_dve, 1)
            nc.scalar.activation(rg_t[:], rg_t[:], ACT.Sqrt, scale=-1.0).then_inc(rg_act, 1)
            for g in range(3):
                if g:
                    for i in range(2):
                        act.wait_ge(yrg_dve if g == 1 else oca_dve, i + 1)
                        square_and_gain(2 + 2 * g + i)
                freed(act, SUMS[g])
                nc.scalar.activation(g_rs[:, g, :], g_rs[:, g, :], ACT.Sqrt).then_inc(g_rt_act, 1)
            for t in range(NT):
                act.wait_ge(x1_dve, 8 + 4 * t)
                act.wait_ge(ssq_act, 4 + t)
                nc.scalar.activation(x1_sq[:], x1[:, t, :], ACT.Square,
                                     accum_out=stat[:, t:t + 1]).then_inc(ssq_act, 1)
                act.wait_ge(xn_dve, 7 + 2 * t)
                nc.scalar.activation(stat[:, 2 + t:3 + t], stat[:, 2 + t:3 + t], ACT.Sqrt).then_inc(std_act, 1)
                evac_x2T(t)
            for t in range(NT):
                act.wait_ge(rt_ps, t + 1)
                nc.scalar.activation(score[:, t, :], ps[:, 4 + t, 0:NE], ACT.Sigmoid).then_inc(score_act, 1)
                act.wait_ge(s_gu_ps, t + 1)
                nc.scalar.activation(s_sg[:, t, :], ps[:, 6 + t, 0:DE], ACT.Silu).then_inc(s_sg_act, 1)
            for t in range(NT):
                nc.scalar.copy(xhi[:, t], xn2[:, t]).then_inc(split_act, 1)
            for i in range(KD // 2):
                act.wait_ge(gather_ps, 2 * i + 1)
                nc.scalar.copy(xg[0][:, 2 * i, :], ps[:, Y[0], :]).then_inc(xg_act, 1)

            def overflow(p):
                lo = nc.scalar.value_load(cum[0:1, bass.ds(2 * p, 1)], min_val=0, max_val=NE)
                hi = nc.scalar.value_load(cum[0:1, bass.ds(2 * p + 2, 1)], min_val=0, max_val=NE)
                with nc.scalar.If(hi > lo):
                    with nc.scalar.Fori(lo, hi) as j:
                        act.wait_ge(ov_gather_ps, 2 * j + 1)
                        nc.scalar.copy(ov_xg[:, 0:4, :], ps[:, Y[0], :].rearrange("p (a b) -> p a b", a=4)).then_inc(ov_xg_act, 1)
                        act.wait_ge(ov_pt_ps, j + 1)
                        nc.scalar.copy(ov_S[:], ps[:, T, 0:SEQ]).then_inc(ov_S_act, 1)
                        act.wait_ge(ov_gu_ps, 2 * j + 3)
                        act.wait_ge(h_dve, p + 1)
                        nc.scalar.activation(e_sg[:], ps[:, U, 0:DE], ACT.Silu).then_inc(ov_sg_act, 1)
                        act.wait_ge(ov_gslot_dve, 2 * j + 2)
                        for half in range(2):
                            act.wait_ge(ov_y_ps, 2 * j + half + 1)
                            nc.scalar.mul(yhi[:, half * 512:(half + 1) * 512], ps[:, Y[half], :],
                                          ov_gslot[:]).then_inc(ov_yhi_act, 1)

            def octets(it, gather_last):
                for j in range(8):
                    p, o, q, ob = 8 * it + j, 2 * it + j // 4, j % 4, j // 4
                    act.wait_ge(gu_ps, 2 * p + 2)
                    nc.scalar.activation(e_sg[:], ps[:, U, 0:DE], ACT.Silu).then_inc(sg_act, 1)
                    overflow(p)
                    if ob == 0 or gather_last:
                        act.wait_ge(gather_ps, 8 * (o + 1) + 2 * q + 1)
                        nc.scalar.copy(xg[1 - ob][:, 2 * q, :], ps[:, Y[0], :]).then_inc(xg_act, 1)
                    act.wait_ge(pt_ps, p + 2)
                    nc.scalar.copy(S[j % 2][:], ps[:, T, 0:SEQ]).then_inc(S_act, 1)
                    act.wait_ge(gslot_dve, 2 * p + 2)
                    for half in range(2):
                        act.wait_ge(y_ps, 2 * p + half + 1)
                        nc.scalar.mul(yhi[:, half * 512:(half + 1) * 512], ps[:, Y[half], :],
                                      gslot[:, j % 2:j % 2 + 1]).then_inc(yhi_act, 1)

            act.sem_inc(S_act, 1)
            act.sem_inc(yhi_act, 1)
            act.wait_ge(cum_dve, 1)
            with act.Fori(0, PAIRS // 8 - 1) as it:
                octets(it, True)
            octets(PAIRS // 8 - 1, False)

        @block.vector
        def _(dve):
            chain = [0]

            def link(ins):
                chain[0] += 1
                ins.then_inc(dve_chain, 1)
                dve.wait_ge(dve_chain, chain[0])

            def mean_eps(col, n_ssq):
                dve.wait_ge(ssq_act, n_ssq)
                nc.vector.tensor_scalar(stat[:, col + 2:col + 4], stat[:, col:col + 2], 1.0 / D, EPS, ALU.mult,
                                        ALU.add).then_inc(xn_dve, 1)

            def scale_rows(src, dst, col, n_std):
                dve.wait_ge(std_act, n_std)
                link(nc.vector.reciprocal(stat[:, col + 2:col + 4], stat[:, col + 2:col + 4]))
                for t in range(NT):
                    nc.vector.tensor_scalar(dst[:, t, :], src[:, t, :], stat[:, col + 2 + t:col + 3 + t], None,
                                            ALU.mult).then_inc(xn_dve, 1)

            mean_eps(0, 2)
            scale_rows(x_in, xn, 0, 1)
            dve.wait_ge(vec_ps, 1)
            nc.vector.tensor_copy(vec[:], ps[:, 3, 0:42]).then_inc(vec_dve, 1)
            dve.wait_ge(vec_dve, 1)
            for k in DVE_K:
                dve.wait_ge(xT_ps, k // 2 + 1)
                nc.vector.tensor_scalar(hT[:, k, :], ps[:, 4 + k // 2, k % 2 * SEQ:(k % 2 + 1) * SEQ], vec[:, MIX + k:MIX + k + 1], None,
                                        ALU.mult).then_inc(xT_dve, 1)
            link(nc.vector.tensor_scalar(lam[:, 2, :], vec[:, LAM:LAM + 2], -1.0, None, ALU.mult))
            nc.vector.tensor_tensor(lam[:, 0, :], vec[:, LAM:LAM + 2], lam[:, 2, :], ALU.min).then_inc(lam_dve, 1)

            def log1p():
                dve.wait_ge(lam_act, 1)
                e = lam[:, 1, :]
                link(nc.vector.tensor_scalar(lam[:, 3, :], e, 2.0, None, ALU.add))
                link(nc.vector.reciprocal(lam[:, 3, :], lam[:, 3, :]))
                link(nc.vector.tensor_tensor(lam[:, 3, :], e, lam[:, 3, :], ALU.mult))
                link(nc.vector.tensor_tensor(lam[:, 4, :], lam[:, 3, :], lam[:, 3, :], ALU.mult))
                terms = 9
                link(nc.vector.tensor_scalar(lam[:, 5, :], lam[:, 4, :], 2.0 / (2 * terms + 1), 2.0 / (2 * terms - 1),
                                             ALU.mult, ALU.add))
                for n in range(terms - 2, -1, -1):
                    link(nc.vector.tensor_tensor(lam[:, 5, :], lam[:, 5, :], lam[:, 4, :], ALU.mult))
                    link(nc.vector.tensor_scalar(lam[:, 5, :], lam[:, 5, :], 2.0 / (2 * n + 1), None, ALU.add))
                link(nc.vector.tensor_tensor(lam[:, 5, :], lam[:, 5, :], lam[:, 3, :], ALU.mult))
                link(nc.vector.tensor_scalar(lam[:, 6, :], lam[:, 2, :], 0.0, None, ALU.max))
                link(nc.vector.tensor_tensor(lam[:, 6, :], lam[:, 6, :], lam[:, 5, :], ALU.add))
                nc.vector.tensor_scalar(lam[:, 7, :], lam[:, 6, :], -8.0, None, ALU.mult).then_inc(lam_dve, 1)

            def evac(n):
                dve.wait_ge(unit_ps, n + 1)
                b = ps[:, n % 4, :]
                if n < 8:
                    dst, src = qk[:, n, :], b[:, 0:SEQ]
                elif n < 10:
                    dst, src = v_sb[:, n - 8, :], b
                elif n < 12:
                    dst, src = ca_raw[:, 0, n - 10, :], b[:, 0:CA]
                elif n < 14:
                    link(nc.vector.tensor_copy(v_ca[:, n - 12, :], b[:, CA:2 * CA]))
                    dst, src = ca_raw[:, 1, n - 12, :], b[:, 0:CA]
                elif n < 16:
                    dst, src = xpad[:, n - 14, 3:3 + SEQ], b[:, 0:SEQ]
                elif n < 18:
                    dst, src = gate[:, n - 16, :], b[:, 0:SEQ]
                else:
                    j = n - 18
                    nc.vector.tensor_scalar(qkca[:, 2 * j:2 * j + 2, :], b.rearrange("p (c q) -> p c q", c=2),
                                            vec[:, QN + j:QN + j + 1], None, ALU.mult).then_inc(unit_dve, 1)
                    return
                nc.vector.tensor_copy(dst, src).then_inc(unit_dve, 1)

            def split_a(i):
                dve.wait_ge(ahi_act, i + 1)
                nc.vector.tensor_tensor((hT_lo, memT_lo)[i][:], (hT, memT)[i][:], (hT_hi, memT_hi)[i][:].bitcast(F32),
                                        ALU.subtract).then_inc(alo_dve, 1)

            def split_w(i):
                dve.wait_ge(whi_act, i + 1)
                c = slice(i % 2 * 4, i % 2 * 4 + 4)
                nc.vector.tensor_tensor((wV_lo, w_kv_lo)[i // 2][:, c, :], (wV, w_kv)[i // 2][:, c, :],
                                        (wV_hi, w_kv_hi)[i // 2][:, c, :].bitcast(F32), ALU.subtract).then_inc(wlo_dve, 1)

            split_a(0)

            def conv():
                freed(dve, 14)
                freed(dve, 15)
                for c in range(2):
                    link(nc.vector.tensor_scalar(xc[:, c, :], xpad[:, c, 3:3 + SEQ], vec[:, CW + 6 + c:CW + 7 + c],
                                                 vec[:, CB + c:CB + c + 1], ALU.mult, ALU.add))
                    for tap in range(3):
                        ins = nc.vector.scalar_tensor_tensor(xc[:, c, :], xpad[:, c, tap:tap + SEQ],
                                                             vec[:, CW + 2 * tap + c:CW + 2 * tap + c + 1], xc[:, c, :],
                                                             ALU.mult, ALU.add)
                        if tap < 2:
                            link(ins)
                        else:
                            ins.then_inc(conv_dve, 1)

            def gelu_argument():
                freed(dve, 16)
                freed(dve, 17)
                link(nc.vector.tensor_tensor(rg_g[:], gate[:], gate[:], ALU.mult))
                link(nc.vector.tensor_scalar(rg_g[:], rg_g[:], 0.044715, 1.0, ALU.mult, ALU.add))
                nc.vector.tensor_tensor(rg_g[:], rg_g[:], gate[:], ALU.mult).then_inc(gelu_dve, 1)

            for kind, n in walk:
                if kind == "unit" and owner[n] == "dve":
                    evac(n)
                elif kind == "split_a":
                    split_a(n)
                elif kind == "split_w":
                    split_w(n)
                elif kind == "mem_norm":
                    mean_eps(4, 4)
                    scale_rows(mem_in, memn, 4, 2)
                elif kind == "memT":
                    for k in DVE_K:
                        dve.wait_ge(memT_ps, k // 2 + 1)
                        nc.vector.tensor_scalar(memT[:, k, :], ps[:, 4 + k // 2, k % 2 * SEQ:(k % 2 + 1) * SEQ],
                                                vec[:, MEM + k:MEM + k + 1], None, ALU.mult).then_inc(memT_dve, 1)
                elif kind == "z":
                    if n == 0:
                        dve.wait_ge(zeroed, 1)
                    dve.wait_ge(mask_pool, 4 * n + 4)
                    b = n % 2
                    kp, rs = keep[b], rest[b]
                    nc.vector.tensor_tensor_scan(rs[:, 0:P][:, ::-1], kp[:, 0:P][:, ::-1], zeros[:, 0:P], 1.0,
                                                 ALU.mult, ALU.add).then_inc(dve_chain, 1)
                    nc.vector.tensor_tensor_scan(rs[:, P + 1:NZ + 1][:, ::-1], kp[:, P:NZ][:, ::-1], zeros[:], 1.0,
                                                 ALU.mult, ALU.add).then_inc(dve_chain, 1)
                    chain[0] += 2
                    dve.wait_ge(dve_chain, chain[0])
                    nc.vector.tensor_tensor(beta[b][:, 0:P], beta[b][:, 0:P], rs[:, 1:P + 1], ALU.mult).then_inc(w_dve, 1)
                    nc.vector.tensor_tensor(beta[b][:, P:NZ], beta[b][:, P:NZ], rs[:, P + 2:NZ + 2],
                                            ALU.mult).then_inc(w_dve, 1)
                elif kind == "av":
                    if n % 2:
                        dve.wait_ge(o_ps, n + 1)
                        c = (n // 2) % 2 * SEQ
                        nc.vector.tensor_copy(yT[:, n // 2, :], ps[:, 7, c:c + SEQ]).then_inc(yT_dve, 1)
                elif kind == "conv":
                    conv()
                elif kind == "gelu":
                    gelu_argument()
                elif kind == "log1p":
                    log1p()
                elif kind == "ca_square":
                    for u in range(10, 14):
                        freed(dve, u)
                    link(nc.vector.tensor_tensor(ca_sq[:], ca_raw[:], ca_raw[:], ALU.mult))
                    link(nc.vector.reduce_sum(ca_rs[:].rearrange("p a t h -> p (a t h)"),
                                              ca_sq[:].rearrange("p a t (h d) -> p (a t h) d", d=HD), AX.X))
                    nc.vector.tensor_scalar(ca_rs[:], ca_rs[:], 1.0 / HD, EPS, ALU.mult, ALU.add).then_inc(ca_ss_dve, 1)
                elif kind == "ca_norm":
                    dve.wait_ge(ca_rt_act, 1)
                    link(nc.vector.reciprocal(ca_rs[:], ca_rs[:]))
                    heads = ca_raw[:].rearrange("p a t (h d) -> p (a t h) d", d=HD)
                    nc.vector.tensor_tensor(heads, heads, ca_rs[:].rearrange("p a t h -> p (a t h)").unsqueeze(2)
                                            .to_broadcast([P, 2 * NT * CA_HEADS, HD]), ALU.mult).then_inc(ca_rs_dve, 1)

            def ca_max(h):
                dve.wait_ge(unit_ps, 23 + h)
                link(nc.vector.reduce_max(mx[:, :, h], ps[:, (22 + h) % 4, :].rearrange("p (t m) -> p t m", t=NT), AX.X))
                nc.vector.tensor_scalar(mx[:, :, h], mx[:, :, h], -SCALE, None, ALU.mult).then_inc(camax_dve, 1)

            def ca_norm(h):
                b = h % 2
                freed(dve, 22 + h)
                sums = stat[:, 8 + 2 * b:10 + 2 * b]
                link(nc.vector.reciprocal(sums, sums))
                for t in range(NT):
                    nc.vector.tensor_scalar(ca_p[b][:, t, :], ca_p[b][:, t, :], stat[:, 8 + 2 * b + t:9 + 2 * b + t],
                                            None, ALU.mult).then_inc(cap_dve, 1)

            def ca_evac(h):
                dve.wait_ge(unit_ps, 28 + h)
                if h == 2:
                    dve.wait_ge(oca_ps, 1)
                if h == 3:
                    dve.wait_ge(unit_ps, 32)
                nc.vector.tensor_copy(ca_pT[h % 2][:], ps[:, (27 + h) % 4, :].rearrange("p (m q) -> p m q", m=2)).then_inc(unit_dve, 1)

            def ca_result(j):
                dve.wait_ge(unit_ps, 32 + j)
                nc.vector.tensor_copy(yT[:, 6 + j, :], ps[:, (31 + j) % 4, 0:SEQ]).then_inc(oca_dve, 1)

            def mean_square(g, width):
                dve.wait_ge(unit_ps, SUMS[g] + 1)
                nc.vector.tensor_scalar(g_rs[:, g, :], ps[:, SUMS[g] % 4, 0:NT], 1.0 / width, EPS, ALU.mult,
                                        ALU.add).then_inc(unit_dve, 1)

            def residual(u):
                g, t, half = projections[u]
                if t == 0 and half == 0:
                    dve.wait_ge(g_rt_act, g + 1)
                    link(nc.vector.reciprocal(g_rs[:, g, :], g_rs[:, g, :]))
                dve.wait_ge(wo_ps, u + 1)
                if g:
                    dve.wait_ge(x1_dve, projections.index((g - 1, t, half)) + 1)
                c = slice(half * 512, (half + 1) * 512)
                nc.vector.scalar_tensor_tensor(x1[:, t, c], ps[:, ACC[2 * t + half], :], g_rs[:, g, t:t + 1], x1[:, t, c],
                                               ALU.mult, ALU.add).then_inc(x1_dve, 1)

            for h in range(CA_HEADS):
                ca_max(h)
            dve.wait_ge(rg_act, 4)
            link(nc.vector.tensor_tensor(rg_u[:], rg_a[:], rg_a[:], ALU.mult))
            nc.vector.scalar_tensor_tensor(rg_t[:], rg_u[:], 1.0, rg_t[:], ALU.add, ALU.mult).then_inc(rg_dve, 1)
            ca_norm(0)
            ca_norm(1)
            mean_square(0, SB)
            ca_evac(0)
            ca_norm(2)
            ca_evac(1)
            ca_norm(3)
            link(nc.vector.tensor_tensor(rg_u[:], rg_i[:], xc[:], ALU.mult))
            dve.wait_ge(rg_act, 5)
            link(nc.vector.tensor_tensor(rg_u[:], rg_u[:], rg_t[:], ALU.mult))
            for c in range(2):
                link(nc.vector.tensor_tensor_scan(rg_r[:, c, :], rg_a[:, c, :], rg_u[:, c, :], 0.0, ALU.mult, ALU.add))
            dve.wait_ge(gelu_act, 1)
            link(nc.vector.tensor_tensor(rg_g[:], rg_g[:], gate[:], ALU.mult))
            for c in range(2):
                nc.vector.tensor_tensor(yT[:, 4 + c, :], rg_g[:, c, :], rg_r[:, c, :], ALU.mult).then_inc(yrg_dve, 1)
            ca_evac(2)
            ca_evac(3)
            ca_result(0)
            dve.wait_ge(x1_loaded, 16)
            for u in range(3):
                residual(u)
            ca_result(1)
            residual(3)
            mean_square(1, RG)
            residual(4)
            mean_square(2, CA)
            for u in range(5, 8):
                residual(u)
            def second_norm(t, meanwhile=()):
                dve.wait_ge(ssq_act, 5 + t)
                rms = stat[:, 2 + t:3 + t]
                nc.vector.tensor_scalar(rms, stat[:, t:t + 1], 1.0 / D, EPS, ALU.mult, ALU.add).then_inc(xn_dve, 1)
                for u in meanwhile:
                    residual(u)
                dve.wait_ge(std_act, 3 + t)
                link(nc.vector.reciprocal(rms, rms))
                dve.wait_ge(gffn_loaded, 16)
                nc.vector.scalar_tensor_tensor(xn2[:, t], x1[:, t, :].rearrange("q (p k) -> q k p", k=KD), rms,
                                               g_ffn[:].rearrange("q (p k) -> q k p", k=KD), ALU.mult,
                                               ALU.mult).then_inc(xn_dve, 1)

            def evac_x2T(t):
                dve.wait_ge(x2T_ps, 2 * t + 2)
                nc.vector.tensor_copy(xn2T[:, 4:8, t * P:(t + 1) * P],
                                      ps[:, 2 * t + 1, :].rearrange("p (k q) -> p k q", k=4)).then_inc(x2T_dve, 1)

            def route(t):
                dve.wait_ge(score_act, t + 1)
                link(nc.vector.tensor_tensor(choice[:, t, :], score[:, t, :], rbias[:], ALU.add))
                for g in range(GROUPS):
                    nc.vector.max(top8[:, t, g, :], choice[:, t, g * EG:(g + 1) * EG]).then_inc(dve_chain, 1)
                chain[0] += GROUPS
                dve.wait_ge(dve_chain, chain[0])
                link(nc.vector.tensor_tensor(grp[:, t, 0:GROUPS], top8[:, t, :, 0], top8[:, t, :, 1], ALU.add))
                link(nc.vector.memset(grp[:, t, 12:16], -HUGE))
                link(nc.vector.max(gtop[:, t, :], grp[:, t, :]))
                link(nc.vector.match_replace(grep[:, t, :], gtop[:, t, :], grp[:, t, :], -HUGE))
                link(nc.vector.tensor_tensor(grep[:, t, 0:GROUPS], grep[:, t, 0:GROUPS], grp[:, t, 0:GROUPS], ALU.is_equal))
                link(nc.vector.tensor_scalar(grp[:, t, 0:GROUPS], grep[:, t, 0:GROUPS], -1.0, 1.0, ALU.mult, ALU.add))
                link(nc.vector.tensor_scalar(grep[:, t, 0:GROUPS], grep[:, t, 0:GROUPS], -HUGE, None, ALU.mult))
                cg = cand[:, t, :].rearrange("p (g e) -> p g e", g=GROUPS)
                taken = grp[:, t, 0:GROUPS].unsqueeze(2).to_broadcast([P, GROUPS, EG])
                off = grep[:, t, 0:GROUPS].unsqueeze(2).to_broadcast([P, GROUPS, EG])
                link(nc.vector.tensor_tensor(cg, choice[:, t, :].rearrange("p (g e) -> p g e", g=GROUPS), taken, ALU.mult))
                link(nc.vector.tensor_tensor(cg, cg, off, ALU.add))
                link(nc.vector.max(gtop[:, t, :], cand[:, t, :]))
                link(nc.vector.match_replace(repl[:, t, :], gtop[:, t, :], cand[:, t, :], HUGE))
                link(nc.vector.tensor_scalar(repl[:, t, :], repl[:, t, :], HUGE, None, ALU.is_equal))
                nc.vector.tensor_copy(picked[:, t, :], repl[:, t, :]).then_inc(route_dve, 1)

            def shared_hidden(t):
                dve.wait_ge(s_sg_act, t + 1)
                nc.vector.tensor_tensor(s_h[:, t].rearrange("q k p -> q p k"), s_sg[:, t, :].rearrange("q (p k) -> q p k", k=KH),
                                        ps[:, 6 + t, DE:2 * DE].rearrange("q (p k) -> q p k", k=KH), ALU.mult).then_inc(s_h_dve, 1)

            second_norm(0, meanwhile=(8,))
            residual(9)
            evac_x2T(0)
            residual(10)
            residual(11)
            second_norm(1)
            dve.wait_ge(rb_loaded, 16)
            dve.wait_ge(consts, 3)
            evac_x2T(1)
            def shared_evac(t):
                dve.wait_ge(s_hT_ps, t + 1)
                nc.vector.tensor_copy(s_hT[:, :, t * P:(t + 1) * P],
                                      ps[:, t, 0:KH * P].rearrange("p (k q) -> p k q", k=KH)).then_inc(s_hT_dve, 1)

            route(0)
            shared_hidden(0)
            route(1)
            shared_evac(0)
            shared_hidden(1)
            dve.wait_ge(count_ps, 1)
            link(nc.vector.scalar_tensor_tensor(posm[:], ps[:, 3, 0:NT * NE].rearrange("p (t e) -> p t e", t=NT), 1.0,
                                                repl[:], ALU.add, ALU.mult))

            def build_pick(o, buf):
                for t in range(NT):
                    nc.vector.tensor_tensor(
                        pick[buf][:, t, :].rearrange("p (e s) -> p e s", s=SLOTS),
                        iota1[:, 0:SLOTS].unsqueeze(1).to_broadcast([P, 8, SLOTS]),
                        posm[:, t, bass.ds(8 * o, 8)].unsqueeze(2).to_broadcast([P, 8, SLOTS]),
                        ALU.is_equal).then_inc(pick_dve, 1)

            shared_evac(1)
            build_pick(0, 0)
            cr = cnt_row
            link(nc.vector.tensor_scalar(cr[:, 1, 0:NE], ps[0:1, 3, 2 * NE:3 * NE], float(SLOTS), None, ALU.is_gt))
            link(nc.vector.tensor_scalar(cr[:, 2, 0:NE], ps[0:1, 3, 2 * NE:3 * NE], float(SLOTS + P), None, ALU.is_gt))
            link(nc.vector.tensor_tensor(cr[:, 1, 0:NE], cr[:, 1, 0:NE], cr[:, 2, 0:NE], ALU.add))
            link(nc.vector.tensor_tensor_scan(cr[:, 0, 1:NE + 1], cr[:, 1, 0:NE], cr[:, 3, 0:NE], 0.0, ALU.add, ALU.add))
            nc.vector.tensor_copy(cum[:], cr[:, 0, :]).then_inc(cum_dve, 1)
            for t in range(NT):
                dve.wait_ge(split_act, t + 1)
                nc.vector.tensor_tensor(xlo[:, t], xn2[:, t], xhi[:, t].bitcast(F32), ALU.subtract).then_inc(split_dve, 1)
            link(nc.vector.tensor_tensor(gatew[:], repl[:], score[:], ALU.mult))
            link(nc.vector.reduce_sum(stat[:, 4:6], gatew[:], AX.X))
            link(nc.vector.tensor_scalar(stat[:, 4:6], stat[:, 4:6], 1e-20, None, ALU.add))
            link(nc.vector.reciprocal(stat[:, 4:6], stat[:, 4:6]))
            for t in range(NT):
                link(nc.vector.tensor_scalar(gatew[:, t, :], gatew[:, t, :], stat[:, 4 + t:5 + t], 2.5, ALU.mult, ALU.mult))
            g4 = gatew[:].rearrange("p t (n two) -> p t n two", two=2)
            link(nc.vector.tensor_copy(gates2[:, :, :, 0:2], g4))
            nc.vector.tensor_tensor(gates2[:, :, :, 2:4], g4, gates2[:, :, :, 0:2].bitcast(F32),
                                    ALU.subtract).then_inc(gates_dve, 1)
            for i in range(KD // 2):
                dve.wait_ge(gather_ps, 2 * i + 2)
                nc.vector.tensor_copy(xg[0][:, 2 * i + 1, :], ps[:, Y[1], :]).then_inc(xg_dve, 1)
            dve.wait_ge(cum_dve, 1)

            def slot_gates(dst, sem, sides=(0, 1)):
                for part, side in enumerate(sides):
                    rws = slice(part * SLOTS, (part + 1) * SLOTS)
                    nc.vector.reduce_sum(dst[rws], ps[rws, T, SEQ + side:SEQ + side + 3:2], AX.X).then_inc(sem, 1)

            def hidden(dst, sem):
                nc.vector.tensor_tensor(dst[:].rearrange("q k p -> q p k"), e_sg[:].rearrange("q (p k) -> q p k", k=KH),
                                        ps[:, U, DE:2 * DE].rearrange("q (p k) -> q p k", k=KH), ALU.mult).then_inc(sem, 1)

            def hidden_T(sem):
                nc.vector.tensor_copy(e_hT[:], ps[:, U, 0:2 * P].rearrange("p (k t) -> p k t", k=KH)).then_inc(sem, 1)

            def overflow(p):
                c0 = nc.vector.value_load(cum[0:1, bass.ds(2 * p, 1)], min_val=0, max_val=NE)
                c2 = nc.vector.value_load(cum[0:1, bass.ds(2 * p + 2, 1)], min_val=0, max_val=NE)
                with nc.vector.If(c2 > c0):
                    c1 = nc.vector.value_load(cum[0:1, bass.ds(2 * p + 1, 1)], min_val=0, max_val=NE)
                    for side, lo, hi in ((0, c0, c1), (1, c1, c2)):
                        with nc.vector.If(hi > lo):
                            with nc.vector.Fori(lo, hi) as j:
                                overflow_item(2 * p + side, side, j, j - lo)

            def overflow_item(e, side, j, c):
                dve.wait_ge(ov_scatter_ps, j + 1)
                first = nc.s_assert_within(
                    c * P + SLOTS, SLOTS, SLOTS + P,
                    skip_runtime_bounds_check_because="an expert has at most 256 tokens, so at most two items")
                for t in range(NT):
                    nc.vector.tensor_tensor(ov_pick[:, t, :], iota1[:, bass.ds(first, P)],
                                            posm[:, t, bass.ds(e, 1)].to_broadcast([P, P]),
                                            ALU.is_equal).then_inc(ov_pick_dve, 1)
                dve.wait_ge(ov_gather_ps, 2 * j + 2)
                nc.vector.tensor_copy(ov_xg[:, 4:8, :], ps[:, Y[1], :].rearrange("p (a b) -> p a b", a=4)).then_inc(ov_xg_dve, 1)
                dve.wait_ge(ov_S_act, j + 1)
                slot_gates(ov_gslot[:], ov_gslot_dve, (side, side))
                dve.wait_ge(ov_sg_act, j + 1)
                hidden(ov_h, ov_h_dve)
                dve.wait_ge(ov_hT_ps, j + 1)
                hidden_T(ov_hTs_dve)
                dve.wait_ge(ov_gslot_dve, 2 * j + 2)
                for half in range(2):
                    dve.wait_ge(ov_yhi_act, 2 * j + half + 1)
                    c = slice(half * 512, (half + 1) * 512)
                    nc.vector.scalar_tensor_tensor(ylo[:, c], ps[:, Y[half], :], ov_gslot[:], yhi[:, c].bitcast(F32),
                                                   ALU.mult, ALU.subtract).then_inc(ov_ylo_dve, 1)

            def octets(it, gather_last):
                for j in range(8):
                    p, o, q, ob = 8 * it + j, 2 * it + j // 4, j % 4, j // 4
                    more = ob == 0 or gather_last
                    if q == 0 and more:
                        dve.wait_ge(pt_ps, p + 1)
                        build_pick(o + 1, 1 - ob)
                    dve.wait_ge(sg_act, p + 1)
                    hidden(e_h, h_dve)
                    overflow(p)
                    if more:
                        dve.wait_ge(gather_ps, 8 * (o + 1) + 2 * q + 2)
                        nc.vector.tensor_copy(xg[1 - ob][:, 2 * q + 1, :], ps[:, Y[1], :]).then_inc(xg_dve, 1)
                    dve.wait_ge(hT_ps, p + 1)
                    hidden_T(hTs_dve)
                    dve.wait_ge(S_act, p + 2)
                    slot_gates(gslot[:, j % 2:j % 2 + 1], gslot_dve)
                    dve.wait_ge(gslot_dve, 2 * p + 2)
                    for half in range(2):
                        dve.wait_ge(yhi_act, 2 * p + half + 2)
                        c = slice(half * 512, (half + 1) * 512)
                        nc.vector.scalar_tensor_tensor(ylo[:, c], ps[:, Y[half], :], gslot[:, j % 2:j % 2 + 1],
                                                       yhi[:, c].bitcast(F32), ALU.mult, ALU.subtract).then_inc(ylo_dve, 1)

            dve.sem_inc(hTs_dve, 1)
            dve.sem_inc(ylo_dve, 1)
            with dve.Fori(0, PAIRS // 8 - 1) as it:
                octets(it, True)
            octets(PAIRS // 8 - 1, False)
            for t in range(NT):
                for half in range(2):
                    dve.wait_ge(last_ps, 2 * t + half + 1)
                    c = slice(half * 512, (half + 1) * 512)
                    nc.vector.tensor_tensor(x1[:, t, c], x1[:, t, c], ps[:, ACC[2 * t + half], :], ALU.add).then_inc(out_dve, 1)

        @block.tensor
        def _(pe):
            mm = nc.tensor.matmul

            pe.wait_ge(consts, 2)
            for _ in range(WARM_UP):
                mm(ps[:, 0, 0:SEQ], ident[:], zeros[:], start=True, stop=True)
            pe.wait_ge(vec_loaded, 16 * 14)
            nc.tensor.transpose(ps[:, 3, 0:42], vecs[:], ident[0:42, 0:42]).then_inc(vec_ps, 1)

            def transposes(src, b0, sem):
                for k in range(KD):
                    for t in range(NT):
                        c = (k % 2) * SEQ + t * P
                        last = nc.tensor.transpose(ps[:, b0 + k // 2, c:c + P], src(t, k), ident[:])
                    if k % 2:
                        last.then_inc(sem, 1)

            pe.wait_ge(xn_dve, 3)
            transposes(lambda t, k: xn[:, t, k * P:(k + 1) * P], 4, xT_ps)

            def unit(n):
                if n >= 4:
                    freed(pe, n - 4)
                b = ps[:, n % 4, :]
                if n < 8 or 14 <= n < 18:
                    if n < 8:
                        pe.wait_ge(wA_loaded[n // 2], 16)
                        w, c = wA[n // 2], n % 2 * P
                    else:
                        g, c = rg_cols[n]
                        pe.wait_ge(wR_loaded[g], 16)
                        w = wR[g]
                    for k in range(KD):
                        if n == 0:
                            if k in ACT_K:
                                pe.wait_ge(xT_act, ACT_K.index(k) + 1)
                            else:
                                pe.wait_ge(xT_dve, DVE_K.index(k) + 1)
                        last = mm(b[:, 0:SEQ], w[:, k, c:c + P], hT[:, k, :], start=k == 0, stop=k == KD - 1)
                elif n < 14:
                    if n in (10, 11):
                        pe.wait_ge(wR_loaded[2], 16)
                        c = (n - 10) * P
                        for k in range(KD):
                            last = mm(b[:, 0:CA], hT[:, k, c:c + P], wR[2][:, k, :], start=k == 0, stop=k == KD - 1)
                    else:
                        i, c = (0, (n - 8) * P) if n < 10 else (1, (n - 12) * P)
                        a_hi, a_lo, w_hi, w_lo = ((hT_hi, hT_lo, wV_hi, wV_lo), (memT_hi, memT_lo, w_kv_hi, w_kv_lo))[i]
                        pe.wait_ge(alo_dve, i + 1)
                        for k in range(KD):
                            if k % 4 == 0:
                                pe.wait_ge(wlo_dve, 2 * i + k // 4 + 1)
                            for m, (a, w) in enumerate(((a_hi, w_hi), (a_lo, w_hi), (a_hi, w_lo))):
                                last = mm(b, a[:, k, c:c + P], w[:, k, :], start=k == 0 and m == 0,
                                          stop=k == KD - 1 and m == 2)
                elif n < 20:
                    pe.wait_ge(ca_rs_dve, 1)
                    for m in range(2):
                        for t in range(NT):
                            c = m * SEQ + t * P
                            last = nc.tensor.transpose(b[:, c:c + P], ca_raw[:, n - 18, t, m * P:(m + 1) * P], ident[:])
                elif n < 22:
                    pe.wait_ge(conv_dve, 2)
                    pe.wait_ge(wg_loaded, 64)
                    w = wg_r if n == 20 else wg_i
                    for c in range(2):
                        for half in range(2):
                            rws = slice(half * HD, (half + 1) * HD)
                            last = mm(b[rws, c * SEQ:(c + 1) * SEQ], w[rws, c, :], xc[rws, c, :], start=True, stop=True)
                elif n < 26:
                    h = n - 22
                    rws = slice(h % 2 * HD, (h % 2 + 1) * HD)
                    freed(pe, 18)
                    freed(pe, 19)
                    for t in range(NT):
                        last = mm(b[:, t * SEQ:(t + 1) * SEQ], qkca[rws, h // 2, t * P:(t + 1) * P],
                                  qkca[rws, 2 + h // 2, :], start=True, stop=True)
                elif n in SUMS:
                    g = SUMS.index(n)
                    pe.wait_ge(ysum_pool, g + 1)
                    for t in range(NT):
                        last = mm(b[:, t:t + 1], y_sq[:, (0, 4, 6)[g], t * P:(t + 1) * P], ones[:, 0:1], start=True, stop=True)
                elif n < 31:
                    h = n - 27
                    pe.wait_ge(cap_dve, 2 * h + 2)
                    for m in range(2):
                        for t in range(NT):
                            c = m * SEQ + t * P
                            last = nc.tensor.transpose(b[:, c:c + P], ca_p[h % 2][:, t, m * P:(m + 1) * P], ident[:])
                last.then_inc(unit_ps, 1)

            for kind, n in walk:
                if kind == "unit":
                    unit(n)
                elif kind == "memT":
                    pe.wait_ge(xn_dve, 6)
                    transposes(lambda t, k: memn[:, t, k * P:(k + 1) * P], 4, memT_ps)
                elif kind == "z":
                    if n == 0:
                        freed(pe, 6)
                        freed(pe, 7)
                        pe.wait_ge(memT_act, KD // 2)
                        pe.wait_ge(memT_dve, KD // 2)
                    if n >= 2:
                        pe.wait_ge(bc_act, 2 * n - 2)
                    rws = slice(n % 2 * HD, (n % 2 + 1) * HD)
                    q, k = qk[rws, n // 2, :], qk[rws, 4 + n // 2, :]
                    mm(ps[:, 4 + n % 2, 0:P], q[:, 0:P], k[:, 0:P], start=True, stop=True)
                    mm(ps[:, 4 + n % 2, P:NZ], q[:, P:SEQ], k, start=True, stop=True).then_inc(z_ps, 1)
                elif kind == "t":
                    if n >= 1:
                        pe.wait_ge(wT_act, n)
                    pe.wait_ge(w_dve, 2 * n + 2)
                    for c in range(3):
                        last = nc.tensor.transpose(ps[:, 6, c * P:(c + 1) * P], beta[n % 2][:, c * P:(c + 1) * P], ident[:])
                    last.then_inc(wT_ps, 1)
                elif kind == "av":
                    if n == 0:
                        freed(pe, 8)
                        freed(pe, 9)
                    if n >= 2 and n % 2 == 0:
                        pe.wait_ge(yT_dve, n // 2)
                    pe.wait_ge(wT_act, n + 1)
                    c = n // 2 % 2 * SEQ
                    o = ps[n % 2 * HD:(n % 2 + 1) * HD, 7, c:c + SEQ]
                    mm(o, v_sb[:, 0, n * HD:(n + 1) * HD], wT[n % 2][:, 0:SEQ], start=True, stop=False)
                    mm(o[:, P:SEQ], v_sb[:, 1, n * HD:(n + 1) * HD], wT[n % 2][:, SEQ:NZ], start=False,
                       stop=True).then_inc(o_ps, 1)
            def ca_out(h):
                if h == 0:
                    freed(pe, 12)
                    freed(pe, 13)
                freed(pe, 27 + h)
                n = 31 + h // 2
                o = ps[h % 2 * HD:(h % 2 + 1) * HD, n % 4, 0:SEQ]
                for m in range(2):
                    last = mm(o, v_ca[:, m, h * HD:(h + 1) * HD], ca_pT[h % 2][:, m, :], start=m == 0, stop=m == 1)
                last.then_inc(unit_ps if h % 2 else oca_ps, 1)

            def project(u, part=None):
                g, t, half = projections[u]
                if u == 0:
                    pe.wait_ge(wo_loaded, 16)
                if g:
                    pe.wait_ge(x1_dve, projections.index((g - 1, t, half)) + 1)
                chunks = ((0, 1, 2, 3), (4, 5), (6, 7))[g]
                for k in part or chunks:
                    if t == 0 and half == 0:
                        pe.wait_ge(yg_act, k + 1)
                    last = mm(ps[:, ACC[2 * t + half], :], yT[:, k, t * P:(t + 1) * P],
                              wo[:, k, half * 512:(half + 1) * 512], start=k == chunks[0], stop=k == chunks[-1])
                if k == chunks[-1]:
                    last.then_inc(wo_ps, 1)

            project(0, (0, 1, 2))
            for n in range(22, 26):
                unit(n)
            project(0, (3,))
            unit(26)
            project(1)
            unit(27)
            unit(28)
            project(2)
            unit(29)
            unit(30)
            ca_out(0)
            ca_out(1)
            project(3)
            ca_out(2)
            ca_out(3)
            unit(33)
            project(4)
            project(5)
            unit(34)
            for u in range(6, 11):
                project(u)
            pe.wait_ge(rt_loaded, 16)
            def transpose_xn2(t):
                pe.wait_ge(xn_dve, 8 + 2 * t)
                for k in range(KD):
                    last = nc.tensor.transpose(ps[:, 2 * t + k // 4, k % 4 * P:(k % 4 + 1) * P], xn2[:, t, k, :], ident[:])
                    if k % 4 == 3:
                        last.then_inc(x2T_ps, 1)

            def router(t):
                pe.wait_ge(x2T_act, t + 1)
                pe.wait_ge(x2T_dve, t + 1)
                for k in range(KD):
                    last = mm(ps[:, 4 + t, 0:NE], xn2T[:, k, t * P:(t + 1) * P], w_rt[:, k, :],
                              start=k == 0, stop=k == KD - 1)
                last.then_inc(rt_ps, 1)

            def shared_gate_up(t, chunks=range(KD)):
                for k in chunks:
                    last = mm(ps[:, 6 + t, :], xn2T[:, k, t * P:(t + 1) * P], ring_gu[0][:, :, k, :],
                              start=k == 0, stop=k == KD - 1)
                if k == KD - 1:
                    last.then_inc(s_gu_ps, 1)

            def shared_transpose(t):
                pe.wait_ge(s_h_dve, t + 1)
                for kk in range(KH):
                    last = nc.tensor.transpose(ps[:, t, kk * P:(kk + 1) * P], s_h[:, t, kk, :], ident[:])
                last.then_inc(s_hT_ps, 1)

            def shared_down(t, half):
                pe.wait_ge(s_hT_dve, t + 1)
                for kk in range(KH):
                    last = mm(ps[:, ACC[2 * t + half], :], s_hT[:, kk, t * P:(t + 1) * P],
                              ring_d[0][:, kk, half * 512:(half + 1) * 512], start=kk == 0, stop=False,
                              skip_group_check=True)
                return last

            transpose_xn2(0)
            project(11)
            router(0)
            pe.wait_ge(gu_loaded[0], 32)
            pe.wait_ge(x1_dve, 12)
            shared_gate_up(0, range(5))
            transpose_xn2(1)
            shared_gate_up(0, range(5, KD))
            router(1)
            shared_gate_up(1, range(5))
            shared_transpose(0)
            shared_gate_up(1, range(5, KD))
            pe.wait_ge(route_dve, 2)
            pb = ps[:, 3, :]
            mm(pb[:, 0:NE], upper[:], picked[:, 0, :], start=True, stop=True)
            mm(pb[:, NE:2 * NE], upper[:], picked[:, 1, :], start=True, stop=False)
            mm(pb[:, NE:2 * NE], ones_b[:], picked[:, 0, :], start=False, stop=True)
            mm(pb[:, 2 * NE:3 * NE], ones_b[:], picked[:, 0, :], start=True, stop=False)
            mm(pb[:, 2 * NE:3 * NE], ones_b[:], picked[:, 1, :], start=False, stop=True).then_inc(count_ps, 1)
            pe.wait_ge(d_loaded[0], 16)
            pe.wait_ge(score_act, 2)
            shared_down(0, 0)
            shared_transpose(1)
            shared_down(0, 1)
            shared_down(1, 0)
            shared_down(1, 1).then_inc(s_down_ps, 1)

            def gather_chunk(k, buf, bank):
                for i, (part, t) in enumerate(((xhi, 0), (xhi, 1), (xlo, 0), (xlo, 1))):
                    last = mm(ps[:, bank, :], part[:, t, k, :], pick[buf][:, t, :], start=i == 0, stop=i == 3)
                last.then_inc(gather_ps, 1)

            pe.wait_ge(split_dve, 2)
            pe.wait_ge(pick_dve, 2)
            pe.wait_ge(cum_dve, 1)
            for k in range(KD):
                if k >= 2:
                    pe.wait_ge(xg_act if k % 2 == 0 else xg_dve, k // 2)
                gather_chunk(k, 0, Y[k % 2])

            def gate_up(rows_a, rows_b, na, nb, sem, gathered=None):
                for k in range(KD):
                    if gathered is not None:
                        pe.wait_ge(xg_act if k % 2 == 0 else xg_dve, gathered + (k // 2 + 1))
                    for side, (lhs, n) in enumerate(((rows_a, na), (rows_b, nb))):
                        last = mm(ps[side * SLOTS:(side + 1) * SLOTS, U, :], lhs(k), ring_gu[n][:, :, k, :],
                                  start=k == 0, stop=k == KD - 1)
                last.then_inc(sem, 2)

            def hidden_T(h, sem):
                for kk in range(KH):
                    last = nc.tensor.transpose(ps[:, U, kk * P:(kk + 1) * P], h[:, kk, :], ident[:])
                last.then_inc(sem, 1)

            def slots_T(picks, gate_cols, sem):
                for t in range(NT):
                    nc.tensor.transpose(ps[:, T, t * P:(t + 1) * P], picks(t).bitcast(F32), ident[:])
                for t in range(NT):
                    last = mm(ps[:, T, SEQ:SEQ + 4], picks(t), gate_cols(t), start=t == 0, stop=t == NT - 1)
                last.then_inc(sem, 1)

            def down(na, nb, sem):
                for half in range(2):
                    for kk in range(KH):
                        for side, n in enumerate((na, nb)):
                            last = mm(ps[side * SLOTS:(side + 1) * SLOTS, Y[half], :],
                                      e_hT[:, kk, side * SLOTS:(side + 1) * SLOTS],
                                      ring_d[n][:, kk, half * 512:(half + 1) * 512], start=kk == 0, stop=kk == KH - 1)
                    last.then_inc(sem, 1)

            def scatter(to_token, hi, lo, sem=None, final=False):
                for t in range(NT):
                    for half in range(2):
                        for i, y in enumerate((hi, lo)):
                            last = mm(ps[:, ACC[2 * t + half], :], to_token[:, t * P:(t + 1) * P],
                                      y[:, half * 512:(half + 1) * 512], start=False, stop=final and i == 1,
                                      skip_group_check=True)
                        if final:
                            last.then_inc(sem, 1)
                if sem is not None and not final:
                    last.then_inc(sem, 1)

            def overflow_item(p, j, n, d_fill):
                pe.wait_ge(ov_pick_dve, 2 * j + 2)
                pe.wait_ge(gates_dve, 1)
                for k in range(KD):
                    for t in range(NT):
                        last = mm(ps[:, Y[k // 4], k % 4 * P:(k % 4 + 1) * P], xn2[:, t, k, :],
                                  ov_pick[:, t, :].bitcast(F32), start=t == 0, stop=t == NT - 1)
                    if k % 4 == 3:
                        last.then_inc(ov_gather_ps, 1)
                slots_T(lambda t: ov_pick[:, t, :], lambda t: gates2[:, t, bass.ds(p, 1), :], ov_pt_ps)
                pe.wait_ge(h_dve, p + 1)
                pe.wait_ge(ov_xg_act, j + 1)
                pe.wait_ge(ov_xg_dve, j + 1)
                gate_up(lambda k: ov_xg[:, k, 0:SLOTS], lambda k: ov_xg[:, k, SLOTS:P], n, n, ov_gu_ps)
                pe.wait_ge(ov_h_dve, j + 1)
                hidden_T(ov_h, ov_hT_ps)
                pe.wait_ge(d_loaded[n], d_fill)
                pe.wait_ge(ov_hTs_dve, j + 1)
                down(n, n, ov_y_ps)
                pe.wait_ge(ov_yhi_act, 2 * j + 2)
                pe.wait_ge(ov_ylo_dve, 2 * j + 2)
                pe.wait_ge(ov_S_act, j + 1)
                scatter(ov_S, yhi, ylo, ov_scatter_ps)

            def octets(it, gather_last):
                for j in range(8):
                    p, o, q, ob = 8 * it + j, 2 * it + j // 4, j % 4, j // 4
                    na, nb = slot(2 * j), slot(2 * j + 1)
                    more = ob == 0 or gather_last
                    pe.wait_ge(gu_loaded[na], 32 * fills(it, 2 * j))
                    pe.wait_ge(gu_loaded[nb], 32 * fills(it, 2 * j + 1))
                    pe.wait_ge(hTs_dve, p + 1)
                    c = 2 * q * SLOTS
                    gate_up(lambda k: xg[ob][:, k, c:c + SLOTS], lambda k: xg[ob][:, k, c + SLOTS:c + 2 * SLOTS],
                            na, nb, gu_ps, 4 * o if q == 0 else None)
                    pe.wait_ge(yhi_act, 2 * p + 1)
                    pe.wait_ge(ylo_dve, 2 * p + 1)
                    pe.wait_ge(S_act, p + 1)
                    if j == 0:
                        pe.wait_ge(zeroed, 2)
                    scatter(S[(j + 1) % 2], yhi, ylo)
                    c0 = nc.tensor.value_load(cum[0:1, bass.ds(2 * p, 1)], min_val=0, max_val=NE)
                    c2 = nc.tensor.value_load(cum[0:1, bass.ds(2 * p + 2, 1)], min_val=0, max_val=NE)
                    with nc.tensor.If(c2 > c0):
                        c1 = nc.tensor.value_load(cum[0:1, bass.ds(2 * p + 1, 1)], min_val=0, max_val=NE)
                        for side, (lo, hi) in enumerate(((c0, c1), (c1, c2))):
                            with nc.tensor.If(hi > lo):
                                with nc.tensor.Fori(lo, hi) as item:
                                    overflow_item(p, item, (na, nb)[side], 16 * fills(it, 2 * j + side))
                    if more:
                        if q == 0:
                            pe.wait_ge(pick_dve, 2 * (o + 2))
                        gather_chunk(2 * q, 1 - ob, Y[0])
                        gather_chunk(2 * q + 1, 1 - ob, Y[1])
                    pe.wait_ge(h_dve, p + 1)
                    hidden_T(e_h, hT_ps)
                    if j == 0:
                        pe.wait_ge(gates_dve, 1)
                    slots_T(lambda t: pick[ob][:, t, c:c + 2 * SLOTS], lambda t: gates2[:, t, bass.ds(p, 1), :], pt_ps)
                    pe.wait_ge(d_loaded[na], 16 * fills(it, 2 * j))
                    pe.wait_ge(d_loaded[nb], 16 * fills(it, 2 * j + 1))
                    pe.wait_ge(hTs_dve, p + 2)
                    if more:
                        pe.wait_ge(xg_act, 4 * (o + 1) + q + 1)
                        pe.wait_ge(xg_dve, 4 * (o + 1) + q + 1)
                    down(na, nb, y_ps)

            pe.sem_inc(pt_ps, 1)
            pe.sem_inc(ov_scatter_ps, 1)
            pe.sem_inc(ov_gu_ps, 1)
            with pe.Fori(0, PAIRS // 8 - 1) as it:
                octets(it, True)
            octets(PAIRS // 8 - 1, False)
            pe.wait_ge(yhi_act, 2 * PAIRS + 1)
            pe.wait_ge(ylo_dve, 2 * PAIRS + 1)
            pe.wait_ge(S_act, PAIRS + 1)
            scatter(S[(PAIRS + 1) % 2], yhi, ylo, last_ps, final=True)


_INS = ['x', 'mem', 'norm_mix_g', 'norm_mem_g', 'w_in', 'conv_w', 'conv_b', 'w_rgate', 'b_rgate', 'w_igate', 'b_igate',
        'lru_lambda', 'w_mem_kv', 'q_norm_g', 'k_norm_g', 'g_out_sb', 'g_out_rg', 'g_out_ca', 'w_out', 'norm_ffn_g',
        'w_router', 'router_bias', 'w_gate_e', 'w_up_e', 'w_down_e', 'w_gate_sh', 'w_up_sh', 'w_down_sh']


def kernel(**inputs):
    import numpy as _np
    import concourse.bacc as _bacc
    from concourse import mybir as _mybir
    from concourse.bass_utils import run_bass_kernel_spmd as _run

    nc = _bacc.Bacc("TRN2", target_bir_lowering=False, num_devices=1)
    arrays, args = {}, []
    for name in _INS:
        a = _np.ascontiguousarray(inputs[name])
        arrays[f"in_{name}"] = a
        args.append(nc.dram_tensor(f"in_{name}", a.shape, _mybir.dt.from_np(a.dtype), kind="ExternalInput").ap())
    o = nc.dram_tensor("out_0", inputs["x"].shape, _mybir.dt.float32, kind="ExternalOutput").ap()
    hybrid_decoder_layer(nc, *args, o)
    r = _run(nc, [arrays], core_ids=[0])
    return r.results[0]["out_0"]
```
